# Optimizing a Trainium2 kernel written in Bass

```python
import math
import jax
import jax.numpy as jnp
from jax import lax
import numpy as np

D_MODEL = 2048
BATCH = 1
SEQ = 512
DEPTH = 2
DEC_BATCH = 8
DEC_SEQ = 8
PAST_LEN = 2048
PAGE_SIZE = 128

D_A = D_MODEL // 2
HD_A = 64
N_Q_A = D_A // HD_A
N_KV_A = 4
GROUP_A = N_Q_A // N_KV_A
WINDOW = 128
D_B = D_MODEL // 2
DK_B = 128
DV_B = 128
H_B = D_B // DV_B
D_QKV_B = 2 * H_B * DK_B + H_B * DV_B
DN_CONV = 4
DN_CHUNK = 64
D_C = D_MODEL
CF_CONV = 31
N_EVEN = (DEPTH + 1) // 2
N_ODD = DEPTH // 2
D_IN_EVEN = N_Q_A * HD_A + 2 * N_KV_A * HD_A + D_A + D_QKV_B + 2 * H_B + D_B
D_IN_ODD = 3 * D_C
EPS = 1e-6

kernel_name = 'hybrid_swa_gdn_conformer_step'

def rms_norm(x, g):
    xf = x.astype(jnp.float32)
    y = xf * lax.rsqrt(jnp.mean(xf * xf, axis=-1, keepdims=True) + EPS)
    return (y * g.astype(jnp.float32)).astype(x.dtype)

def layer_norm(x, g, b):
    xf = x.astype(jnp.float32)
    xc = xf - jnp.mean(xf, axis=-1, keepdims=True)
    y = xc * lax.rsqrt(jnp.mean(xc * xc, axis=-1, keepdims=True) + EPS)
    return (y * g.astype(jnp.float32) + b.astype(jnp.float32)).astype(x.dtype)

def l2_normalize(x):
    return x * lax.rsqrt(jnp.sum(x * x, axis=-1, keepdims=True) + EPS)

def causal_depthwise_conv(x, prev, w):
    k = w.shape[0]
    xp = jnp.concatenate([prev.astype(x.dtype), x], axis=1)
    y = lax.conv_general_dilated(xp, w.astype(x.dtype)[:, None, :], window_strides=(1,),
                                 padding='VALID', dimension_numbers=('NWC', 'WIO', 'NWC'),
                                 feature_group_count=x.shape[-1])
    return y, xp[:, xp.shape[1] - (k - 1):]

def window_mask(qpos, kpos):
    d = qpos[..., :, None] - kpos[..., None, :]
    return (d >= 0) & (d <= WINDOW) & (kpos[..., None, :] >= 0)

def sink_attention(q, k, v, mask, sinks):
    s = jnp.einsum('...qhgd,...khd->...hgqk', q, k).astype(jnp.float32) * (HD_A ** -0.5)
    s = jnp.where(mask, s, -jnp.inf)
    sk = sinks.astype(jnp.float32)[:, :, None, None]
    m = jnp.maximum(jnp.max(s, axis=-1, keepdims=True), sk)
    e = jnp.exp(s - m)
    p = e / (jnp.sum(e, axis=-1, keepdims=True) + jnp.exp(sk - m))
    return jnp.einsum('...hgqk,...khd->...qhgd', p.astype(v.dtype), v)

def swa_banded(q, k, v, sinks):
    n, t = q.shape[:2]
    nb = t // WINDOW
    qb = q.reshape(n, nb, WINDOW, N_KV_A, GROUP_A, HD_A)
    kb = k.reshape(n, nb, WINDOW, N_KV_A, HD_A)
    vb = v.reshape(n, nb, WINDOW, N_KV_A, HD_A)

    def with_prev(z):
        prev = jnp.concatenate([jnp.zeros_like(z[:, :1]), z[:, :-1]], axis=1)
        return jnp.concatenate([prev, z], axis=2)

    blk = jnp.arange(nb)[:, None] * WINDOW
    qpos = blk + jnp.arange(WINDOW)[None, :]
    kpos = blk - WINDOW + jnp.arange(2 * WINDOW)[None, :]
    mask = window_mask(qpos, kpos)[:, None, None]
    o = sink_attention(qb, with_prev(kb), with_prev(vb), mask, sinks)
    return o.reshape(n, t, D_A)

def swa_with_buffer(q, k, v, k_buf, v_buf, sinks):
    n, t = q.shape[:2]
    buf = k_buf.shape[1]
    kk = jnp.concatenate([k_buf.astype(k.dtype), k], axis=1)
    vv = jnp.concatenate([v_buf.astype(v.dtype), v], axis=1)
    qpos = PAST_LEN + jnp.arange(t)
    kpos = PAST_LEN - buf + jnp.arange(buf + t)
    o = sink_attention(q, kk, vv, window_mask(qpos, kpos), sinks)
    return o.reshape(n, t, D_A), kk[:, t:], vv[:, t:]

def gated_delta_rule(q, k, v, g, beta, s0):
    f32 = jnp.float32
    n, t, h, _ = q.shape
    out_dtype = q.dtype
    q = l2_normalize(q.astype(f32)) * (DK_B ** -0.5)
    k = l2_normalize(k.astype(f32))
    v = v.astype(f32)
    c = min(DN_CHUNK, t)
    pad = (-t) % c
    nc = (t + pad) // c

    def chunks(z):
        z = jnp.pad(z, [(0, 0), (0, pad)] + [(0, 0)] * (z.ndim - 2))
        z = z.reshape((n, nc, c) + z.shape[2:])
        return jnp.moveaxis(jnp.moveaxis(z, 3, 2), 1, 0)

    qc, kc, vc, gc, bc = (chunks(z) for z in (q, k, v, g, beta))
    gcum = jnp.cumsum(gc, axis=-1)
    tril = jnp.tril(jnp.ones((c, c), dtype=bool))
    diff = gcum[..., :, None] - gcum[..., None, :]
    decay = jnp.where(tril, jnp.exp(jnp.where(tril, diff, 0.0)), 0.0)
    kb = kc * bc[..., None]
    lower = jnp.tril(jnp.einsum('...id,...jd->...ij', kb, kc) * decay, -1)
    a_mat = lower + jnp.eye(c, dtype=f32)
    rhs = jnp.concatenate([vc * bc[..., None], kb * jnp.exp(gcum)[..., None]], axis=-1)
    sol = lax.linalg.triangular_solve(a_mat, rhs, left_side=True, lower=True, unit_diagonal=True)
    u, w = sol[..., :DV_B], sol[..., DV_B:]
    attn = jnp.einsum('...id,...jd->...ij', qc, kc) * decay
    qg = qc * jnp.exp(gcum)[..., None]
    kg = kc * jnp.exp(gcum[..., -1:] - gcum)[..., None]
    g_last = jnp.exp(gcum[..., -1])

    def step(s, xs):
        u_i, w_i, attn_i, qg_i, kg_i, gl_i = xs
        v_new = u_i - jnp.einsum('nhck,nhkv->nhcv', w_i, s)
        o = jnp.einsum('nhck,nhkv->nhcv', qg_i, s) + jnp.einsum('nhij,nhjv->nhiv', attn_i, v_new)
        s = s * gl_i[..., None, None] + jnp.einsum('nhck,nhcv->nhkv', kg_i, v_new)
        return s, o

    s_fin, o = lax.scan(step, s0.astype(f32), (u, w, attn, qg, kg, g_last))
    o = jnp.moveaxis(jnp.moveaxis(o, 0, 1), 2, 3).reshape(n, nc * c, h, DV_B)[:, :t]
    return o.astype(out_dtype), s_fin.astype(s0.dtype)

def gated_deltanet_branch(qkv, a, b, z, conv_prev, s0, conv_w, a_log, dt_bias, norm_g):
    n, t = qkv.shape[:2]
    f32 = jnp.float32
    cqkv, conv_new = causal_depthwise_conv(qkv, conv_prev, conv_w)
    cqkv = jax.nn.silu(cqkv)
    q, k, v = jnp.split(cqkv, [H_B * DK_B, 2 * H_B * DK_B], axis=-1)
    g = -jnp.exp(a_log.astype(f32)) * jax.nn.softplus(a.astype(f32) + dt_bias.astype(f32))
    beta = jax.nn.sigmoid(b.astype(f32))
    o, s_new = gated_delta_rule(q.reshape(n, t, H_B, DK_B), k.reshape(n, t, H_B, DK_B),
                                v.reshape(n, t, H_B, DV_B), g, beta, s0)
    o = rms_norm(o, norm_g).reshape(n, t, D_B) * jax.nn.silu(z)
    return o, s_new, conv_new

def conformer_conv_branch(h, w_in, w_out, conv_prev, conv_w, conv_b, ln_g, ln_b):
    val, gate, z = jnp.split(h @ w_in, 3, axis=-1)
    u = val * jax.nn.sigmoid(gate)
    c, conv_new = causal_depthwise_conv(u, conv_prev, conv_w)
    c = layer_norm(c + conv_b.astype(c.dtype), ln_g, ln_b)
    y = jax.nn.silu(c) * jax.nn.silu(z)
    return y @ w_out, conv_new

def split_even(u):
    sizes = (N_Q_A * HD_A, N_KV_A * HD_A, N_KV_A * HD_A, D_A, D_QKV_B, H_B, H_B, D_B)
    idx = []
    acc = 0
    for s in sizes[:-1]:
        acc += s
        idx.append(acc)
    return jnp.split(u, idx, axis=-1)

def trunk(x, caches, norm_gain, w_in_even, w_out_even, attn_sinks, dn_conv_w, dn_a_log,
          dn_dt_bias, dn_norm_gain, w_in_odd, w_out_odd, cf_conv_w, cf_conv_b, cf_ln_gain,
          cf_ln_bias, final_norm_gain):
    n, t, _ = x.shape
    dtype = x.dtype
    new_k, new_v, new_s, new_dnc, new_cfc = [], [], [], [], []
    for layer in range(DEPTH):
        i = layer // 2
        h = rms_norm(x, norm_gain[layer])
        if layer % 2 == 0:
            qa, ka, va, za, qkv_b, a_b, b_b, z_b = split_even(h @ w_in_even[i])
            qa = qa.reshape(n, t, N_KV_A, GROUP_A, HD_A)
            ka = ka.reshape(n, t, N_KV_A, HD_A)
            va = va.reshape(n, t, N_KV_A, HD_A)
            sinks = attn_sinks[i].reshape(N_KV_A, GROUP_A)
            if caches is None:
                o_a = swa_banded(qa, ka, va, sinks)
                buf = min(WINDOW, t)
                k_buf, v_buf = ka[:, t - buf:], va[:, t - buf:]
                dn_prev = jnp.zeros((n, DN_CONV - 1, D_QKV_B), dtype)
                s0 = jnp.zeros((n, H_B, DK_B, DV_B), dtype)
            else:
                o_a, k_buf, v_buf = swa_with_buffer(qa, ka, va, caches[0][i], caches[1][i], sinks)
                s0 = caches[2][i]
                dn_prev = caches[3][i]
            o_a = o_a * jax.nn.silu(za)
            o_b, s_new, dnc_new = gated_deltanet_branch(qkv_b, a_b, b_b, z_b, dn_prev, s0,
                                                        dn_conv_w[i], dn_a_log[i],
                                                        dn_dt_bias[i], dn_norm_gain[i])
            y = jnp.concatenate([o_a, o_b], axis=-1) @ w_out_even[i]
            new_k.append(k_buf)
            new_v.append(v_buf)
            new_s.append(s_new)
            new_dnc.append(dnc_new)
        else:
            if caches is None:
                cf_prev = jnp.zeros((n, CF_CONV - 1, D_C), dtype)
            else:
                cf_prev = caches[4][i]
            y, cf_new = conformer_conv_branch(h, w_in_odd[i], w_out_odd[i], cf_prev, cf_conv_w[i],
                                              cf_conv_b[i], cf_ln_gain[i], cf_ln_bias[i])
            new_cfc.append(cf_new)
        x = x + y
    states = (jnp.stack(new_k), jnp.stack(new_v), jnp.stack(new_s), jnp.stack(new_dnc),
              jnp.stack(new_cfc))
    return rms_norm(x, final_norm_gain), states

def setup_inputs(seed: int = 0) -> dict:
    key = jax.random.key(seed)
    ks = jax.random.split(key, 24)
    f32 = jnp.float32

    def nrm(k, shape, scale):
        return jax.random.normal(k, shape, f32) * scale

    buf = min(WINDOW, PAST_LEN)
    dt = jnp.exp(jax.random.uniform(ks[12], (N_EVEN, H_B), f32, math.log(1e-3), math.log(1e-1)))
    return {
        'x_prompt': nrm(ks[0], (BATCH, SEQ, D_MODEL), 1.0),
        'x_sample': nrm(ks[1], (DEC_BATCH, DEC_SEQ, D_MODEL), 1.0),
        'cache_win_k': nrm(ks[2], (N_EVEN, DEC_BATCH, buf, N_KV_A, HD_A), 1.0),
        'cache_win_v': nrm(ks[3], (N_EVEN, DEC_BATCH, buf, N_KV_A, HD_A), 1.0),
        'state_dn': nrm(ks[4], (N_EVEN, DEC_BATCH, H_B, DK_B, DV_B), 0.1),
        'state_dn_conv': nrm(ks[5], (N_EVEN, DEC_BATCH, DN_CONV - 1, D_QKV_B), 1.0),
        'state_cf_conv': nrm(ks[6], (N_ODD, DEC_BATCH, CF_CONV - 1, D_C), 1.0),
        'norm_gain': 1.0 + nrm(ks[7], (DEPTH, D_MODEL), 0.02),
        'w_in_even': nrm(ks[8], (N_EVEN, D_MODEL, D_IN_EVEN), D_MODEL ** -0.5),
        'w_out_even': nrm(ks[9], (N_EVEN, D_A + D_B, D_MODEL), (D_A + D_B) ** -0.5),
        'attn_sinks': nrm(ks[10], (N_EVEN, N_Q_A), 0.5),
        'dn_conv_w': nrm(ks[11], (N_EVEN, DN_CONV, D_QKV_B), DN_CONV ** -0.5),
        'dn_a_log': jnp.log(jax.random.uniform(ks[13], (N_EVEN, H_B), f32, 1.0, 16.0)),
        'dn_dt_bias': dt + jnp.log(-jnp.expm1(-dt)),
        'dn_norm_gain': 1.0 + nrm(ks[14], (N_EVEN, DV_B), 0.02),
        'w_in_odd': nrm(ks[15], (N_ODD, D_MODEL, D_IN_ODD), D_MODEL ** -0.5),
        'w_out_odd': nrm(ks[16], (N_ODD, D_C, D_MODEL), D_C ** -0.5),
        'cf_conv_w': nrm(ks[17], (N_ODD, CF_CONV, D_C), CF_CONV ** -0.5),
        'cf_conv_b': nrm(ks[18], (N_ODD, D_C), 0.02),
        'cf_ln_gain': 1.0 + nrm(ks[19], (N_ODD, D_C), 0.02),
        'cf_ln_bias': nrm(ks[20], (N_ODD, D_C), 0.02),
        'final_norm_gain': 1.0 + nrm(ks[21], (D_MODEL,), 0.02),
    }

def reference(x_prompt, x_sample, cache_win_k, cache_win_v, state_dn, state_dn_conv,
              state_cf_conv, norm_gain, w_in_even, w_out_even, attn_sinks, dn_conv_w, dn_a_log,
              dn_dt_bias, dn_norm_gain, w_in_odd, w_out_odd, cf_conv_w, cf_conv_b, cf_ln_gain,
              cf_ln_bias, final_norm_gain):
    weights = (norm_gain, w_in_even, w_out_even, attn_sinks, dn_conv_w, dn_a_log, dn_dt_bias,
               dn_norm_gain, w_in_odd, w_out_odd, cf_conv_w, cf_conv_b, cf_ln_gain, cf_ln_bias,
               final_norm_gain)
    y_prompt, (p_k, p_v, p_dn, p_dnc, p_cfc) = trunk(x_prompt, None, *weights)
    y_sample, (s_k, s_v, s_dn, s_dnc, s_cfc) = trunk(
        x_sample, (cache_win_k, cache_win_v, state_dn, state_dn_conv, state_cf_conv), *weights)
    return (y_prompt, y_sample, p_k, p_v, p_dn, p_dnc, p_cfc, s_k, s_v, s_dn, s_dnc, s_cfc)


_drawn_inputs = setup_inputs


def setup_inputs(seed=0):
    import zlib

    import numpy as np

    out = dict(_drawn_inputs(seed))
    spreads = {}
    factors = {'attn_sinks': 32.622,
     'dn_norm_gain': 7.064,
     'cf_conv_b': 4.439,
     'cf_ln_gain': 31.198,
     'cf_ln_bias': 30.246,
     'final_norm_gain': 7.609}
    for name, (base, spread) in spreads.items():
        noise = np.random.default_rng([zlib.crc32(name.encode()), seed]).standard_normal(out[name].shape)
        drawn = base * np.exp(spread * noise) if base else spread * noise
        out[name] = jnp.asarray(drawn.astype(out[name].dtype))
    for name, factor in factors.items():
        out[name] = (out[name] * factor).astype(out[name].dtype)
    return out
```

```python
from contextlib import ExitStack

import numpy as np
import concourse.bass as bass
from concourse import mybir

F32 = mybir.dt.float32
F32R = mybir.dt.float32r
ALU = mybir.AluOpType
ACT = mybir.ActivationFunctionType
AX_X = mybir.AxisListType.X

P = 128
D = 2048
KT = D // P
NB, NT = 8, 8
SEQ = 512
NC = SEQ // P
NS = NB * NT
HP, HS = SEQ // 2, NS // 2
HALF = HP + HS
TOK = 2 * HALF
H = 8
W = 128
EPS = 1e-6
CF = 31
CP = CF - 1
LEVELS = 7
NEG = -1.0e30

N_AB, N_HEAD, N_KV, N_Q, N_ZA = 0, 1, 1 + 4 * H, 5 + 4 * H, 13 + 4 * H
N_OUT0 = N_ZA + 8
N_VG = N_OUT0 + KT
N_Z1 = N_VG + 2 * KT
N_OUT1 = N_Z1 + KT
N_TILES = N_OUT1 + KT

C_ID, C_TRI, C_ONE, C_NEG = 0, 128, 256, 384
C_CAU = 512
C_LVL = C_CAU + 256
C_TRIS = C_LVL + LEVELS * 128
C_ONES, C_NEGS = C_TRIS + 64, C_TRIS + 128
C_SEQ = C_NEGS + 64
C_WIN = C_SEQ + NB
N_CONST = C_WIN + W + NT

P_G0, P_G1, P_GF = 0, 16, 32
P_DNW = 48
P_CFW = P_DNW + H * 12
P_CFB = P_CFW + KT * CF
P_LNG, P_LNB = P_CFB + 16, P_CFB + 32
P_DNG = P_LNB + 16
P_ALOG, P_DTB = P_DNG + 1, P_DNG + 9
P_SINK = P_DTB + 8
P_SINKS = P_SINK + 16
N_PARAM = P_SINKS + 1


class Steps:

    def __init__(self, sem, names):
        self.sem, self.names, self.index = sem, names, {n: i for i, n in enumerate(names)}

    def at(self, name, it=0):
        return it * len(self.names) + self.index[name] + 1


class Tally:

    def __init__(self, sem):
        self.sem, self.base, self.k, self.it, self.per = sem, 0, 0, None, 0

    def inc(self, ins):
        ins.then_inc(self.sem, 1)
        self.k += 1

    def now(self):
        return self.base + self.k if self.it is None else self.it * self.per + (self.base + self.k)

    def enter(self, it, per):
        self.base, self.k, self.it, self.per = self.base + self.k, 0, it, per

    def leave(self, rounds):
        assert self.k == self.per, f"{self.sem}: {self.k} increments in a round, not {self.per}"
        self.base, self.k, self.it = self.base + rounds * self.per, 0, None


LV = range(1, LEVELS)
PE_HEAD = (["kv_tok", "gcum", "norm", "gram", "m0"] + [f"{s}{i}" for i in LV for s in ("a", "x")]
           + ["u0", "so0"] + [f"{s}{c}" for c in range(1, NC) for s in ("s", "u", "so")] + ["o_chan"])
DVE_HEAD = (["kg", "dmask", "ssum", "vs", "Mt", "attn", "X", "Xt"] + [f"X{i}" for i in LV]
            + ["vp0", "S0", "o0"] + [f"{s}{c}" for c in range(1, NC) for s in ("r", "vp", "S", "o")]
            + ["on", "y"])
ACT_HEAD = ["sq", "decay"] + [f"A{i}" for i in LV] + [f"q{c}" for c in range(1, NC)] + ["osq"]
POOL_HEAD = (["scalars", "gB", "nrm", "rn", "bn", "bp"] + [f"L{i}" for i in range(LEVELS)]
             + ["f1", "f2", "f3", "f4", "f5"])
PE_PLAN = {0: "kv_tok", 1: "gcum", 2: "norm", 4: "gram", 6: "m0"}
PE_PLAN |= {7 + i: n for i, n in enumerate(PE_HEAD[5:-1])}
PE_PLAN |= {31: "o_chan"}


def counts(names):
    return {n: i + 1 for i, n in enumerate(names)}


_groups = [["k_tok"], ["v_tok"], ["norm"], [], ["gram"], ["gcum"], [], ["m0"], ["a1"], ["x1"], ["a2"], ["x2"]]
SAMP_PLAN = [[(n, None) for n in g] for g in _groups] + [[("st", 0)]]
for _h in range(H):
    SAMP_PLAN += [[("tr", _h)], [("u", _h)], [("o", _h), ("ns", _h)] + [("st", _h + 1)] * (_h + 1 < H)]
SAMP_PLAN += [[("o_chan", None)]]
SAMP_PLAN = SAMP_PLAN[:31] + [[s for g in SAMP_PLAN[31:] for s in g]]
SPE = counts([n if h is None else f"{n}{h}" for g in SAMP_PLAN for n, h in g])
SD = counts(["kg", "ssum", "vs", "dmask", "dmask2", "Mt", "Mtb", "attn", "X", "Xt", "X1", "Xt1", "Xt2"]
            + [f"{s}{h}" for h in range(H) for s in ("r", "vp", "o", "S")] + ["on"])
SA = counts(["sq", "decay", "A1", "A2"] + [f"{s}{h}" for h in range(H) for s in ("ks", "q")] + ["osq"])
SP_ = counts(["gB", "nrm", "rn", "bn", "bp", "L0", "L1", "L2"] + [f"vx{h}" for h in range(H)]
             + ["f1", "f2", "f3", "f4", "f5"])
SATT_PLAN = {1: "last_turn", 3: "last", 5: "scores", 12: "turn", 14: "turn_new", 17: "v_new0", 20: "weigh0", 23: "v_new1",
             26: "weigh1"}
SAP = counts(list(SATT_PLAN.values())[2:])
SATT_ACT = {2: ["last"], 9: ["exp"], 13: ["turned"], 18: ["v_new0"], 24: ["v_new1"]}
PE_AT = {n: i for i, n in PE_PLAN.items()}
ACT_PLAN = {0: ["sq"], 2: ["decay"]} | {PE_AT[f"a{i}"]: [f"A{i}"] for i in LV}
ACT_PLAN |= {PE_AT[f"s{c}"]: [f"q{c}"] for c in range(1, NC)} | {30: ["osq"]}
DVE_PLAN = {0: ["kg"], 1: ["dmask"], 2: ["ssum"], 3: ["vs"], 4: ["Mt", "attn"], 6: ["X", "Xt"]}
DVE_PLAN |= {PE_AT[f"x{i}"]: [f"X{i}"] for i in LV} | {PE_AT["u0"]: ["vp0"], PE_AT["so0"]: ["S0", "o0"]}
for _c in range(1, NC):
    DVE_PLAN |= {PE_AT[f"s{_c}"]: [f"r{_c}"], PE_AT[f"u{_c}"]: [f"vp{_c}"], PE_AT[f"so{_c}"]: [f"S{_c}", f"o{_c}"]}
DVE_PLAN |= {30: ["on"], 31: ["y"]}
_at = {(n if h is None else f"{n}{h}"): i for i, g in enumerate(SAMP_PLAN) for n, h in g}
_after = {"kg": "k_tok", "ssum": "norm", "vs": "v_tok", "dmask": "gcum", "dmask2": "gcum", "Mt": "gcum",
          "Mtb": "gcum", "attn": "gcum", "X": "m0", "Xt": "m0", "X1": "x1", "Xt1": "x1", "Xt2": "x2",
          "on": f"ns{H - 1}"}
_after |= {f"{s}{h}": f"{q}{h}" for h in range(H) for s, q in (("r", "tr"), ("vp", "u"), ("o", "o"), ("S", "ns"))}
_aact = {"sq": "k_tok", "decay": "gcum", "A1": "a1", "A2": "a2", "osq": f"ns{H - 1}"}
_aact |= {f"{s}{h}": f"{q}{h}" for h in range(H) for s, q in (("ks", "st"), ("q", "tr"))}


def by_slot(order, after):
    plan, last = {}, 0
    for n in order:
        last = max(last, _at[after[n]])
        plan.setdefault(last, []).append(n)
    return plan


SAMP_DVE, SAMP_ACT = by_slot(SD, _after), by_slot(SA, _aact)
LN_SQ = {2: range(0, 6), 3: range(6, 12), 4: range(12, 16)}
LN_Y = {6: (0, 1), 7: (2, 3), 8: (4, 5), 9: (6, 7), 10: (8,)} | {k + 2: (k,) for k in range(9, 14)} | {16: (14, 15)}
SAD = counts(["bias0", "bias1", "bias2", "max", "max2", "neg", "sub", "den", "inv", "prob", "turned_new",
              "out0", "out1"])
SAA = counts(["exp", "turned", "v_new0", "v_new1"])
SATT_DVE = {3: "last", 5: "bias", 11: "prob", 15: "turned_new", 20: "out0", 26: "out1"}
POOL_PLAN = {0: ["scalars", "gB"], 2: ["nrm", "rn", "bn", "bp"], 4: ["L0", "L1"], 7: ["L2"]}
POOL_PLAN |= {PE_AT[f"a{l - 2}"] + 1: [f"L{l}"] for l in range(3, LEVELS)} | {30: ["f1", "f2", "f3", "f4", "f5"]}
DVE_TAPS = 16
POOL_TAPS = CF - DVE_TAPS
POOL_SUMS = POOL_TAPS - 1
ZRING = 6


def blk(c):
    return (c // 2) * HALF + (c % 2) * P


def hybrid_step(nc, x, wt, const, param, dn_prev, state_in, k_cache, v_cache, cf_prev,
                y, win_k, win_v, dn_out, dnc_out, cf_out, cfs_out, swk_out, swv_out, sdn_out):
    x1_dram = nc.dram_tensor("x1_scratch", (KT, P, TOK), F32, kind="Internal").ap()
    with ExitStack() as ctx:
        def sb(name, shape, dt=F32):
            return ctx.enter_context(nc.sbuf_tensor(name, shape, dt))

        def sem(name):
            return ctx.enter_context(nc.semaphore(name))

        act_hi = sb("act_hi", [P, KT, TOK], F32R)
        act_lo = sb("act_lo", [P, KT, TOK], F32R)
        full = sb("full", [P, KT, TOK])
        w_raw = sb("w_raw", [P, 2, 8 * P])
        w_hi = sb("w_hi", [P, 2, KT * P], F32R)
        w_lo = sb("w_lo", [P, 2, KT * P], F32R)
        cst = sb("cst", [P, N_CONST])
        par = sb("par", [P, N_PARAM])
        small = sb("small", [P, 464])
        arena = sb("arena", [P, 12076])
        acc = ctx.enter_context(nc.psum_tensor("acc", [P, 2, 2, 512], F32))
        gp = ctx.enter_context(nc.psum_tensor("gp", [P, 4, 512], F32))

        ident, tri, ones = cst[:, C_ID:C_ID + P], cst[:, C_TRI:C_TRI + P], cst[:, C_ONE:C_ONE + P]
        negm, caus = cst[:, C_NEG:C_NEG + P], cst[:, C_CAU:C_CAU + 2 * P]

        cfw = par[:, P_CFW:P_CFW + KT * CF].rearrange("p (j t) -> p j t", t=CF)
        cfb = par[:, P_CFB:P_CFB + KT].unsqueeze(2)

        def halves(ap):
            return ap.rearrange("p (a c) -> p a c", a=2)

        def bank4(lo, n=1):
            return gp[:, lo:lo + n, :].rearrange("p b (c t) -> p (b c) t", t=P)

        o = 0

        def cut(n, *dims):
            nonlocal o
            a = arena[:, o:o + n]
            o += n
            assert o <= 11500, o
            return a

        conv_in = cut(3 + SEQ + NB * (3 + NT) + 1)
        cin_p = conv_in[:, 0:3 + SEQ]
        cin_s = conv_in[:, 3 + SEQ:3 + SEQ + NB * (3 + NT)].rearrange("p (b t) -> p b t", b=NB)
        kqv0 = cut(3 * SEQ).rearrange("p (s t) -> p s t", s=3)
        conv_y = cut(SEQ + NS)
        conv_t = cut(SEQ + NS)
        kqv1 = cut(3 * SEQ).rearrange("p (s t) -> p s t", s=3)
        kqv = [kqv0, kqv1]
        kg = cut(SEQ).rearrange("p (c t) -> p c t", t=P)
        vs = cut(SEQ).rearrange("p (c t) -> p c t", t=P)
        attn = cut(SEQ).rearrange("p (c t) -> p c t", t=P)
        o_tok = cut(SEQ).rearrange("p (c t) -> p c t", t=P)
        a1 = cut(SEQ).rearrange("p (c t) -> p c t", t=P)
        st = cut(P)
        rr, vp, qs = cut(P), cut(P), cut(P)
        head_top = o
        dnc = cut(3 * H * 27).rearrange("p (n s t) -> p n s t", s=9, t=3)
        samp = cut(H * 3 * NS).rearrange("p (h s t) -> p h s t", h=H, s=3)
        gates = cut(H * 35).rearrange("p (h k c) -> p h k c", h=H, k=7)
        KG, KNG, KEG, KNEG, KEK, KEL, KBETA = range(7)
        fa = full[:, 0:8, :].rearrange("p k t -> p (k t)")
        dec = fa[:, 0:512].rearrange("p (c t) -> p c t", t=P)
        mt = fa[:, 512:1024].rearrange("p (c t) -> p c t", t=P)
        mtl = [fa[:, 1024 + 512 * i:1536 + 512 * i].rearrange("p (c t) -> p c t", t=P) for i in range(2)]
        gB = fa[:, 2048:2560].rearrange("p (c t) -> p c t", t=P)
        xx = fa[:, 2560:3584].rearrange("p (s c t) -> p s c t", s=2, t=P)
        sqkq = fa[:, 3584:4608].rearrange("p (s t) -> p s t", s=2)
        sqkq_c = fa[:, 3584:4608].rearrange("p (s c t) -> p (s c) t", s=2, t=P)
        on = fa[:, 3584:4096].rearrange("p (c t) -> p c t", t=P)
        hs = small[:, 0:35].rearrange("p (k c) -> p k c", k=7)
        cw = [small[:, 40:52], small[:, 52:64]]
        ssum, nrm, rn = small[:, 64:72], small[:, 72:80], small[:, 80:88]
        bp, bn = small[:, 88:92], small[:, 92:96]
        osum, f_a, f_b = small[:, 96:100], small[:, 100:104], small[:, 104:108]
        mhalf = small[:, 108:124]
        dng = small[:, 124:125]
        ea = small[:, 128:136]
        lg, lb = small[:, 136:152], small[:, 152:168]
        sm4 = small[:, 168:464]

        cb = 0

        def tiny(n):
            nonlocal cb
            cb += n
            assert cb <= 296
            return sm4[:, cb - n:cb]

        nmax, esum, esink, dsink = ([tiny(4), tiny(4)] for _ in range(4))
        amax, nmax_s, esum_s, amax_s, dsink_s = tiny(4), tiny(8), tiny(8), tiny(8), tiny(8)
        sos, ssum_s, nrm_s, rn_s = tiny(8), tiny(16)[0:NS], tiny(16)[0:NS], tiny(16)[0:NS]
        bn_s, bp_s, fa_s, fb_s = (tiny(8)[0:NS] for _ in range(4))
        egl_s = tiny(64).rearrange("p (h b) -> p h b", h=H)
        sos = sos[0:NS]
        eps_p2 = tiny(8)
        mh = mhalf

        x_in = [sem(f"x_in{i}") for i in range(4)]
        cst_in, par_in, prev_in = sem("cst_in"), sem("par_in"), sem("prev_in")
        raw_in = [sem("raw_in0"), sem("raw_in1")]
        whi_done, wlo_done = sem("whi_done"), sem("wlo_done")
        w_used = sem("w_used")
        acc_free = [sem("acc_free0"), sem("acc_free1")]
        ahi_done, alo_even, alo_odd = sem("ahi_done"), sem("alo_even"), sem("alo_odd")
        scaled, sq_used = sem("scaled"), sem("sq_used")
        sq_done, sq_summed = sem("sq_done"), sem("sq_summed")
        norm_sum, var_ready, root = sem("norm_sum"), sem("var_ready"), sem("root")
        dve_t, act_t, pool_t = Tally(sem("dve_order")), Tally(sem("act_order")), Tally(sem("pool_order"))
        pe_h, dve_h = Steps(sem("pe_head"), PE_HEAD), Steps(sem("dve_head"), DVE_HEAD)
        act_h, pool_h = Steps(sem("act_head"), ACT_HEAD), Steps(sem("pool_head"), POOL_HEAD)
        conv_copied, conv_tanh, conv_done = sem("conv_copied"), sem("conv_tanh"), sem("conv_done")
        conv_silu = sem("conv_silu")
        prev_put, last_taken = sem("prev_put"), sem("last_taken")
        z_tanh = sem("z_tanh")
        state_out = sem("state_out")
        out_small, vnew_stored, dnc_stored = sem("out_small"), sem("vnew_stored"), sem("dnc_stored")
        prep, prep_pe, prep_act = sem("prep"), sem("prep_pe"), sem("prep_act")
        s0_in = [sem("s0_in0"), sem("s0_in1")]
        sdn_stored = [sem("sdn_stored0"), sem("sdn_stored1")]
        ys_done = sem("ys_done")
        gated, halved = sem("gated"), sem("halved")
        samp_pe, samp_dve = sem("samp_pe"), sem("samp_dve")
        samp_act, samp_pool = sem("samp_act"), sem("samp_pool")
        kc_in, vc_in = sem("kc_in"), sem("vc_in")
        vtok_pe, vtok_done = sem("vtok_pe"), sem("vtok_done")
        scores, biased, exped, probs = sem("scores"), sem("biased"), sem("exped"), sem("probs")
        turned, turned_out, weighed, attn_out = sem("turned"), sem("turned_out"), sem("weighed"), sem("attn_out")
        q_samp_put = sem("q_samp_put")
        sa_pe, sa_dve, sa_act = sem("sa_pe"), sem("sa_dve"), sem("sa_act")
        res_in = [sem("res_in0"), sem("res_in1")]
        res_free, x1_stored = sem("res_free"), sem("x1_stored")
        u_free, uprev_in = [sem("u_free0"), sem("u_free1")], [sem("uprev_in0"), sem("uprev_in1")]
        gate_tanh, cf_stored = sem("gate_tanh"), sem("cf_stored")
        tap_prod, tap_sum, c_done, c_summed = sem("tap_prod"), sem("tap_sum"), sem("c_done"), sem("c_summed")
        zz_tanh = sem("zz_tanh")
        centred, ln_sq, ln_aff, ln_tanh, y_done = (sem("centred"), sem("ln_sq"), sem("ln_aff"), sem("ln_tanh"),
                                                   sem("y_done"))
        ln_scaled = sem("ln_scaled")
        fin_stored = sem("fin_stored")
        n_small = 10
        finals = [(x1_stored, 16 * KT), (state_out, 16 * H), (dnc_stored, 16), (out_small, 16 * n_small),
                  (vnew_stored, 32), (sdn_stored[0], 16 * (H // 2)), (sdn_stored[1], 16 * (H // 2)),
                  (cf_stored, 32 * KT), (fin_stored, 16 * KT)]
        block = ctx.enter_context(nc.Block())

        kv = arena[:, 0:4 * TOK].rearrange("p (s t) -> p s t", s=4)
        v_tok = arena[:, 2304:3328].rearrange("p (c r d) -> p c r d", c=NC, r=2)
        kc = arena[:, 3328:5376].rearrange("p (r b t) -> p r b t", r=2, b=NB)
        vc = arena[:, 5376:7424].rearrange("p (b d) -> p b d", b=NB)
        prob = [arena[:, 7424 + 1024 * i:8448 + 1024 * i].rearrange("p (g t) -> p g t", g=4)
                for i in range(2)]
        probT = arena[:, 9472:10496].rearrange("p (w g t) -> p w g t", w=2, g=4)
        zs_samp = arena[:, 10988:11500].rearrange("p (k a c) -> p k a c", k=8, a=2)
        prob_s = arena[:, 7424:8512].rearrange("p (b t) -> p b t", b=NB)
        probT_s = arena[:, 8512:9536].rearrange("p (b t) -> p b t", b=NB)
        q_samp = arena[:, 8512:9024].rearrange("p (r b q) -> p r b q", r=2, b=NB)
        probT_n = arena[:, 9536:10560].rearrange("p (b t) -> p b t", b=NB)
        v_new = arena[:, 2304:4352 - 1024].rearrange("p (b d) -> p b d", b=NB)
        s0 = [arena[:, 2304 + 1024 * i:3328 + 1024 * i].rearrange("p (b d) -> p b d", b=NB) for i in range(2)]
        vpx = arena[0:NS, 4352:5376].rearrange("p (b d) -> p b d", b=NB)
        ksqs = arena[:, 5376:5504].rearrange("p (s t) -> p s t", s=2)
        rs_, vps, qss = arena[0:NS, 5504:5632], arena[0:NS, 5632:5760], arena[0:NS, 5760:5888]
        o_s = arena[0:NS, 5888:6912].rearrange("p (h d) -> p h d", h=H)
        sq_s = arena[:, 5888:6912].rearrange("p (h t) -> p h t", h=H)
        a1_s = arena[0:NS, 6912:7424].rearrange("p (h t) -> p h t", h=H)
        dec_s, mt_s, gB_s, x_s = (arena[0:NS, 2304 + 512 * i:2816 + 512 * i].rearrange("p (h t) -> p h t", h=H)
                                  for i in range(4))
        mtl_s = [arena[0:NS, 4352 + 512 * i:4864 + 512 * i].rearrange("p (h t) -> p h t", h=H)
                 for i in range(2)]
        attn_s = arena[0:NS, 10364:10876].rearrange("p (h t) -> p h t", h=H)
        xt_s = arena[0:NS, 10876:11388].rearrange("p (h t) -> p h t", h=H)
        kg_s = fa[0:NS, 2304:3328].rearrange("p (h d) -> p h d", h=H)
        vs_s = fa[0:NS, 3328:4352].rearrange("p (h d) -> p h d", h=H)
        za_t = arena[:, 11500:11500 + TOK]
        sqb4 = [arena[:, i * TOK:(i + 1) * TOK] for i in range(4)]
        ab_t = arena[:, 7000:7000 + TOK]
        xm, sp_e, tb, xa = (arena[:, 7680 + 40 * i:7720 + 40 * i].rearrange("p (c k) -> p c k", k=8) for i in range(4))
        gmask = arena[0:NS, 6936:7000].rearrange("p (h b) -> p h b", h=H)
        ab_tok = arena[:, 7600:7680].rearrange("p (c k) -> p c k", k=16)
        sqb = [arena[:, 0:TOK], arena[:, TOK:2 * TOK]]
        res = [arena[:, 2 * TOK:3 * TOK], arena[:, 3 * TOK:4 * TOK]]
        ssq, rstd = arena[:, 4 * TOK:5 * TOK], arena[:, 5 * TOK:6 * TOK]
        LIN = CP + SEQ + NB * (CP + NT)
        u_in = [arena[:, 6 * TOK + LIN * i:6 * TOK + LIN * (i + 1)] for i in range(2)]
        o = 6 * TOK + 2 * LIN
        u_p = [u[:, 0:CP + SEQ] for u in u_in]
        u_s = [u[:, CP + SEQ:LIN].rearrange("p (b t) -> p b t", b=NB) for u in u_in]
        c_buf = arena[:, o:o + TOK]
        prod = [arena[:, o + 8 * TOK + i * SEQ:o + 8 * TOK + (i + 1) * SEQ] for i in range(2)]
        pacc = arena[:, o + 8 * TOK + 2 * SEQ:o + 8 * TOK + 3 * SEQ]
        tg = [arena[:, 3 * TOK:4 * TOK], arena[:, o + TOK:o + 2 * TOK]]
        csum, mean = ssq, rstd
        zring = [arena[:, o + (2 + i) * TOK:o + (3 + i) * TOK] for i in range(ZRING)]

        def acc_of(s):
            return acc[:, s, :, 0:HALF]

        def per_row(ap, n):
            return ap.unsqueeze(2).to_broadcast([ap.shape[0], ap.shape[1], n])

        def per_group(ap, g):
            return ap.unsqueeze(1).to_broadcast([ap.shape[0], g, ap.shape[1]])

        @block.sync
        def _(sp):
            def weights(n, first=False):
                for half in range(2):
                    if not first:
                        sp.wait_ge(wlo_done, 2 * n + half - 1)
                    sp.dma_start(w_raw[:, half, :], wt[n, :, half * 1024:(half + 1) * 1024]) \
                        .then_inc(raw_in[half], 16)

            sp.dma_start(cst[:], const).then_inc(cst_in, 16)
            for i in range(4):
                sp.dma_start(full[:, 4 * i:4 * i + 4, :], x[4 * i:4 * i + 4].rearrange("k p t -> p k t")) \
                    .then_inc(x_in[i], 16)
            sp.dma_start(par[:], param).then_inc(par_in, 16)
            weights(0, first=True)
            sp.dma_start(dnc[:, :, 1:9, :], dn_prev).then_inc(prev_in, 16)
            with sp.Fori(1, N_Q) as n:
                weights(n)

            def sampled_state(h):
                if h == 0:
                    sp.wait_ge(samp_dve, SD["Xt2"])
                if h >= 2:
                    sp.wait_ge(sdn_stored[h % 2], 16 * (h // 2))
                sp.dma_start(s0[h % 2], state_in[h].rearrange("p (b d) -> p b d", b=NB)).then_inc(s0_in[h % 2], 16)

            for n, heads in ((0, ()), (1, ()), (2, (0, 1)), (3, (2, 3)), (4, (4, 5, 6, 7))):
                weights(N_Q + n)
                for h in heads:
                    sampled_state(h)
            for n in range(N_Q + 5, N_ZA + 1):
                weights(n)
            for i in range(2):
                sp.wait_ge(sdn_stored[i], 16 * (H // 2))
            sp.wait_ge(ys_done, 1)
            sp.dma_start(kc, k_cache.rearrange("r p b t -> p r b t")).then_inc(kc_in, 16)
            sp.dma_start(vc, v_cache.rearrange("p (b d) -> p b d", b=NB)).then_inc(vc_in, 16)
            for n in range(N_ZA + 1, N_OUT0):
                weights(n)

            def out_section(n0, source):
                weights(n0)
                weights(n0 + 1)
                if n0 == N_OUT0:
                    sp.wait_ge(res_free, 1)
                else:
                    sp.wait_ge(acc_free[0], N_VG // 2 + 1 + KT)
                    sp.wait_ge(x1_stored, 16 * KT)
                for j in range(2):
                    sp.dma_start(res[j], source[j]).then_inc(res_in[j], 16)
                with sp.Fori(0, KT // 2 - 1) as i:
                    for j in range(2):
                        weights(2 * i + (n0 + 2 + j))
                        sp.wait_ge(acc_free[1 - j], i + ((n0 + j) // 2 + 1))
                        sp.dma_start(res[j], source[2 * i + 2 + j]).then_inc(res_in[j], 16)

            out_section(N_OUT0, x)
            with sp.Fori(0, KT // 2) as i:
                for b in range(2):
                    weights(4 * i + (N_VG + 2 * b))
                    weights(4 * i + (N_VG + 2 * b + 1))
                    sp.wait_ge(u_free[b], i + 1)
                    sp.dma_start(u_s[b][:, :, 0:CP], cf_prev[2 * i + b]).then_inc(uprev_in[b], 16)
            with sp.Fori(N_Z1, N_OUT1) as n:
                weights(n)
            out_section(N_OUT1, x1_dram)
            for s, v in finals:
                sp.wait_ge(s, v)

        @block.tensor
        def _(pe):
            def proj(m, s, e, turn=None):
                half = e // 4
                if e % 4 == 0:
                    pe.wait_ge(wlo_done, 4 * m + (2 * s + half + 1))
                if e == 0 and not (isinstance(m, int) and m == 0):
                    pe.wait_ge(acc_free[s], m)
                for k in (2 * e, 2 * e + 1):
                    if turn is not None:
                        pe.wait_ge((alo_even, alo_odd)[k % 2], 8 * turn + k // 2 + 1)
                    wk = slice(k * P, (k + 1) * P)
                    for j, (w, a) in enumerate(((w_hi, act_hi), (w_hi, act_lo), (w_lo, act_hi))):
                        for i in range(2):
                            ins = pe.matmul(acc[:, s, i, 0:HALF], w[:, s, wk], a[:, k, i * HALF:(i + 1) * HALF],
                                            start=(k == 0 and j == 0), stop=(k == KT - 1 and j == 2))
                if e % 4 == 3:
                    ins.then_inc(w_used, 1)

            def tile_of(m, s, turn=None):
                for e in range(8):
                    proj(m, s, e, turn)

            def sum_channels(source):
                for i in range(2):
                    ins = pe.matmul(gp[:, i, 0:HALF], ones, source[:, i * HALF:(i + 1) * HALF],
                                    start=True, stop=True)
                ins.then_inc(norm_sum, 1)

            pe.wait_ge(cst_in, 16)
            for k in range(KT):
                pe.wait_ge(sq_done, k + 1)
                for i in range(2):
                    ins = pe.matmul(gp[:, i, 0:HALF], ones, sqb4[k % 4][:, i * HALF:(i + 1) * HALF],
                                    start=(k == 0), stop=(k == KT - 1))
                ins.then_inc(sq_used, 1)
            tile_of(0, 0, turn=0)

            def gates_pe():
                pe.wait_ge(acc_free[0], 1)
                for c in range(NC):
                    pe.transpose(gp[:, 0, 16 * c:16 * c + 16], ab_t[0:16, c * P:(c + 1) * P], ident[0:16, 0:16])
                pe.transpose(gp[0:NS, 0, 64:80], ab_t[0:16, SEQ:SEQ + NS], ident[0:16, 0:16]).then_inc(prep_pe, 1)
                pe.wait_ge(prep, 2)
                gk = gates[:, :, KG, 0:4]
                gks = gates[0:NS, :, KG, 4]
                pe.matmul(gp[:, 1, 80:144], ones[0:NS, :], gmask.rearrange("p h b -> p (h b)"), start=True, stop=True)
                pe.matmul(gp[:, 1, 0:32], tri, gk, start=True, stop=True)
                pe.matmul(gp[:, 1, 32:64], ones, gk, start=True, stop=True)
                pe.matmul(gp[0:NS, 1, 64:72], cst[0:NS, C_TRIS:C_TRIS + NS], gks, start=True, stop=True)
                pe.matmul(gp[0:NS, 1, 72:80], cst[0:NS, C_ONES:C_ONES + NS], gks, start=True,
                          stop=True).then_inc(prep_pe, 1)

            def head_step(it, kb, name):
                kt, qt, vt = kqv[kb][:, 0, :], kqv[kb][:, 1, :], kqv[kb][:, 2, :]
                ck = lambda c: slice(c * P, (c + 1) * P)
                if name == "kv_tok":
                    pe.wait_ge(conv_silu, 3 * it + 3)
                    if not (isinstance(it, int) and it == 0):
                        pe.wait_ge(dve_h.sem, dve_h.at("y", it - 1))
                    else:
                        pe.wait_ge(prep, 4)
                    for c in range(NC):
                        pe.transpose(gp[:, 0, ck(c)], kt[:, ck(c)], ident)
                    for c in range(NC):
                        ins = pe.transpose(gp[:, 1, ck(c)], vt[:, ck(c)], ident)
                elif name == "gcum":
                    pe.wait_ge(pool_h.sem, pool_h.at("gB", it))
                    for c in range(NC):
                        ins = pe.matmul(gp[:, 2, ck(c)], gB[:, c, :], tri, start=True, stop=True)
                elif name == "norm":
                    pe.wait_ge(act_h.sem, act_h.at("sq", it))
                    for c in range(8):
                        ins = pe.matmul(gp[:, 3, c:c + 1], sqkq_c[:, c, :], ones[:, 0:1], start=True, stop=True)
                elif name == "gram":
                    pe.wait_ge(dve_h.sem, dve_h.at("ssum", it))
                    for c in range(NC):
                        ins = pe.matmul(gp[:, 2 + c // 2, (c % 2) * 256:(c % 2) * 256 + 256], kt[:, ck(c)],
                                        kqv[kb][:, 0:2, ck(c)], start=True, stop=True)
                elif name == "m0":
                    pe.wait_ge(pool_h.sem, pool_h.at("L0", it))
                    pe.wait_ge(dve_h.sem, dve_h.at("vs", it))
                    for c in range(NC):
                        ins = pe.transpose(gp[:, 0, ck(c)], mtl[0][:, c, :], ident)
                elif name[0] == "a":
                    l = int(name[1])
                    pe.wait_ge(pool_h.sem, pool_h.at(f"L{l}", it))
                    pe.wait_ge(dve_h.sem, dve_h.at("Xt" if l == 1 else f"X{l - 1}", it))
                    for c in range(NC):
                        ins = pe.matmul(gp[:, 1, ck(c)], mtl[l % 2][:, c, :], xx[:, 0, c, :], start=True, stop=True)
                elif name[0] == "x":
                    l = int(name[1])
                    pe.wait_ge(act_h.sem, act_h.at(f"A{l}", it))
                    if l == 1:
                        pe.wait_ge(dve_h.sem, dve_h.at("attn", it))
                    if l < LEVELS - 1:
                        for c in range(NC):
                            pe.matmul(gp[:, 2, ck(c)], xx[:, 1, c, :], a1[:, c, :], start=True, stop=True)
                    for c in range(NC):
                        ins = pe.matmul(gp[:, 3, ck(c)], a1[:, c, :], xx[:, 1, c, :], start=True, stop=True)
                elif name == "o_chan":
                    pe.wait_ge(dve_h.sem, dve_h.at("on", it))
                    for c in range(NC):
                        ins = pe.transpose(gp[:, 0, ck(c)], on[:, c, :], ident)
                elif name[0:2] == "so":
                    c = int(name[2])
                    pe.wait_ge(dve_h.sem, dve_h.at(f"vp{c}", it))
                    pe.matmul(gp[:, 3, 0:P], kg[:, c, :], vp, start=True, stop=True)
                    ins = pe.matmul(gp[:, 0, 0:P], attn[:, c, :], vp, start=True, stop=True)
                elif name[0] == "s":
                    c = int(name[1])
                    pe.wait_ge(dve_h.sem, dve_h.at(f"o{c - 1}", it))
                    if c > 1:
                        pe.wait_ge(act_h.sem, act_h.at(f"q{c - 1}", it))
                    pe.matmul(gp[:, 0, 0:P], kt[:, ck(c)], st, start=True, stop=True)
                    ins = pe.matmul(gp[:, 1, 0:P], qt[:, ck(c)], st, start=True, stop=True)
                elif name[0] == "u":
                    c = int(name[1])
                    pe.wait_ge(dve_h.sem, dve_h.at(f"X{LEVELS - 1}" if c == 0 else f"r{c}", it))
                    ins = pe.matmul(gp[:, 2, 0:P], xx[:, 1, c, :], vs[:, 0, :] if c == 0 else rr,
                                    start=True, stop=True)
                ins.then_inc(pe_h.sem, 1)

            def head_unit(hp, it=None, kb=0):
                for ti in range(4):
                    for e in range(8):
                        proj(2 * hp + (1 + ti) // 2, (1 + ti) % 2, e)
                        if it is not None and 8 * ti + e in PE_PLAN:
                            head_step(it, kb, PE_PLAN[8 * ti + e])

            for ti in range(4):
                tile_of((1 + ti) // 2, (1 + ti) % 2)
                if ti == 0:
                    gates_pe()
            with pe.Fori(0, 3) as i:
                head_unit(2 * i + 1, 2 * i, 0)
                head_unit(2 * i + 2, 2 * i + 1, 1)
            head_unit(7, 6, 0)
            head_unit(8, 7, 1)

            def samp_step(name, h=None):
                col = lambda h: slice((h % 4) * P, (h % 4 + 1) * P)
                sc = lambda h: slice(h * NS, (h + 1) * NS)
                if name == "k_tok":
                    pe.wait_ge(dve_h.sem, dve_h.at("y", H - 1))
                    pe.wait_ge(conv_silu, 3 * H)
                    for h in range(H):
                        ins = pe.transpose(gp[0:NS, h // 4, col(h)], samp[:, h, 0, :], ident)
                elif name == "v_tok":
                    pe.wait_ge(samp_dve, SD["kg"])
                    for h in range(H):
                        ins = pe.transpose(gp[0:NS, 2 + h // 4, col(h)], samp[:, h, 2, :], ident)
                elif name == "norm":
                    pe.wait_ge(samp_act, SA["sq"])
                    for h in range(H):
                        for j in range(2):
                            ins = pe.matmul(gp[0:NS, 0, 2 * h + j:2 * h + j + 1], sq_s[:, h, j * NS:(j + 1) * NS],
                                            ones[:, 0:1], start=True, stop=True)
                elif name == "gram":
                    pe.wait_ge(samp_dve, SD["ssum"])
                    for h in range(H):
                        ins = pe.matmul(gp[0:NS, h // 4, col(h)], samp[:, h, 0, :], samp[:, h, 0:2, :],
                                        start=True, stop=True)
                elif name == "gcum":
                    pe.wait_ge(samp_dve, SD["vs"])
                    pe.wait_ge(samp_pool, SP_["gB"])
                    for h in range(H):
                        ins = pe.matmul(gp[0:NS, 2, sc(h)], gB_s[:, h, :], cst[0:NS, C_TRIS:C_TRIS + NS],
                                        start=True, stop=True)
                elif name == "m0":
                    pe.wait_ge(samp_pool, SP_["L0"])
                    for h in range(H):
                        ins = pe.transpose(gp[0:NS, 2, sc(h)], mtl_s[0][:, h, :], ident[0:NS, 0:NS])
                elif name in ("a1", "a2"):
                    l = int(name[1])
                    pe.wait_ge(samp_pool, SP_[f"L{l}"])
                    pe.wait_ge(samp_dve, SD["Xt"] if l == 1 else SD["Xt1"])
                    for h in range(H):
                        ins = pe.matmul(gp[0:NS, 3, sc(h)], mtl_s[l % 2][:, h, :], x_s[:, h, :], start=True, stop=True)
                elif name in ("x1", "x2"):
                    l = int(name[1])
                    pe.wait_ge(samp_act, SA[f"A{l}"])
                    if l == 1:
                        for h in range(H):
                            pe.matmul(gp[0:NS, 2, sc(h)], xt_s[:, h, :], a1_s[:, h, :], start=True, stop=True)
                    for h in range(H):
                        ins = pe.matmul(gp[0:NS, 0, sc(h)], a1_s[:, h, :], xt_s[:, h, :], start=True, stop=True)
                elif name == "st":
                    pe.wait_ge(s0_in[h % 2], 16 * (h // 2 + 1))
                    pe.wait_ge(samp_dve, SD["Xt2"] if h == 0 else SD[f"vp{h - 1}"])
                    for b in range(NB):
                        ins = pe.matmul(gp[:, 2, 0:2 * NS].rearrange("p (s t) -> p s t", s=2)[:, :, b * NT:(b + 1) * NT],
                                        s0[h % 2][:, b, :], samp[:, h, 0:2, b * NT:(b + 1) * NT],
                                        start=True, stop=True)
                elif name == "tr":
                    pe.wait_ge(samp_act, SA[f"ks{h}"])
                    if h:
                        pe.wait_ge(samp_dve, SD[f"S{h - 1}"])
                    pe.transpose(gp[0:NS, 3, 0:P], ksqs[:, 0, :], ident)
                    ins = pe.transpose(gp[0:NS, 1, 0:P], ksqs[:, 1, :], ident)
                elif name == "u":
                    pe.wait_ge(samp_dve, SD[f"r{h}"])
                    ins = pe.matmul(gp[0:NS, 2, 0:P], xt_s[:, h, :], rs_, start=True, stop=True)
                elif name == "o":
                    pe.wait_ge(samp_dve, SD[f"vp{h}"])
                    ins = pe.matmul(gp[0:NS, 3, 0:P], attn_s[:, h, :], vps, start=True, stop=True)
                elif name == "ns":
                    pe.wait_ge(samp_pool, SP_[f"vx{h}"])
                    pe.wait_ge(samp_act, SA[f"q{h}"])
                    for i in range(2):
                        ins = pe.matmul(gp[:, i, :], kg_s[:, h, :], vpx[:, 4 * i:4 * i + 4, :], start=True, stop=True)
                elif name == "o_chan":
                    pe.wait_ge(samp_dve, SD["on"])
                    for h in range(H):
                        ins = pe.transpose(gp[:, 2, sc(h)], o_s[:, h, :], ident[0:NS, 0:NS])
                ins.then_inc(samp_pe, 1)

            for t in range(4):
                for e in range(8):
                    proj(N_Q // 2 + (t + N_Q % 2) // 2, (N_Q + t) % 2, e)
                    for name, h in SAMP_PLAN[8 * t + e]:
                        samp_step(name, h)

            pe.wait_ge(ys_done, 1)
            for r in range(2):
                for c in range(NC):
                    ins = pe.transpose(gp[:, r, c * P:(c + 1) * P], kv[:, 2 * r + 1, blk(c):blk(c) + P], ident)
            ins.then_inc(vtok_pe, 1)

            def att_scores(u):
                r, c, jj = u // 8, (u // 2) % 4, u % 2
                n = N_Q + 4 * r + 3
                pe.wait_ge(acc_free[n % 2], n // 2 + 1)
                if u == 0:
                    pe.wait_ge(vtok_done, 1)
                else:
                    pe.wait_ge(biased, u)
                for q in range(2):
                    rows = slice(64 * q, 64 * q + 64)
                    for j in range(2):
                        lhs = full[rows, 4 * r + 2 * jj + j, blk(c):blk(c) + P]
                        for w in range(0 if c else 1, 2):
                            ins = pe.matmul(gp[:, q, j * 256 + w * P:j * 256 + (w + 1) * P], lhs,
                                            kv[rows, 2 * r, blk(c - 1 + w):blk(c - 1 + w) + P],
                                            start=True, stop=True)
                ins.then_inc(scores, 1)

            def att_turn(u):
                c = (u // 2) % 4
                pe.wait_ge(probs, u + 1)
                if u:
                    pe.wait_ge(attn_out, u)
                for w in range(0 if c else 1, 2):
                    for g in range(4):
                        ins = pe.transpose(gp[:, 2 + w, g * P:(g + 1) * P], prob[u % 2][:, g, w * P:(w + 1) * P], ident)
                ins.then_inc(turned, 1)

            def att_weigh(u):
                r, c = u // 8, (u // 2) % 4
                pe.wait_ge(turned_out, u + 1)
                for q in range(2):
                    for w in range(0 if c else 1, 2):
                        ins = pe.matmul(gp[64 * q:64 * q + 64, 2, 0:256], v_tok[:, c - 1 + w, r, 64 * q:64 * q + 64],
                                        probT[:, w, 2 * q:2 * q + 2, :], start=(w == (0 if c else 1)), stop=(w == 1))
                ins.then_inc(weighed, 1)

            def sampled_attention(name):
                if name == "scores":
                    pe.wait_ge(kc_in, 16)
                    pe.wait_ge(biased, 16)
                    pe.wait_ge(attn_out, 16)
                    pe.wait_ge(q_samp_put, 4)
                    for b in range(NB):
                        sc = (b // 4) * HALF + HP + (b % 4) * NT
                        for g in range(4):
                            rows = slice(64 * (g % 2), 64 * (g % 2) + 64)
                            lhs = q_samp[rows, g // 2, b, :]
                            o_ = gp[32 * g:32 * g + 32, b // 3, (b % 3) * 136:(b % 3) * 136 + 136]
                            pe.matmul(o_[:, 0:W], lhs, kc[rows, g // 2, b, :], start=True, stop=True)
                            ins = pe.matmul(o_[:, W:W + NT], lhs, kv[rows, 2 * (g // 2), sc:sc + NT],
                                            start=True, stop=True)
                elif name == "turn":
                    pe.wait_ge(sa_dve, SAD["prob"])
                    for b in range(NB):
                        ins = pe.transpose(gp[:, b // 4, (b % 4) * P:(b % 4 + 1) * P], prob_s[:, b, 0:W], ident)
                elif name == "turn_new":
                    for b in range(NB):
                        ins = pe.transpose(gp[0:NT, 2 + b // 4, (b % 4) * P:(b % 4 + 1) * P], prob_s[:, b, W:W + NT],
                                           ident)
                elif name[0:5] == "v_new":
                    r = int(name[5])
                    pe.wait_ge(sa_act if r == 0 else sa_dve, SAA["turned"] if r == 0 else SAD["out0"])
                    if r == 0:
                        pe.wait_ge(sa_dve, SAD["turned_new"])
                    for b in range(NB):
                        sc = (b // 4) * HALF + HP + (b % 4) * NT
                        ins = pe.transpose(gp[0:NT, b // 4, (b % 4) * P:(b % 4 + 1) * P],
                                           kv[:, 2 * r + 1, sc:sc + NT], ident)
                elif name[0:5] == "weigh":
                    r = int(name[5])
                    pe.wait_ge(sa_act, SAA[f"v_new{r}"])
                    pe.wait_ge(vc_in, 16)
                    for q in range(2):
                        g = 2 * r + q
                        for b in range(NB):
                            o_ = gp[64 * q:64 * q + 64, 2, 0:256].rearrange("p (j b t) -> p b j t", j=4, b=NB)[:, b]
                            pe.matmul(o_, vc[:, b, 64 * g:64 * g + 64], probT_s[:, b, 32 * g:32 * g + 32],
                                      start=True, stop=False)
                            ins = pe.matmul(o_, v_new[0:NT, b, 64 * q:64 * q + 64],
                                            probT_n[0:NT, b, 32 * g:32 * g + 32], start=False, stop=True)
                ins.then_inc(sa_pe, 1)

            def attention_unit(u, e):
                if e == 1:
                    att_scores(u)
                    if u:
                        att_turn(u - 1)
                if e == 3 and u:
                    att_weigh(u - 1)

            for t in range(4, 8):
                for e in range(8):
                    n = N_Q + t
                    proj(n // 2, n % 2, e)
                    attention_unit(2 * (t - 4) + e // 4, e % 4)
            for t in range(8):
                for e in range(8):
                    n = N_ZA + t
                    proj(n // 2, n % 2, e)
                    if t < 4:
                        attention_unit(8 + 2 * t + e // 4, e % 4)
                    elif 8 * (t - 4) + e in SATT_PLAN:
                        if SATT_PLAN[8 * (t - 4) + e] == "last_turn":
                            att_turn(15)
                        elif SATT_PLAN[8 * (t - 4) + e] == "last":
                            att_weigh(15)
                        else:
                            sampled_attention(SATT_PLAN[8 * (t - 4) + e])
            def out_section(n0, turn):
                tile_of(n0 // 2, n0 % 2, turn)
                assert n0 % 2 == 1
                with pe.Fori(0, KT // 2 - 1) as i:
                    tile_of(i + (n0 + 1) // 2, 0)
                    tile_of(i + (n0 + 1) // 2, 1)
                tile_of((n0 + KT - 1) // 2, 0)
                pe.wait_ge(sq_summed, KT if turn == 1 else 2 * KT)
                sum_channels(ssq)

            out_section(N_OUT0, 1)
            tile_of(N_VG // 2, N_VG % 2, turn=2)
            tile_of((N_VG + 1) // 2, (N_VG + 1) % 2)
            with pe.Fori(0, KT - 1) as i:
                tile_of(i + (N_VG + 2) // 2, (N_VG + 2) % 2)
                tile_of(i + (N_VG + 3) // 2, (N_VG + 3) % 2)

            def z_tiles(first, pairs):
                n = N_Z1 + first
                with pe.Fori(0, pairs) as i:
                    tile_of(i + n // 2, n % 2)
                    tile_of(i + (n + 1) // 2, (n + 1) % 2)

            z_tiles(0, 1)
            pe.wait_ge(c_summed, KT)
            sum_channels(csum)
            z_tiles(2, 2)
            pe.wait_ge(c_summed, 2 * KT)
            sum_channels(csum)
            z_tiles(6, 5)
            out_section(N_OUT1, 3)

        @block.scalar
        def _(act):
            def copy(out, in_, scale=1.0):
                return act.activation(out, in_, ACT.Copy, scale=scale)

            def split_hi(m, s, half):
                act.wait_ge(raw_in[half], 32 * m + (16 * s + 16))
                if not (isinstance(m, int) and m == 0):
                    act.wait_ge(w_used, 4 * m + (2 * s - 3 + half))
                hs_ = slice(half * 1024, (half + 1) * 1024)
                copy(w_hi[:, s, hs_], w_raw[:, half, :]).then_inc(whi_done, 1)

            def next_split(m, s, e):
                if e in (0, 4):
                    split_hi(m + s, 1 - s, e // 4)

            def tile_done(m, s):
                act.wait_ge(w_used, 4 * m + (2 * s + 2))

            def act_split(turn):
                for k in range(KT):
                    if turn in (0, 2):
                        act.wait_ge(scaled, 8 * turn + k + 1)
                    copy(act_hi[:, k, :], full[:, k, :]).then_inc(ahi_done, 1)

            def take_root(turn):
                act.wait_ge(var_ready, turn + 1)
                act.activation(ssq, ssq, ACT.Sqrt).then_inc(root, 1)

            for k in range(KT):
                act.wait_ge(x_in[k // 4], 16)
                if k >= 4:
                    act.wait_ge(sq_used, k - 3)
                act.activation(sqb4[k % 4], full[:, k, :], ACT.Square).then_inc(sq_done, 1)
            split_hi(0, 0, 0)
            split_hi(0, 0, 1)
            take_root(0)
            split_hi(0, 1, 0)
            act_split(0)
            split_hi(0, 1, 1)

            def head_act(it, kb, name):
                if name == "sq":
                    act.wait_ge(conv_silu, 3 * it + 3)
                    if not (isinstance(it, int) and it == 0):
                        act.wait_ge(pe_h.sem, pe_h.at("o_chan", it - 1))
                    ins = act.activation(sqkq, kqv[kb][:, 0:2, :], ACT.Square)
                elif name == "decay":
                    act.wait_ge(dve_h.sem, dve_h.at("dmask", it))
                    for c in range(NC):
                        ins = act.activation(dec[:, c, :], dec[:, c, :], ACT.Exp, bias=hs[:, KNG, c:c + 1])
                elif name[0] == "A":
                    act.wait_ge(pe_h.sem, pe_h.at(f"a{name[1]}", it))
                    ins = copy(a1, bank4(1))
                elif name[0] == "q":
                    c = int(name[1])
                    act.wait_ge(pe_h.sem, pe_h.at(f"s{c}", it))
                    ins = copy(qs, gp[:, 1, 0:P], hs[:, KEG, c:c + 1])
                elif name == "osq":
                    act.wait_ge(dve_h.sem, dve_h.at("o3", it))
                    for c in range(NC):
                        ins = act.activation(a1[:, c, :], o_tok[:, c, :], ACT.Square, accum_out=osum[:, c:c + 1])
                ins.then_inc(act_h.sem, 1)

            def evacuate_qkv(hp, j):
                m, s = 2 * hp + (1 + j) // 2, (1 + j) % 2
                tile_done(m, s)
                if not (isinstance(hp, int) and hp == 0 and j == 0):
                    act.wait_ge(conv_done, 3 * hp + j)
                    act.wait_ge(last_taken, 3 * hp + j)
                copy(halves(cin_p[:, 3:3 + SEQ]), acc[:, s, :, 0:HP])
                copy(cin_s[:, :, 3:3 + NT].rearrange("p (a b) t -> p a b t", a=2),
                     acc[:, s, :, HP:HALF].rearrange("p a (b t) -> p a b t", t=NT)).then_inc(acc_free[s], 1)

            def conv_tanh_(hp, j):
                act.wait_ge(conv_done, 3 * hp + (j + 1))
                act.activation(conv_t, conv_y, ACT.Tanh).then_inc(conv_tanh, 1)

            def z_gate(hp):
                tile_done(2 * hp + 2, 0)
                act.wait_ge(conv_silu, 3 * hp + 3)
                act.activation(halves(conv_t), acc_of(0), ACT.Tanh, scale=0.5).then_inc(z_tanh, 1)

            def head_unit(hp, it=None, kb=0, convs=True):
                for ti in range(4):
                    for e in range(8):
                        next_split(2 * hp + (1 + ti) // 2, (1 + ti) % 2, e)
                        if it is not None:
                            for name in ACT_PLAN.get(8 * ti + e, ()):
                                head_act(it, kb, name)
                        if e == 1 and ti == 0 and it is not None:
                            z_gate(hp - 1)
                        if convs and ti and e == 1:
                            evacuate_qkv(hp, ti - 1)
                        if convs and ti and e == 6:
                            conv_tanh_(hp, ti - 1)
                        if not convs and ti and e == 1:
                            evacuate_kv(ti - 1)

            def evacuate_kv(j):
                tile_done((N_KV + j) // 2, (N_KV + j) % 2)
                if j == 0:
                    act.wait_ge(conv_silu, 3 * H)
                    act.wait_ge(acc_free[0], 2 * H + 1)
                    act.wait_ge(last_taken, 3 * H)
                    act.wait_ge(pe_h.sem, pe_h.at("o_chan", H - 2))
                copy(halves(kv[:, j, :]), acc_of((N_KV + j) % 2)).then_inc(acc_free[(N_KV + j) % 2], 1)

            for ti in range(4):
                for e in range(8):
                    next_split((1 + ti) // 2, (1 + ti) % 2, e)
                    if ti == 0 and e == 1:
                        tile_done(0, 0)
                        copy(halves(ab_t[0:16, 0:SEQ]), acc[0:16, 0, :, 0:HP])
                        copy(halves(ab_t[0:16, SEQ:TOK]), acc[0:16, 0, :, HP:HALF]).then_inc(acc_free[0], 1)
                        act.wait_ge(prep, 1)
                        act.activation(sp_e, xm, ACT.Exp).then_inc(act_t.sem, 1)
                        act.activation(tb, ab_tok[:, :, 8:16], ACT.Tanh, scale=0.5)
                        act.activation(ea, par[:, P_ALOG:P_ALOG + 8], ACT.Exp)
                        act.wait_ge(act_t.sem, 1)
                        act.activation(sp_e, sp_e, ACT.Ln, bias=1.0).then_inc(prep_act, 1)
                        act.wait_ge(prep, 3)
                        act.activation(egl_s, egl_s, ACT.Exp)
                        act.activation(gates[:, :, KEG, :], gates[:, :, KEG, :], ACT.Exp)
                        act.activation(gates[:, :, KEK:KEL + 1, :], gates[:, :, KEK:KEL + 1, :], ACT.Exp) \
                           .then_inc(prep_act, 1)
                    if ti and e == 1:
                        evacuate_qkv(0, ti - 1)
                    if ti and e == 6:
                        conv_tanh_(0, ti - 1)
            with act.Fori(0, 3) as i:
                head_unit(2 * i + 1, 2 * i, 0)
                head_unit(2 * i + 2, 2 * i + 1, 1)
            head_unit(7, 6, 0)
            head_unit(8, 7, 1, convs=False)

            def query(j):
                tile_done((N_Q + j) // 2, (N_Q + j) % 2)
                if j == 0:
                    act.wait_ge(dve_h.sem, dve_h.at("y", H - 1))
                copy(full[:, j, :].rearrange("p (a c) -> p a c", a=2), acc_of((N_Q + j) % 2)) \
                    .then_inc(acc_free[(N_Q + j) % 2], 1)

            def samp_act_step(name):
                if name == "sq":
                    act.wait_ge(samp_dve, SD["kg"])
                    ins = act.activation(sq_s, samp[:, :, 0:2, :].rearrange("p h s t -> p h (s t)"), ACT.Square)
                elif name == "decay":
                    act.wait_ge(samp_dve, SD["dmask2"])
                    ins = act.activation(dec_s, dec_s, ACT.Exp)
                elif name in ("A1", "A2"):
                    act.wait_ge(samp_pe, SPE[f"a{name[1]}"])
                    act.wait_ge(state_out, 16 * H)
                    ins = copy(a1_s, gp[0:NS, 3, :].rearrange("p (h t) -> p h t", h=H))
                elif name[0:2] == "ks":
                    h = int(name[2:])
                    act.wait_ge(samp_pe, SPE[f"st{h}"])
                    ins = copy(ksqs, gp[:, 2, 0:P].rearrange("p (s t) -> p s t", s=2))
                elif name[0] == "q":
                    h = int(name[1:])
                    act.wait_ge(samp_pe, SPE[f"tr{h}"])
                    if h:
                        act.wait_ge(samp_dve, SD[f"o{h - 1}"])
                    ins = copy(qss, gp[0:NS, 1, 0:P], gates[0:NS, h, KEG, 4:5])
                elif name == "osq":
                    act.wait_ge(samp_dve, SD[f"o{H - 1}"])
                    act.wait_ge(samp_pe, SPE[f"ns{H - 1}"])
                    for h in range(H):
                        ins = act.activation(vpx[:, h, :], o_s[:, h, :], ACT.Square,
                                             accum_out=sos[:, h:h + 1])
                ins.then_inc(samp_act, 1)

            for t in range(4):
                n = N_Q + t
                for e in range(8):
                    next_split(n // 2, n % 2, e)
                    if e == 1:
                        if t == 0:
                            act.wait_ge(w_used, 2 * N_Q)
                            copy(halves(kv[:, 3, :]), acc_of(0)).then_inc(acc_free[0], 1)
                        else:
                            query(t - 1)
                    for name in SAMP_ACT.get(8 * t + e, ()):
                        samp_act_step(name)

            def att_exp(u):
                c = (u // 2) % 4
                lo = 0 if c else P
                act.wait_ge(biased, u + 1)
                pr = prob[u % 2]
                for g in range(4):
                    act.activation(pr[:, g, lo:], pr[:, g, lo:], ACT.Exp, bias=nmax[u % 2][:, g:g + 1],
                                   accum_out=esum[u % 2][:, g:g + 1])
                act.activation(esink[u % 2], dsink[u % 2], ACT.Exp).then_inc(exped, 1)

            def att_turn_out(u):
                act.wait_ge(turned, u + 1)
                if u:
                    act.wait_ge(weighed, u)
                for w in range(0 if (u // 2) % 4 else 1, 2):
                    ins = copy(probT[:, w, :, :], bank4(2 + w))
                ins.then_inc(turned_out, 1)

            act.wait_ge(ys_done, 1)
            for i in range(2):
                act.wait_ge(sdn_stored[i], 16 * (H // 2))
            act.wait_ge(vtok_pe, 1)
            copy(v_tok.rearrange("p c r d -> p r c d"), bank4(0, 2).rearrange("p (r c) d -> p r c d", r=2)) \
                .then_inc(vtok_done, 1)
            for t in range(4, 16):
                n = N_Q + t
                for e in range(8):
                    next_split(n // 2, n % 2, e)
                    if e == 1 and t <= 8:
                        query(t - 1)
                    if e == 1 and t > 8:
                        tile_done((n - 1) // 2, (n - 1) % 2)
                        if t > 9:
                            act.wait_ge(acc_free[n % 2], (n - 2) // 2 + 1)
                        act.activation(halves(za_t), acc_of((n - 1) % 2), ACT.Tanh, scale=0.5).then_inc(z_tanh, 1)
                    if t < 12:
                        u = 2 * (t - 4) + e // 4
                        if e % 4 == 2 and u:
                            att_turn_out(u - 1)
                        if e % 4 == 2:
                            att_exp(u)
                    else:
                        for name in SATT_ACT.get(8 * (t - 12) + e, ()):
                            if name == "last":
                                att_turn_out(15)
                            elif name == "exp":
                                act.wait_ge(sa_dve, SAD["sub"])
                                for b in range(NB):
                                    act.activation(prob_s[:, b, :], prob_s[:, b, :], ACT.Exp,
                                                   bias=nmax_s[:, b:b + 1], accum_out=esum_s[:, b:b + 1])
                                act.activation(dsink_s, dsink_s, ACT.Exp).then_inc(sa_act, 1)
                            elif name == "turned":
                                act.wait_ge(sa_pe, SAP["turn"])
                                copy(probT_s, bank4(0, 2)).then_inc(sa_act, 1)
                            elif name[0:5] == "v_new":
                                act.wait_ge(sa_pe, SAP[name])
                                if name == "v_new0":
                                    act.wait_ge(out_small, 16 * n_small)
                                if name == "v_new1":
                                    act.wait_ge(sa_pe, SAP["weigh0"])
                                    act.wait_ge(vnew_stored, 16)
                                copy(v_new[0:NT], gp[0:NT, 0:2, :].rearrange("p k (b d) -> p (k b) d", d=P)) \
                                    .then_inc(sa_act, 1)

            n = N_OUT0 - 1
            tile_done(n // 2, n % 2)
            act.wait_ge(acc_free[1 - n % 2], (n - 1) // 2 + 1)
            act.activation(halves(za_t), acc_of(n % 2), ACT.Tanh, scale=0.5).then_inc(z_tanh, 1)

            def out_section(n0, turn):
                def post(j, jp, first=False):
                    added(j)
                    if not first:
                        act.wait_ge(sq_summed, (0 if turn == 1 else KT) + j - 1)
                    act.activation(sqb[jp], full[:, j, :], ACT.Square).then_inc(sq_done, 1)
                    if turn == 1:
                        act.dma_start(x1_dram[j], full[:, j, :]).then_inc(x1_stored, 16)

                def added(j):
                    if isinstance(j, int):
                        act.wait_ge(acc_free[(n0 + j) % 2], (n0 + j) // 2 + 1)

                if turn == 1:
                    act.wait_ge(gated, 1)
                else:
                    act.wait_ge(y_done, KT)
                act.wait_ge(w_used, 2 * n0)
                act_split(turn)
                split_hi((n0 + 1) // 2, (n0 + 1) % 2, 0)
                split_hi((n0 + 1) // 2, (n0 + 1) % 2, 1)
                for j in (1, 2):
                    n = n0 + j
                    split_hi((n + 1) // 2, (n + 1) % 2, 0)
                    split_hi((n + 1) // 2, (n + 1) % 2, 1)
                    post(j - 1, (j - 1) % 2, first=True)
                with act.Fori(0, KT // 2 - 2) as i:
                    for b in range(2):
                        n = n0 + 3 + b
                        for half in range(2):
                            split_hi(i + (n + 1) // 2, (n + 1) % 2, half)
                        act.wait_ge(acc_free[1 - b], i + ((n0 + 2 + b) // 2 + 1))
                        post(2 * i + 2 + b, b)
                n = n0 + KT - 1
                if n + 1 < N_TILES:
                    split_hi((n + 1) // 2, (n + 1) % 2, 0)
                    split_hi((n + 1) // 2, (n + 1) % 2, 1)
                post(KT - 2, 0)
                post(KT - 1, 1)

            out_section(N_OUT0, 1)
            take_root(1)
            act_split(2)
            split_hi((N_VG + 1) // 2, (N_VG + 1) % 2, 0)
            split_hi((N_VG + 1) // 2, (N_VG + 1) % 2, 1)

            def gate(m, s, j, b, first=False):
                act.wait_ge(w_used, 4 * m + (2 * s + 2))
                if not first:
                    act.wait_ge(acc_free[0], j + N_VG // 2)
                act.activation(halves(tg[b]), acc_of(s), ACT.Tanh, scale=0.5).then_inc(gate_tanh, 1)

            def taps(j, b, part):
                act.wait_ge(acc_free[0], j + (N_VG // 2 + 2))
                for i in (range(0, 8) if part == 0 else range(8, POOL_TAPS)):
                    tap = DVE_TAPS + i
                    act.wait_ge(tap_sum, j * POOL_SUMS + (i if i < 2 else 1 + max(i - 2, 1)))
                    copy(prod[(i + b * POOL_TAPS) % 2], u_p[b][:, tap:tap + SEQ],
                         cfw[:, j, tap:tap + 1]).then_inc(tap_prod, 1)

            n = N_VG
            for half in range(2):
                split_hi((n + 2) // 2, 1, half)
            gate(n // 2, 1, 0, 0, first=True)
            with act.Fori(0, KT // 2 - 1) as i:
                for b in (1, 0):
                    m = 2 * i + (n + 2) // 2 + (1 - b)
                    j = 2 * i + (2 - b)
                    for half in range(2):
                        split_hi(m + 1, 0, half)
                    taps(j - 1, 1 - b, 0)
                    for half in range(2):
                        split_hi(m + 1, 1, half)
                    gate(m, 1, j, b)
                    taps(j - 1, 1 - b, 1)
            m = (n + 2 * (KT - 1)) // 2
            for half in range(2):
                split_hi(m + 1, 0, half)
            taps(KT - 2, 0, 0)
            for half in range(2):
                split_hi(m + 1, 1, half)
            gate(m, 1, KT - 1, 1)
            taps(KT - 2, 0, 1)

            def z_tanh_(j):
                act.wait_ge(w_used, 2 * (N_Z1 + j + 1))
                if j >= ZRING:
                    act.wait_ge(y_done, j - ZRING + 1)
                act.activation(halves(zring[j % ZRING]), acc_of((N_Z1 + j) % 2), ACT.Tanh, scale=0.5) \
                    .then_inc(zz_tanh, 1)

            def affine(k):
                act.wait_ge(ln_scaled, k + 1)
                act.activation(full[:, k, :], full[:, k, :], ACT.Identity, scale=lg[:, k:k + 1],
                               bias=lb[:, k:k + 1]).then_inc(ln_aff, 1)
                act.wait_ge(ln_aff, k + 1)
                if k >= 2:
                    act.wait_ge(y_done, k - 1)
                act.activation(sqb[k % 2], full[:, k, :], ACT.Tanh).then_inc(ln_tanh, 1)

            for t in range(KT + 1):
                n = N_Z1 + t
                if t < KT:
                    split_hi((n + 1) // 2, (n + 1) % 2, 0)
                    split_hi((n + 1) // 2, (n + 1) % 2, 1)
                if t == 0:
                    taps(KT - 1, 1, 0)
                    taps(KT - 1, 1, 1)
                if t:
                    z_tanh_(t - 1)
                for k in LN_SQ.get(t, ()):
                    act.wait_ge(centred, k + 1)
                    if k >= 2:
                        act.wait_ge(c_summed, KT + k - 1)
                    act.activation(sqb[k % 2], full[:, k, :], ACT.Square).then_inc(ln_sq, 1)
                if t == 6:
                    act.wait_ge(var_ready, 3)
                    act.activation(ssq, ssq, ACT.Sqrt).then_inc(root, 1)
                for k in LN_Y.get(t, ()):
                    affine(k)
            out_section(N_OUT1, 3)
            take_root(3)
            for k in range(KT):
                act.wait_ge(scaled, 2 * KT + k + 1)
                act.dma_start(y[k], full[:, k, :]).then_inc(fin_stored, 16)
            act.wait_ge(fin_stored, 16 * KT)

        @block.vector
        def _(dve):
            def order(ins):
                dve_t.inc(ins)

            def fence():
                dve.wait_ge(dve_t.sem, dve_t.now())

            def tt(out, a, b, op):
                return dve.tensor_tensor(out, a, b, op)

            def stt(out, a, scalar, b, op0, op1):
                return dve.scalar_tensor_tensor(out=out, in0=a, scalar=scalar, in1=b, op0=op0, op1=op1)

            def ts(out, a, s0_, s1_=None, op0=ALU.mult, op1=None):
                if s1_ is None:
                    return dve.tensor_scalar(out, a, s0_, None, op0)
                return dve.tensor_scalar(out, a, s0_, s1_, op0, op1)

            ADD, SUB, MUL = ALU.add, ALU.subtract, ALU.mult

            def split_lo(m, s, half):
                dve.wait_ge(whi_done, 4 * m + (2 * s + half + 1))
                hs_ = slice(half * 1024, (half + 1) * 1024)
                tt(w_lo[:, s, hs_], w_raw[:, half, :], w_hi[:, s, hs_].bitcast(F32), SUB).then_inc(wlo_done, 1)

            def next_split(m, s, e):
                if e in (0, 4):
                    split_lo(m + s, 1 - s, e // 4)

            def act_lo_even(turn, k):
                dve.wait_ge(ahi_done, KT * turn + k + 1)
                tt(act_lo[:, k, :], full[:, k, :], act_hi[:, k, :].bitcast(F32), SUB).then_inc(alo_even, 1)

            def take_mean_square(turn, sums):
                if sums:
                    dve.wait_ge(norm_sum, sums)
                else:
                    dve.wait_ge(sq_used, KT)
                ts(halves(ssq), gp[:, 0:2, 0:HALF], 1.0 / D, EPS, MUL, ADD).then_inc(var_ready, 1)

            def take_reciprocal(turn):
                dve.wait_ge(root, turn + 1)
                order(dve.reciprocal(rstd, ssq))
                fence()

            def scale_and_split(turn, gain, sems_before=()):
                for s_, v_ in sems_before:
                    dve.wait_ge(s_, v_)
                for k in range(KT):
                    stt(full[:, k, :], full[:, k, :], par[:, gain + k:gain + k + 1], rstd, MUL, MUL) \
                        .then_inc(scaled, 1)
                    if k >= 2 and k % 2 == 0:
                        act_lo_even(turn, k - 2)
                act_lo_even(turn, KT - 2)

            dve.wait_ge(par_in, 16)
            ts(par[:, P_DNW:P_DNW + 96], par[:, P_DNW:P_DNW + 96], 0.5)
            ts(dng, par[:, P_DNG:P_DNG + 1], 0.5 * P ** 0.5)
            ts(lg, par[:, P_LNG:P_LNG + KT], 0.5)
            ts(lb, par[:, P_LNB:P_LNB + KT], 0.5).then_inc(halved, 1)
            take_mean_square(0, 0)
            split_lo(0, 0, 0)
            split_lo(0, 0, 1)
            take_reciprocal(0)
            scale_and_split(0, P_G0)
            split_lo(0, 1, 0)
            split_lo(0, 1, 1)

            def gate_scalars():
                order(dve.memset(gates, 0.0))
                order(dve.memset(ab_tok, 0.0))
                fence()
                dve.wait_ge(prep_pe, 1)
                dve.tensor_copy(ab_tok[:, 0:4, :], gp[:, 0, 0:64].rearrange("p (c k) -> p c k", k=16))
                order(dve.tensor_copy(ab_tok[0:NS, 4, :], gp[0:NS, 0, 64:80]))
                fence()
                order(tt(xa, ab_tok[:, :, 0:8], per_group(par[:, P_DTB:P_DTB + 8], 5), ADD))
                fence()
                stt(xm, xa, -1.0, xa, MUL, ALU.min).then_inc(prep, 1)
                dve.wait_ge(prep_act, 1)
                chan = lambda k: gates[:, :, k, :].rearrange("p h c -> p c h")
                order(stt(xa, xa, 0.0, sp_e, ALU.max, ADD))
                fence()
                stt(chan(KG), xa, -1.0, per_group(ea, 5), MUL, MUL)
                order(ts(chan(KBETA), tb, 0.5, 0.5, MUL, ADD))
                fence()
                tt(gmask, gates[0:NS, :, KG, 4].unsqueeze(2).to_broadcast([NS, H, NB]),
                   per_group(cst[0:NS, C_SEQ:C_SEQ + NB], H), MUL).then_inc(prep, 1)
                dve.wait_ge(prep_pe, 2)
                gch = lambda lo: gp[:, 1, lo:lo + 32].rearrange("p (h c) -> p h c", h=H)
                for rows, c, gc, tot in ((slice(0, P), slice(0, 4), gch(0), gch(32)),
                                         (slice(0, NS), slice(4, 5), gp[0:NS, 1, 64:72].unsqueeze(2),
                                          gp[0:NS, 1, 72:80].unsqueeze(2))):
                    ts(gates[rows, :, KNG, c], gc, -1.0)
                    dve.tensor_copy(gates[rows, :, KEG, c], gc)
                    order(dve.tensor_copy(gates[rows, :, KEL, c], tot))
                    fence()
                    order(tt(gates[rows, :, KEK, c], tot, gates[rows, :, KNG, c], ADD))
                dve.tensor_copy(egl_s, gp[:, 1, 80:144].rearrange("p (h b) -> p h b", h=H)).then_inc(prep, 1)
                dve.wait_ge(prep_act, 2)
                ts(gates[:, :, KNEG, :], gates[:, :, KEG, :], -1.0).then_inc(prep, 1)

            def conv(hp, kb, j):
                m, s = 2 * hp + (1 + j) // 2, (1 + j) % 2
                dve.wait_ge(acc_free[s], m + 1)
                dve.wait_ge(prev_put, 3 * hp + (j + 1))
                if not (isinstance(hp, int) and hp == 0 and j == 0):
                    dve.wait_ge(conv_silu, 3 * hp + j)
                dst_s = conv_y[:, SEQ:SEQ + NS].rearrange("p (b t) -> p b t", b=NB)
                for tap in range(4):
                    w = cw[kb][:, 4 * j + tap:4 * j + tap + 1]
                    a_, b_ = cin_p[:, tap:tap + SEQ], cin_s[:, :, tap:tap + NT]
                    if tap == 0:
                        order(ts(conv_y[:, 0:SEQ], a_, w))
                        order(ts(dst_s, b_, w))
                    else:
                        dve.wait_ge(dve_t.sem, dve_t.now() - 1)
                        order(stt(conv_y[:, 0:SEQ], a_, w, conv_y[:, 0:SEQ], MUL, ADD))
                        dve.wait_ge(dve_t.sem, dve_t.now() - 1)
                        ins = stt(dst_s, b_, w, dst_s, MUL, ADD)
                        if tap == 3:
                            ins.then_inc(conv_done, 1)
                        else:
                            order(ins)

            def silu(hp, kb, j):
                dve.wait_ge(conv_tanh, 3 * hp + (j + 1))
                stt(kqv[kb][:, j, :], conv_t[:, 0:SEQ], 1.0, conv_y[:, 0:SEQ], ADD, MUL)
                stt(samp[:, hp, j, :], conv_t[:, SEQ:SEQ + NS], 1.0, conv_y[:, SEQ:SEQ + NS], ADD, MUL) \
                    .then_inc(conv_silu, 1)

            def z_product(hp):
                dve.wait_ge(z_tanh, hp + 1)
                stt(halves(full[:, 8 + hp, :]), halves(conv_t), 1.0, acc_of(0), ADD, MUL).then_inc(acc_free[0], 1)

            def head_dve(it, kb, name):
                pe_at = lambda n: dve.wait_ge(pe_h.sem, pe_h.at(n, it))
                col = lambda row, c: hs[:, row, c:c + 1]
                if name == "kg":
                    pe_at("kv_tok")
                    dve.wait_ge(pool_h.sem, pool_h.at("scalars", it))
                    ins = tt(kg, bank4(0), per_row(hs[:, KEK, 0:4], P), MUL)
                elif name == "dmask":
                    pe_at("gcum")
                    ins = tt(dec, bank4(2), per_group(negm, 4), ADD)
                elif name == "ssum":
                    pe_at("norm")
                    ins = ts(ssum, gp[:, 3, 0:8], EPS, None, ADD)
                elif name == "vs":
                    dve.wait_ge(pool_h.sem, pool_h.at("rn", it))
                    ins = tt(vs, bank4(1), per_row(rn[:, 0:4], P), MUL)
                elif name == "Mt":
                    pe_at("gram")
                    dve.wait_ge(act_h.sem, act_h.at("decay", it))
                    dve.wait_ge(pool_h.sem, pool_h.at("bp", it))
                    for c in range(NC):
                        ins = stt(mt[:, c, :], gp[:, 2 + c // 2, (c % 2) * 256:(c % 2) * 256 + P], bp[:, c:c + 1],
                                  dec[:, c, :], MUL, MUL)
                elif name == "attn":
                    qk = gp[:, 2:4, :].rearrange("p b (c s t) -> p (b c) s t", s=2, t=P)[:, :, 1, :]
                    ins = tt(attn, qk, dec, MUL)
                elif name == "X":
                    pe_at("m0")
                    ins = tt(xx[:, 0], per_group(ident, 4), bank4(0), SUB)
                elif name == "Xt":
                    ins = tt(xx[:, 1], per_group(ident, 4), mtl[0], SUB)
                elif name[0] == "X":
                    l = int(name[1])
                    pe_at(f"x{l}")
                    if l < LEVELS - 1:
                        xf = xx.rearrange("p s c t -> p s (c t)")
                        ins = tt(xf, xf, gp[:, 2:4, :], SUB)
                    else:
                        ins = tt(xx[:, 1], xx[:, 1], bank4(3), SUB)
                elif name[0:2] == "vp":
                    c = int(name[2])
                    pe_at(f"u{c}")
                    ins = ts(vp, gp[:, 2, 0:P], bp[:, c:c + 1])
                elif name[0] == "S":
                    c = int(name[1])
                    pe_at(f"so{c}")
                    if c == 0:
                        if not (isinstance(it, int) and it == 0):
                            dve.wait_ge(state_out, 16 * it)
                        ins = dve.tensor_copy(st, gp[:, 3, 0:P])
                    else:
                        ins = stt(st, st, col(KEL, c), gp[:, 3, 0:P], MUL, ADD)
                elif name[0] == "o" and name != "on":
                    c = int(name[1])
                    if c == 0:
                        ins = dve.tensor_copy(o_tok[:, 0, :], gp[:, 0, 0:P])
                    else:
                        dve.wait_ge(act_h.sem, act_h.at(f"q{c}", it))
                        ins = tt(o_tok[:, c, :], gp[:, 0, 0:P], qs, ADD)
                elif name[0] == "r":
                    c = int(name[1])
                    pe_at(f"s{c}")
                    ins = stt(rr, gp[:, 0, 0:P], col(KNEG, c), vs[:, c, :], MUL, ADD)
                elif name == "on":
                    dve.wait_ge(pool_h.sem, pool_h.at("f5", it))
                    ins = tt(on, o_tok, per_row(f_a, P), MUL)
                else:
                    pe_at("o_chan")
                    dve.wait_ge(acc_free[0], 2 * it + 3)
                    dst = halves(full[:, 8 + it, :])[:, :, 0:HP]
                    ins = stt(dst, gp[:, 0, :].rearrange("p (a t) -> p a t", a=2), dng, dst, MUL, MUL)
                ins.then_inc(dve_h.sem, 1)

            def head_unit(hp, it=None, kb=0, convs=True):
                for ti in range(4):
                    for e in range(8):
                        next_split(2 * hp + (1 + ti) // 2, (1 + ti) % 2, e)
                        if it is not None:
                            for name in DVE_PLAN.get(8 * ti + e, ()):
                                head_dve(it, kb, name)
                            if ti == 0 and e == 2:
                                z_product(it)
                        elif ti == 0 and e == 1:
                            gate_scalars()
                        if convs and ti and e == 3:
                            conv(hp, 1 - kb, ti - 1)
                        if convs and ti and e == 7:
                            silu(hp, 1 - kb, ti - 1)

            head_unit(0, kb=1)
            with dve.Fori(0, 3) as i:
                dve_t.enter(i, 2 * 3 * 7)
                head_unit(2 * i + 1, 2 * i, 0)
                head_unit(2 * i + 2, 2 * i + 1, 1)
                dve_t.leave(3)
            head_unit(7, 6, 0)
            head_unit(8, 7, 1, convs=False)

            def samp_dve_step(name):
                pe_at = lambda n: dve.wait_ge(samp_pe, SPE[n])
                own = lambda n: dve.wait_ge(samp_dve, SD[n])
                gcol = lambda row, h: gates[0:NS, h, row, 4:5]
                b64 = lambda ap: ap.rearrange("p (h t) -> p h t", t=NS)
                ids = per_group(ident[0:NS, 0:NS], H)
                wide = lambda s_: gp[0:NS, 0:2, :].rearrange("p b (h s t) -> p (b h) s t", s=2, t=NS)[:, :, s_, :]
                if name == "kg":
                    pe_at("k_tok")
                    ins = tt(kg_s, gp[0:NS, 0:2, :].rearrange("p b (h d) -> p (b h) d", d=P),
                             per_row(gates[0:NS, :, KEK, 4], P), MUL)
                elif name == "ssum":
                    pe_at("norm")
                    ins = ts(ssum_s, gp[0:NS, 0, 0:16], EPS, None, ADD)
                elif name == "vs":
                    pe_at("v_tok")
                    dve.wait_ge(samp_pool, SP_["rn"])
                    ins = tt(vs_s, gp[0:NS, 2:4, :].rearrange("p b (h d) -> p (b h) d", d=P),
                             per_row(rn_s.rearrange("p (h s) -> p h s", s=2)[:, :, 0], P), MUL)
                elif name == "dmask":
                    pe_at("gcum")
                    ins = tt(dec_s, b64(gp[0:NS, 2, :]), per_group(cst[0:NS, C_NEGS:C_NEGS + NS], H), ADD)
                elif name == "dmask2":
                    own("dmask")
                    ins = tt(dec_s, dec_s, per_row(gates[0:NS, :, KNG, 4], NS), ADD)
                elif name == "Mt":
                    pe_at("gram")
                    dve.wait_ge(samp_act, SA["decay"])
                    ins = tt(mt_s, wide(0), dec_s, MUL)
                elif name == "Mtb":
                    own("Mt")
                    dve.wait_ge(samp_pool, SP_["bp"])
                    ins = tt(mt_s, mt_s, per_row(bp_s, NS), MUL)
                elif name == "attn":
                    ins = tt(attn_s, wide(1), dec_s, MUL)
                elif name == "X":
                    pe_at("m0")
                    ins = tt(x_s, ids, b64(gp[0:NS, 2, :]), SUB)
                elif name == "Xt":
                    ins = tt(xt_s, ids, mtl_s[0], SUB)
                elif name == "X1":
                    pe_at("x1")
                    ins = tt(x_s, x_s, b64(gp[0:NS, 2, :]), SUB)
                elif name in ("Xt1", "Xt2"):
                    pe_at(f"x{name[2]}")
                    ins = tt(xt_s, xt_s, b64(gp[0:NS, 0, :]), SUB)
                elif name == "on":
                    own(f"o{H - 1}")
                    dve.wait_ge(samp_pool, SP_["f5"])
                    ins = tt(o_s, o_s, per_row(fa_s, P), MUL)
                elif name[0] == "r":
                    h = int(name[1:])
                    pe_at(f"tr{h}")
                    ins = stt(rs_, gp[0:NS, 3, 0:P], gcol(KNEG, h), vs_s[:, h, :], MUL, ADD)
                elif name[0:2] == "vp":
                    h = int(name[2:])
                    pe_at(f"u{h}")
                    if h:
                        dve.wait_ge(samp_pool, SP_[f"vx{h - 1}"])
                    ins = ts(vps, gp[0:NS, 2, 0:P], bp_s[:, h:h + 1])
                elif name[0] == "o":
                    h = int(name[1:])
                    pe_at(f"o{h}")
                    dve.wait_ge(samp_act, SA[f"q{h}"])
                    ins = tt(o_s[:, h, :], gp[0:NS, 3, 0:P], qss, ADD)
                else:
                    h = int(name[1:])
                    pe_at(f"ns{h}")
                    for b in range(NB):
                        ins = stt(s0[h % 2][:, b, :], s0[h % 2][:, b, :], egl_s[:, h, b:b + 1],
                                  gp[:, b // 4, (b % 4) * P:(b % 4 + 1) * P], MUL, ADD)
                ins.then_inc(samp_dve, 1)

            for t in range(4):
                n = N_Q + t
                for e in range(8):
                    next_split(n // 2, n % 2, e)
                    for name in SAMP_DVE.get(8 * t + e, ()):
                        samp_dve_step(name)
            dve.wait_ge(samp_pe, SPE["o_chan"])
            for a_ in range(2):
                dst = full[:, 8:16, a_ * HALF + HP:(a_ + 1) * HALF]
                ins = stt(dst, gp[:, 2, :].rearrange("p (h a c) -> p h a c", h=H, a=2)[:, :, a_, :], dng, dst, MUL, MUL)
            ins.then_inc(ys_done, 1)

            def att_bias(u):
                r, c, jj = u // 8, (u // 2) % 4, u % 2
                lo = 0 if c else P
                pr, sink = prob[u % 2][:, :, lo:], par[:, P_SINK + 8 * r + 4 * jj:P_SINK + 8 * r + 4 * jj + 4]
                dve.wait_ge(scores, u + 1)
                if u >= 2:
                    dve.wait_ge(turned, u - 1)
                if u == 1:
                    dve.wait_ge(dnc_stored, 16)
                s_ = gp[:, 0:2, :].rearrange("p q (j w) -> p (q j) w", j=2)[:, :, lo:]
                order(stt(pr, s_, 0.125, per_group(caus[:, lo:], 4), MUL, ADD))
                fence()
                order(dve.tensor_reduce(amax, pr, AX_X, ALU.max))
                fence()
                order(tt(amax, amax, sink, ALU.max))
                fence()
                ts(nmax[u % 2], amax, -1.0)
                tt(dsink[u % 2], sink, amax, SUB).then_inc(biased, 1)

            def att_probs(u):
                lo = 0 if (u // 2) % 4 else P
                pr = prob[u % 2][:, :, lo:]
                dve.wait_ge(exped, u + 1)
                order(tt(esum[u % 2], esum[u % 2], esink[u % 2], ADD))
                fence()
                order(dve.reciprocal(esum[u % 2], esum[u % 2]))
                fence()
                tt(pr, pr, per_row(esum[u % 2], 2 * P - lo), MUL).then_inc(probs, 1)

            def att_out(u):
                r, c, jj = u // 8, (u // 2) % 4, u % 2
                dve.wait_ge(weighed, u + 1)
                dve.tensor_copy(full[:, 4 * r + 2 * jj:4 * r + 2 * jj + 2, blk(c):blk(c) + P],
                                gp[:, 2, 0:256].rearrange("p (j t) -> p j t", j=2)).then_inc(attn_out, 1)

            def za_product(i):
                n = N_ZA + i
                dve.wait_ge(z_tanh, H + i + 1)
                order(stt(halves(za_t), halves(za_t), 1.0, acc_of(n % 2), ADD, MUL))
                dve.wait_ge(attn_out, 8 * (i // 4 + 1))
                fence()
                dst = halves(full[:, i, :])[:, :, 0:HP]
                stt(dst, halves(za_t)[:, :, 0:HP], 0.5, dst, MUL, MUL)
                dve.tensor_copy(zs_samp[:, i], halves(za_t)[:, :, HP:HALF]).then_inc(acc_free[n % 2], 1)

            def samp_att(name):
                if name == "bias":
                    dve.wait_ge(sa_pe, SAP["scores"])
                    for i_, nb in enumerate((3, 3, 2)):
                        stt(prob_s[:, 3 * i_:3 * i_ + nb, :],
                            gp[:, i_, 0:136 * nb].rearrange("p (b t) -> p b t", b=nb), 0.125,
                            per_group(cst[:, C_WIN:C_WIN + W + NT], nb), MUL, ADD).then_inc(sa_dve, 1)
                    own("bias2")
                    dve.tensor_reduce(amax_s, prob_s, AX_X, ALU.max).then_inc(sa_dve, 1)
                    own("max")
                    sink = par[:, P_SINKS:P_SINKS + 1]
                    ts(amax_s, amax_s, sink, None, ALU.max).then_inc(sa_dve, 1)
                    own("max2")
                    ts(nmax_s, amax_s, -1.0).then_inc(sa_dve, 1)
                    own("neg")
                    ts(dsink_s, nmax_s, sink, None, ADD).then_inc(sa_dve, 1)
                elif name == "prob":
                    dve.wait_ge(sa_act, SAA["exp"])
                    tt(esum_s, esum_s, dsink_s, ADD).then_inc(sa_dve, 1)
                    own("den")
                    dve.reciprocal(esum_s, esum_s).then_inc(sa_dve, 1)
                    own("inv")
                    tt(prob_s, prob_s, per_row(esum_s, W + NT), MUL).then_inc(sa_dve, 1)
                elif name == "turned_new":
                    dve.wait_ge(sa_pe, SAP["turn_new"])
                    dve.tensor_copy(probT_n[0:NT], bank4(2, 2)[0:NT]).then_inc(sa_dve, 1)
                else:
                    r = int(name[3])
                    dve.wait_ge(sa_pe, SAP[f"weigh{r}"])
                    for a_ in range(2):
                        ins = dve.tensor_copy(full[:, 4 * r:4 * r + 4, a_ * HALF + HP:(a_ + 1) * HALF],
                                              gp[:, 2, 0:256].rearrange("p (j a c) -> p j a c", j=4, a=2)[:, :, a_, :])
                    ins.then_inc(sa_dve, 1)

            own = lambda n_: dve.wait_ge(sa_dve, SAD[n_])
            for t in range(4, 16):
                n = N_Q + t
                for e in range(8):
                    next_split(n // 2, n % 2, e)
                    if t < 12:
                        u = 2 * (t - 4) + e // 4
                        if e % 4 == 1:
                            att_bias(u)
                        if e % 4 == 3:
                            att_probs(u)
                            if u:
                                att_out(u - 1)
                    elif 8 * (t - 12) + e in SATT_DVE:
                        name = SATT_DVE[8 * (t - 12) + e]
                        if name == "last":
                            att_out(15)
                        else:
                            samp_att(name)
                    if e == 5 and t > 8:
                        za_product(t - 9)
            za_product(7)
            own("out1")
            for n in (N_OUT0 - 2, N_OUT0 - 1):
                dve.wait_ge(acc_free[n % 2], n // 2 + 1)
            dve.wait_ge(out_small, 16 * n_small)
            dve.wait_ge(vnew_stored, 32)
            for a_ in range(2):
                dst = full[:, 0:8, a_ * HALF + HP:(a_ + 1) * HALF]
                stt(dst, zs_samp[:, :, a_, :], 0.5, dst, MUL, MUL).then_inc((res_free, gated)[a_], 1)

            def out_section(n0, turn):
                def add_residual(m, s, j, jp, rnd):
                    dve.wait_ge(w_used, 4 * m + (2 * s + 2))
                    dve.wait_ge(res_in[jp], 16 * rnd + (16 if turn == 1 else 16 + 8 * KT))
                    tt(halves(full[:, j, :]), acc_of(s), halves(res[jp]), ADD).then_inc(acc_free[s], 1)

                if turn == 3:
                    dve.wait_ge(y_done, KT)
                for k in range(0, KT, 2):
                    act_lo_even(turn, k)
                for half in range(2):
                    split_lo((n0 + 1) // 2, (n0 + 1) % 2, half)
                dve.wait_ge(ahi_done, KT * (turn + 1))
                dve.wait_ge(alo_odd, 8 * (turn + 1))
                for j in (1, 2):
                    n = n0 + j
                    add_residual((n - 1) // 2, (n - 1) % 2, j - 1, (j - 1) % 2, (j - 1) // 2)
                    for half in range(2):
                        split_lo((n + 1) // 2, (n + 1) % 2, half)
                with dve.Fori(0, KT // 2 - 2) as i:
                    for b in range(2):
                        n = n0 + 3 + b
                        add_residual(i + (n - 1) // 2, (n - 1) % 2, 2 * i + 2 + b, b, i + 1)
                        for half in range(2):
                            split_lo(i + (n + 1) // 2, (n + 1) % 2, half)
                n = n0 + KT - 1
                add_residual((n - 1) // 2, (n - 1) % 2, KT - 2, 0, KT // 2 - 1)
                if n + 1 < N_TILES:
                    split_lo((n + 1) // 2, (n + 1) % 2, 0)
                    split_lo((n + 1) // 2, (n + 1) % 2, 1)
                add_residual(n // 2, n % 2, KT - 1, 1, KT // 2 - 1)

            out_section(N_OUT0, 1)
            take_mean_square(1, 1)
            take_reciprocal(1)
            scale_and_split(2, P_G1, [(x1_stored, 16 * KT)])
            split_lo((N_VG + 1) // 2, (N_VG + 1) % 2, 0)
            split_lo((N_VG + 1) // 2, (N_VG + 1) % 2, 1)

            c_s = c_buf[:, SEQ:SEQ + NS].rearrange("p (b t) -> p b t", b=NB)

            def sigmoid(j, b):
                dve.wait_ge(gate_tanh, j + 1)
                ts(tg[b], tg[b], 0.5, 0.5, MUL, ADD).then_inc(acc_free[1], 1)

            def glu(j, b, rnd):
                dve.wait_ge(w_used, 4 * j + (4 * (N_VG // 2 + 1) + 2))
                dve.wait_ge(acc_free[1], j + (N_VG // 2 + 1))
                dve.wait_ge(u_free[b], rnd + 1)
                tt(halves(u_p[b][:, CP:CP + SEQ]), acc[:, 0, :, 0:HP], halves(tg[b])[:, :, 0:HP], MUL)
                tt(u_s[b][:, :, CP:CP + NT].rearrange("p (a b) t -> p a b t", a=2),
                   acc[:, 0, :, HP:HALF].rearrange("p a (b t) -> p a b t", t=NT),
                   halves(tg[b])[:, :, HP:HALF].rearrange("p a (b t) -> p a b t", t=NT), MUL).then_inc(acc_free[0], 1)

            def conv_taps(j, b, rnd, taps):
                for k in taps:
                    wk = cfw[:, j, k:k + 1]
                    if k == 0:
                        dve.wait_ge(acc_free[0], j + (N_VG // 2 + 2))
                        dve.wait_ge(uprev_in[b], 16 * rnd + 16)
                        order(ts(c_s, u_s[b][:, :, k:k + NT], wk))
                    else:
                        dve.wait_ge(dve_t.sem, dve_t.now() - k % 2)
                        order(stt(c_s, u_s[b][:, :, k:k + NT], wk, c_s, MUL, ADD))
                    if k % 2 == 0:
                        q = k // 2
                        wq = cfw[:, j, q:q + 1]
                        if q == 0:
                            order(ts(c_buf[:, 0:SEQ], u_p[b][:, q:q + SEQ], wq))
                        else:
                            dve.wait_ge(dve_t.sem, dve_t.now() - 2)
                            order(stt(c_buf[:, 0:SEQ], u_p[b][:, q:q + SEQ], wq, c_buf[:, 0:SEQ], MUL, ADD))

            def combine(j, b):
                dve.wait_ge(tap_sum, POOL_SUMS * j + (1 + POOL_SUMS))
                dve.wait_ge(cf_stored, 32 * j + 32)
                fence()
                stt(halves(full[:, j, :])[:, :, 0:HP], halves(c_buf[:, 0:SEQ]), cfb[:, j, :], halves(pacc), ADD, ADD) \
                    .then_inc(u_free[b], 1)
                ts(halves(full[:, j, :])[:, :, HP:HALF], halves(c_buf[:, SEQ:SEQ + NS]), cfb[:, j, :], None, ADD) \
                    .then_inc(c_done, 1)

            n = N_VG
            for half in range(2):
                split_lo((n + 2) // 2, 1, half)
            sigmoid(0, 0)

            def conformer_pair(j, b, rnd):
                m = j + N_VG // 2
                glu(j - 1, 1 - b, rnd)
                for half in range(2):
                    split_lo(m + 1, 0, half)
                conv_taps(j - 1, 1 - b, rnd, range(0, 14))
                for half in range(2):
                    split_lo(m + 1, 1, half)
                sigmoid(j, b)
                conv_taps(j - 1, 1 - b, rnd, range(14, CF))
                if isinstance(j, int):
                    dve.wait_ge(ahi_done, 3 * KT)
                    dve.wait_ge(alo_odd, 24)
                combine(j - 1, 1 - b)

            conformer_pair(1, 1, 0)
            with dve.Fori(0, KT // 2 - 1) as i:
                dve_t.enter(i, 2 * (DVE_TAPS + CF))
                conformer_pair(2 * i + 2, 0, i)
                conformer_pair(2 * i + 3, 1, i + 1)
                dve_t.leave(KT // 2 - 1)
            glu(KT - 1, 1, KT // 2 - 1)
            for half in range(2):
                split_lo((N_Z1 + 1) // 2, (N_Z1 + 1) % 2, half)
            conv_taps(KT - 1, 1, KT // 2 - 1, range(CF))
            combine(KT - 1, 1)

            for t in range(1, KT + 1):
                n = N_Z1 + t
                dve.wait_ge(zz_tanh, t)
                zr = zring[(t - 1) % ZRING]
                stt(halves(zr), halves(zr), 1.0, acc_of((n - 1) % 2), ADD, MUL).then_inc(acc_free[(n - 1) % 2], 1)
                if t < KT:
                    split_lo((n + 1) // 2, (n + 1) % 2, 0)
                    split_lo((n + 1) // 2, (n + 1) % 2, 1)
                if t == 2:
                    dve.wait_ge(norm_sum, 2)
                    order(ts(halves(mean), gp[:, 0:2, 0:HALF], 1.0 / D))
                    fence()
                    dve.wait_ge(c_done, KT)
                    for k in range(KT):
                        tt(full[:, k, :], full[:, k, :], mean, SUB).then_inc(centred, 1)
                if t == 6:
                    take_mean_square(2, 3)
                    take_reciprocal(2)
                for k in LN_Y.get(t, ()):
                    tt(full[:, k, :], full[:, k, :], rstd, MUL).then_inc(ln_scaled, 1)
                for k in LN_Y.get(t, ()):
                    dve.wait_ge(ln_tanh, k + 1)
                    order(stt(full[:, k, :], sqb[k % 2], 1.0, full[:, k, :], ADD, MUL))
                    fence()
                    dve.wait_ge(acc_free[(N_Z1 + k) % 2], (N_Z1 + k) // 2 + 1)
                    stt(full[:, k, :], full[:, k, :], 0.5, zring[k % ZRING], MUL, MUL).then_inc(y_done, 1)
            out_section(N_OUT1, 3)
            take_mean_square(3, 4)
            take_reciprocal(3)
            for k in range(KT):
                stt(full[:, k, :], full[:, k, :], par[:, P_GF + k:P_GF + k + 1], rstd, MUL, MUL).then_inc(scaled, 1)

        @block.gpsimd
        def _(pool):
            def order(ins):
                pool_t.inc(ins)

            def fence():
                pool.wait_ge(pool_t.sem, pool_t.now())

            def tt(out, a, b, op=ALU.mult):
                return pool.tensor_tensor(out, a, b, op)

            def copy(out, a):
                one = ones[0:a.shape[0], 0:1]
                return tt(out, a, (one if len(a.shape) == 2 else one.unsqueeze(2)).to_broadcast(list(a.shape)))

            def act_lo_odd(turn):
                for k in range(1, KT, 2):
                    pool.wait_ge(ahi_done, KT * turn + k + 1)
                    tt(act_lo[:, k, :], full[:, k, :], act_hi[:, k, :].bitcast(F32), ALU.subtract) \
                        .then_inc(alo_odd, 1)

            pool.memset(mhalf, -0.5)
            pool.memset(eps_p2, EPS * P * P)
            act_lo_odd(0)
            pool.wait_ge(root, 1)
            order(pool.memset(cin_p[:, 0:3], 0.0))
            pool.wait_ge(halved, 1)
            pool.wait_ge(prev_in, 16)

            dnw = par[:, P_DNW:P_DNW + 12 * H].rearrange("p (h t) -> p h t", h=H)

            def put_prev(hp, kb, j):
                if not (isinstance(hp, int) and hp == 0 and j == 0):
                    pool.wait_ge(conv_done, 3 * hp + j)
                if j == 0:
                    copy(cw[kb], dnw[:, hp, :])
                copy(cin_s[:, :, 0:3], dnc[:, 3 * hp + j, 1:9, :]).then_inc(prev_put, 1)

            def take_last(hp, j):
                m, s = 2 * hp + (1 + j) // 2, (1 + j) % 2
                pool.wait_ge(acc_free[s], m + 1)
                pool.wait_ge(prev_put, 3 * hp + (j + 1))
                copy(dnc[:, 3 * hp + j, 0, :], cin_p[:, SEQ:SEQ + 3])
                copy(dnc[:, 3 * hp + j, 1:9, :], cin_s[:, :, NT:NT + 3]).then_inc(last_taken, 1)

            def head_pool(it, name):
                own = lambda n: pool.wait_ge(pool_h.sem, pool_h.at(n, it))
                dv = lambda n: pool.wait_ge(dve_h.sem, dve_h.at(n, it))
                if name == "scalars":
                    if isinstance(it, int) and it == 0:
                        pool.wait_ge(prep, 4)
                    else:
                        pool.wait_ge(dve_h.sem, dve_h.at("y", it - 1))
                    ins = copy(hs, gates[:, it])
                elif name == "gB":
                    own("scalars")
                    ins = copy(gB, per_row(hs[:, KG, 0:4], P))
                elif name == "nrm":
                    dv("ssum")
                    ins = tt(nrm, ssum, mh[:, 0:8], ALU.pow)
                elif name == "rn":
                    own("nrm")
                    ins = tt(rn, ssum, nrm)
                elif name == "bn":
                    ins = tt(bn, hs[:, KBETA, 0:4], nrm[:, 0:4])
                elif name == "bp":
                    own("bn")
                    ins = tt(bp, bn, nrm[:, 0:4])
                elif name[0] == "L":
                    l = int(name[1])
                    dv("Mt")
                    if l == 2:
                        dv("Xt")
                    if l >= 2:
                        pool.wait_ge(pe_h.sem, pe_h.at("m0" if l == 2 else f"a{l - 2}", it))
                    lo = C_LVL + l * P
                    ins = tt(mtl[l % 2], mt, per_group(cst[:, lo:lo + P], 4))
                elif name == "f1":
                    pool.wait_ge(act_h.sem, act_h.at("osq", it))
                    ins = tt(f_a, osum, nrm[:, 4:8])
                elif name == "f2":
                    own("f1")
                    ins = tt(f_b, f_a, nrm[:, 4:8])
                elif name == "f3":
                    own("f2")
                    ins = tt(f_a, f_b, eps_p2[:, 0:4], ALU.add)
                elif name == "f4":
                    own("f3")
                    ins = tt(f_b, f_a, mh[:, 0:4], ALU.pow)
                else:
                    own("f4")
                    ins = tt(f_a, f_b, nrm[:, 4:8])
                ins.then_inc(pool_h.sem, 1)

            def head_unit(hp, it=None, kb=0, convs=True):
                for ti in range(4):
                    for e in range(8):
                        if it is not None:
                            for name in POOL_PLAN.get(8 * ti + e, ()):
                                head_pool(it, name)
                            if 8 * ti + e == 29:
                                pool.wait_ge(dve_h.sem, dve_h.at(f"S{NC - 1}", it))
                                pool.dma_start(dn_out[it], st).then_inc(state_out, 16)
                        if convs and ti and e == 1:
                            take_last(hp, ti - 1)
                        if convs and (ti == 0 or e == 5) and 8 * ti + e in (0, 13, 21):
                            put_prev(hp, 1 - kb, ti)

            head_unit(0, kb=1)
            with pool.Fori(0, 3) as i:
                head_unit(2 * i + 1, 2 * i, 0)
                head_unit(2 * i + 2, 2 * i + 1, 1)
            head_unit(7, 6, 0)
            pool.wait_ge(last_taken, 3 * H)
            pool.dma_start(dnc_out, dnc.rearrange("p n s t -> p (n s t)")).then_inc(dnc_stored, 16)
            head_unit(8, 7, 1, convs=False)

            def samp_pool_step(name):
                own = lambda n: pool.wait_ge(samp_pool, SP_[n])
                kq = lambda ap, j: ap.rearrange("p (h s) -> p h s", s=2)[:, :, j]
                if name == "gB":
                    pool.wait_ge(dve_h.sem, dve_h.at("y", H - 1))
                    ins = copy(gB_s, per_row(gates[0:NS, :, KG, 4], NS))
                elif name == "nrm":
                    pool.wait_ge(samp_dve, SD["ssum"])
                    ins = tt(nrm_s, ssum_s, mh[0:NS, 0:16], ALU.pow)
                elif name == "rn":
                    own("nrm")
                    ins = tt(rn_s, ssum_s, nrm_s)
                elif name == "bn":
                    ins = tt(bn_s, gates[0:NS, :, KBETA, 4], kq(nrm_s, 0))
                elif name == "bp":
                    own("bn")
                    ins = tt(bp_s, bn_s, kq(nrm_s, 0))
                elif name[0] == "L":
                    l = int(name[1])
                    pool.wait_ge(samp_dve, SD["Mtb"])
                    if l == 2:
                        pool.wait_ge(samp_dve, SD["Xt"])
                    lo = C_LVL + l * P
                    ins = tt(mtl_s[l % 2], mt_s, per_group(cst[0:NS, lo:lo + NS], H))
                elif name[0:2] == "vx":
                    h = int(name[2:])
                    pool.wait_ge(samp_dve, SD[f"vp{h}"])
                    if h:
                        pool.wait_ge(samp_pe, SPE[f"ns{h - 1}"])
                    ins = tt(vpx, vps.unsqueeze(1).to_broadcast([NS, NB, P]), per_row(cst[0:NS, C_SEQ:C_SEQ + NB], P))
                elif name == "f1":
                    pool.wait_ge(samp_act, SA["osq"])
                    ins = tt(fa_s, sos, kq(nrm_s, 1))
                elif name == "f2":
                    own("f1")
                    ins = tt(fb_s, fa_s, kq(nrm_s, 1))
                elif name == "f3":
                    own("f2")
                    ins = tt(fa_s, fb_s, eps_p2[0:NS], ALU.add)
                elif name == "f4":
                    own("f3")
                    ins = tt(fb_s, fa_s, mh[0:NS, 0:8], ALU.pow)
                else:
                    own("f4")
                    ins = tt(fa_s, fb_s, kq(nrm_s, 1))
                ins.then_inc(samp_pool, 1)

            def store_state(h):
                pool.wait_ge(samp_dve, SD[f"S{h}"])
                pool.dma_start(sdn_out[h], s0[h % 2].rearrange("p b d -> p (b d)")).then_inc(sdn_stored[h % 2], 16)

            for name in SP_:
                if name == "f1":
                    store_state(H - 1)
                samp_pool_step(name)
                if name[0:2] == "vx" and name != "vx0":
                    store_state(int(name[2:]) - 1)

            pool.wait_ge(vtok_done, 1)
            pool.dma_start(win_v, v_tok[:, NC - 1].rearrange("p r d -> p (r d)")).then_inc(out_small, 16)
            pool.wait_ge(kc_in, 16)
            for r in range(2):
                pool.dma_start(win_k[r], kv[:, 2 * r, blk(NC - 1):blk(NC - 1) + P]).then_inc(out_small, 16)
                pool.dma_start(swk_out[r, :, :, 0:W - NT], kc[:, r, :, NT:W]).then_inc(out_small, 16)
                for a_ in range(2):
                    pool.dma_start(swk_out[r, :, 4 * a_:4 * a_ + 4, W - NT:W],
                                   kv[:, 2 * r, a_ * HALF + HP:(a_ + 1) * HALF].rearrange("p (b t) -> p b t", t=NT)) \
                        .then_inc(out_small, 16)
            pool.wait_ge(vc_in, 16)
            pool.dma_start(swv_out[0:W - NT], vc[NT:W].rearrange("p b d -> p (b d)")).then_inc(out_small, 16)
            pool.wait_ge(turned, 16)
            pool.wait_ge(acc_free[(N_Q + 7) % 2], (N_Q + 7) // 2 + 1)
            for r in range(2):
                for a_ in range(2):
                    copy(q_samp[:, r, 4 * a_:4 * a_ + 4, :].rearrange("p b (g t) -> p g b t", g=4),
                                     full[:, 4 * r:4 * r + 4, a_ * HALF + HP:(a_ + 1) * HALF]
                                     .rearrange("p g (b t) -> p g b t", t=NT)).then_inc(q_samp_put, 1)
            for r in range(2):
                pool.wait_ge(sa_act, SAA[f"v_new{r}"])
                pool.dma_start(swv_out[W - NT:W].rearrange("p (b r d) -> p r b d", b=NB, r=2)[:, r], v_new[0:NT]) \
                    .then_inc(vnew_stored, 16)

            def out_section(turn):
                act_lo_odd(turn)
                base = KT if turn == 1 else 2 * KT
                for j in range(2):
                    pool.wait_ge(sq_done, base + j + 1)
                    if j == 0:
                        pool.tensor_copy(ssq, sqb[0]).then_inc(sq_summed, 1)
                    else:
                        pool.wait_ge(sq_summed, base - KT + 1)
                        tt(ssq, ssq, sqb[1], ALU.add).then_inc(sq_summed, 1)
                with pool.Fori(0, KT // 2 - 1) as i:
                    for b in range(2):
                        pool.wait_ge(sq_done, 2 * i + (base + 3 + b))
                        pool.wait_ge(sq_summed, 2 * i + (base - KT + 2 + b))
                        tt(ssq, ssq, sqb[b], ALU.add).then_inc(sq_summed, 1)

            out_section(1)
            act_lo_odd(2)
            for b in range(2):
                pool.memset(u_p[b][:, 0:CP], 0.0).then_inc(u_free[b], 1)
            pool.memset(pacc, 0.0).then_inc(tap_sum, 1)

            def conv_tile(j, b, rnd):
                pool.wait_ge(acc_free[0], j + (N_VG // 2 + 2))
                pool.wait_ge(uprev_in[b], 16 * rnd + 16)
                pool.dma_start(cf_out[j], u_p[b][:, SEQ:SEQ + CP]).then_inc(cf_stored, 16)
                pool.dma_start(cfs_out[j].rearrange("p (b t) -> p b t", b=NB), u_s[b][:, :, NT:NT + CP]).then_inc(cf_stored, 16)
                for i_ in range(1, POOL_TAPS):
                    src = prod[(i_ + b * POOL_TAPS) % 2]
                    pool.wait_ge(tap_prod, POOL_TAPS * j + (i_ + 1))
                    if i_ == 1:
                        if not (isinstance(j, int) and j == 0):
                            pool.wait_ge(c_done, j)
                        tt(pacc, prod[(b * POOL_TAPS) % 2], src, ALU.add).then_inc(tap_sum, 1)
                    else:
                        pool.wait_ge(tap_sum, POOL_SUMS * j + i_)
                        tt(pacc, pacc, src, ALU.add).then_inc(tap_sum, 1)

            def sum_tile(j, source, ready):
                pool.wait_ge(ready, j + 1)
                if isinstance(j, int) and j == 0:
                    return pool.tensor_copy(csum, source).then_inc(c_summed, 1)
                pool.wait_ge(c_summed, j)
                tt(csum, csum, source, ALU.add).then_inc(c_summed, 1)

            conv_tile(0, 0, 0)
            conv_tile(1, 1, 0)
            pool.wait_ge(scaled, 2 * KT)
            sum_tile(0, full[:, 0, :], c_done)
            with pool.Fori(0, KT // 2 - 1) as i:
                for b in range(2):
                    conv_tile(2 * i + 2 + b, b, i + 1)
                    sum_tile(2 * i + 1 + b, full[:, 2 * i + 1 + b, :], c_done)
            sum_tile(KT - 1, full[:, KT - 1, :], c_done)
            pool.wait_ge(norm_sum, 2)
            for k in range(KT):
                pool.wait_ge(ln_sq, k + 1)
                if k == 0:
                    pool.tensor_copy(csum, sqb[0]).then_inc(c_summed, 1)
                else:
                    pool.wait_ge(c_summed, KT + k)
                    tt(csum, csum, sqb[k % 2], ALU.add).then_inc(c_summed, 1)
            out_section(3)


_OUT = [("y", (KT, P, TOK)), ("win_k", (2, P, P)), ("win_v", (P, 2 * P)), ("dn", (H, P, P)), ("dnc", (P, 3 * H * 27)),
        ("cf", (KT, P, CP)), ("cfs", (KT, P, NB * CP)), ("swk", (2, P, NB, W)), ("swv", (W, NB * 2 * P)),
        ("sdn", (H, P, NB * P))]


def _constants():
    i, j = np.arange(P)[None, :], np.arange(P)[:, None]
    c = np.zeros((P, N_CONST), np.float32)
    c[:, C_ID:C_ID + P] = i == j
    c[:, C_TRI:C_TRI + P] = j <= i
    c[:, C_ONE:C_ONE + P] = 1
    c[:, C_NEG:C_NEG + P] = np.where(j <= i, 0, NEG)
    c[:, C_CAU:C_CAU + P] = np.where(i >= j, 0, NEG)
    c[:, C_CAU + P:C_CAU + 2 * P] = np.where(i <= j, 0, NEG)
    for l in range(LEVELS):
        b = 1 << l
        c[:, C_LVL + l * P:C_LVL + (l + 1) * P] = (i // (2 * b) == j // (2 * b)) & (j // b % 2 == 0) & (i // b % 2 == 1)
    i, j = i[:, :NS], j[:NS]
    same = i // NT == j // NT
    c[:NS, C_TRIS:C_TRIS + NS] = same & (j <= i)
    c[:NS, C_ONES:C_ONES + NS] = same
    c[:NS, C_NEGS:C_NEGS + NS] = np.where(same & (j <= i), 0, NEG)
    c[:NS, C_SEQ:C_SEQ + NB] = j // NT == np.arange(NB)[None, :]
    t = np.arange(P)[:, None] % NT
    c[:, C_WIN:C_WIN + W] = np.where(np.arange(W)[None, :] >= t, 0, NEG)
    c[:, C_WIN + W:] = np.where(np.arange(NT)[None, :] <= t, 0, NEG)
    return c


def kernel(x_prompt, x_sample, cache_win_k, cache_win_v, state_dn, state_dn_conv, state_cf_conv, norm_gain,
           w_in_even, w_out_even, attn_sinks, dn_conv_w, dn_a_log, dn_dt_bias, dn_norm_gain, w_in_odd, w_out_odd,
           cf_conv_w, cf_conv_b, cf_ln_gain, cf_ln_bias, final_norm_gain):
    import concourse.bacc as bacc
    from concourse.bass_utils import run_bass_kernel_spmd

    f32 = np.float32
    x_prompt, x_sample, cache_win_k, cache_win_v, state_dn, state_dn_conv, state_cf_conv = (
        np.asarray(a) for a in (x_prompt, x_sample, cache_win_k, cache_win_v, state_dn, state_dn_conv, state_cf_conv))
    w0, wo0, w1, wo1 = (np.asarray(a)[0] for a in (w_in_even, w_out_even, w_in_odd, w_out_odd))

    def channel_major(prompt, sample):
        x = np.empty((2, HALF, D), f32)
        x[:, :HP] = prompt.reshape(2, HP, D)
        x[:, HP:] = sample.reshape(2, HS, D)
        return np.ascontiguousarray(x.reshape(TOK, KT, P).transpose(1, 2, 0))

    QA, KA, VA, ZA, QKV = 0, 1024, 1280, 1536, 2560
    AB, ZB = QKV + 3 * D // 2, QKV + 3 * D // 2 + 16

    def tiles(w, first=0):
        return w.reshape(KT, P, -1, P).transpose(2, 1, 0, 3).reshape(-1, P, KT * P)

    heads = [[(2 * r) * 4 + g, (2 * r + 1) * 4 + g] for r in range(2) for g in range(4)]
    perm = np.concatenate([np.arange(64 * h, 64 * h + 64) for pair in heads for h in pair])
    wt = np.zeros((N_TILES, P, D), f32)
    ab = np.zeros((D, P), f32)
    ab[:, 0:16] = w0[:, AB:AB + 16]
    wt[N_AB:N_AB + 1] = tiles(ab)
    for h in range(H):
        c = QKV + h * P
        cols = [w0[:, c + D // 2:c + D // 2 + P], w0[:, c:c + P], w0[:, c + D:c + D + P], w0[:, ZB + h * P:ZB + (h + 1) * P]]
        wt[N_HEAD + 4 * h:N_HEAD + 4 * h + 4] = tiles(np.concatenate(cols, 1))
    for r in range(2):
        wt[N_KV + 2 * r:N_KV + 2 * r + 2] = tiles(np.concatenate(
            [w0[:, KA + r * P:KA + (r + 1) * P], w0[:, VA + r * P:VA + (r + 1) * P]], 1))
    wt[N_Q:N_Q + 8] = tiles(w0[:, QA:QA + 1024][:, perm])
    wt[N_ZA:N_ZA + 8] = tiles(w0[:, ZA:ZA + 1024][:, perm])
    wt[N_OUT0:N_OUT0 + KT] = tiles(np.concatenate([wo0[:1024][perm], wo0[1024:]], 0))
    wt[N_VG:N_VG + 2 * KT:2] = tiles(w1[:, D:2 * D])
    wt[N_VG + 1:N_VG + 2 * KT:2] = tiles(w1[:, :D])
    wt[N_Z1:N_Z1 + KT] = tiles(w1[:, 2 * D:])
    wt[N_OUT1:] = tiles(wo1)

    param = np.zeros((P, N_PARAM), f32)
    per_channel = lambda v: np.asarray(v).reshape(-1, P).T
    for c, v in ((P_G0, norm_gain[0]), (P_G1, norm_gain[1]), (P_GF, final_norm_gain), (P_CFB, cf_conv_b[0]),
                 (P_LNG, cf_ln_gain[0]), (P_LNB, cf_ln_bias[0])):
        param[:, c:c + KT] = per_channel(v)
    dnw = np.asarray(dn_conv_w)[0].reshape(4, 3, H, P)[:, [1, 0, 2]]
    param[:, P_DNW:P_DNW + 12 * H] = dnw.transpose(3, 2, 1, 0).reshape(P, -1)
    param[:, P_CFW:P_CFW + KT * CF] = np.asarray(cf_conv_w)[0].reshape(CF, KT, P).transpose(2, 1, 0).reshape(P, -1)
    param[:, P_DNG] = np.asarray(dn_norm_gain)[0]
    param[:, P_ALOG:P_ALOG + H] = np.asarray(dn_a_log)[0]
    param[:, P_DTB:P_DTB + H] = np.asarray(dn_dt_bias)[0]
    sinks = np.asarray(attn_sinks)[0]
    order = [(2 * r + q) * 4 + 2 * jj + j for r in range(2) for jj in range(2) for q in range(2) for j in range(2)]
    param[:, P_SINK:P_SINK + 16] = sinks[order]
    param[:, P_SINKS] = np.repeat(sinks, NT)

    prev = state_dn_conv[0].reshape(NB, 3, 3, H, P)[:, :, [1, 0, 2]].transpose(4, 3, 2, 0, 1).reshape(P, 3 * H, NB, 3)
    arrays = dict(
        x=channel_major(x_prompt[0], x_sample), wt=wt, const=_constants(), param=param,
        dn_prev=prev,
        state_in=state_dn[0].transpose(1, 2, 0, 3).reshape(H, P, NB * P),
        k_cache=cache_win_k[0].reshape(NB, W, 2, P).transpose(2, 3, 0, 1),
        v_cache=cache_win_v[0].reshape(NB, W, 2 * P).transpose(1, 0, 2).reshape(W, -1),
        cf_prev=state_cf_conv[0].reshape(NB, CP, KT, P).transpose(2, 3, 0, 1))
    arrays = {k: np.ascontiguousarray(v) for k, v in arrays.items()}

    nc = bacc.Bacc("TRN2", target_bir_lowering=False, num_devices=1)
    args = [nc.dram_tensor(k, v.shape, F32, kind="ExternalInput").ap() for k, v in arrays.items()]
    args += [nc.dram_tensor("out_" + k, shape, F32, kind="ExternalOutput").ap() for k, shape in _OUT]
    hybrid_step(nc, *args)
    got = run_bass_kernel_spmd(nc, [arrays], core_ids=[0]).results[0]
    o = {k: got["out_" + k] for k, _ in _OUT}

    y = o["y"].transpose(2, 0, 1).reshape(2, HALF, D)
    dnc = o["dnc"].reshape(P, H, 3, 9, 3)[:, :, [1, 0, 2]].transpose(3, 4, 2, 1, 0).reshape(9, 3, 3 * H * P)
    return (y[:, :HP].reshape(1, SEQ, D), y[:, HP:].reshape(NB, NT, D),
            o["win_k"].transpose(2, 0, 1).reshape(1, 1, W, 4, 64), o["win_v"].reshape(1, 1, W, 4, 64),
            o["dn"].reshape(1, 1, H, P, P), dnc[0].reshape(1, 1, 3, -1),
            o["cf"].transpose(2, 0, 1).reshape(1, 1, CP, D),
            o["swk"].transpose(2, 3, 0, 1).reshape(1, NB, W, 4, 64),
            o["swv"].reshape(W, NB, 4, 64).transpose(1, 0, 2, 3)[None],
            o["sdn"].reshape(H, P, NB, P).transpose(2, 0, 1, 3)[None], dnc[1:][None],
            o["cfs"].reshape(KT, P, NB, CP).transpose(2, 3, 0, 1).reshape(1, NB, CP, D))
```

```python
from contextlib import ExitStack

import numpy as np
import concourse.bass as bass
from concourse import mybir

F32 = mybir.dt.float32
F32R = mybir.dt.float32r
ALU = mybir.AluOpType
ACT = mybir.ActivationFunctionType
AX_X = mybir.AxisListType.X

P = 128
D = 2048
KT = D // P
NB, NT = 8, 8
SEQ = 512
NC = SEQ // P
NS = NB * NT
HP, HS = SEQ // 2, NS // 2
HALF = HP + HS
TOK = 2 * HALF
H = 8
W = 128
EPS = 1e-6
CF = 31
CP = CF - 1
LEVELS = 7
NEG = -1.0e30

N_AB, N_HEAD, N_KV, N_Q, N_ZA = 0, 1, 1 + 4 * H, 5 + 4 * H, 13 + 4 * H
N_OUT0 = N_ZA + 8
N_VG = N_OUT0 + KT
N_Z1 = N_VG + 2 * KT
N_OUT1 = N_Z1 + KT
N_TILES = N_OUT1 + KT

C_ID, C_TRI, C_ONE, C_NEG = 0, 128, 256, 384
C_CAU = 512
C_LVL = C_CAU + 256
C_TRIS = C_LVL + LEVELS * 128
C_ONES, C_NEGS = C_TRIS + 64, C_TRIS + 128
C_SEQ = C_NEGS + 64
C_WIN = C_SEQ + NB
N_CONST = C_WIN + W + NT

P_G0, P_G1, P_GF = 0, 16, 32
P_DNW = 48
P_CFW = P_DNW + H * 12
P_CFB = P_CFW + KT * CF
P_LNG, P_LNB = P_CFB + 16, P_CFB + 32
P_DNG = P_LNB + 16
P_ALOG, P_DTB = P_DNG + 1, P_DNG + 9
P_SINK = P_DTB + 8
P_SINKS = P_SINK + 16
N_PARAM = P_SINKS + 1


class Steps:

    def __init__(self, sem, names):
        self.sem, self.names, self.index = sem, names, {n: i for i, n in enumerate(names)}

    def at(self, name, it=0):
        return it * len(self.names) + self.index[name] + 1


class Tally:

    def __init__(self, sem):
        self.sem, self.base, self.k, self.it, self.per = sem, 0, 0, None, 0

    def inc(self, ins):
        ins.then_inc(self.sem, 1)
        self.k += 1

    def now(self):
        return self.base + self.k if self.it is None else self.it * self.per + (self.base + self.k)

    def enter(self, it, per):
        self.base, self.k, self.it, self.per = self.base + self.k, 0, it, per

    def leave(self, rounds):
        assert self.k == self.per, f"{self.sem}: {self.k} increments in a round, not {self.per}"
        self.base, self.k, self.it = self.base + rounds * self.per, 0, None


LV = range(1, LEVELS)
PE_HEAD = (["kv_tok", "gcum", "norm", "gram", "m0"] + [f"{s}{i}" for i in LV for s in ("a", "x")]
           + ["u0", "so0"] + [f"{s}{c}" for c in range(1, NC) for s in ("s", "u", "so")] + ["o_chan"])
DVE_HEAD = (["kg", "dmask", "ssum", "vs", "Mt", "attn", "X", "Xt"] + [f"X{i}" for i in LV]
            + ["vp0", "S0", "o0"] + [f"{s}{c}" for c in range(1, NC) for s in ("r", "vp", "S", "o")]
            + ["on", "y"])
ACT_HEAD = ["sq", "decay"] + [f"A{i}" for i in LV] + [f"q{c}" for c in range(1, NC)] + ["osq"]
POOL_HEAD = (["scalars", "gB", "nrm", "rn", "bn", "bp"] + [f"L{i}" for i in range(LEVELS)]
             + ["f1", "f2", "f3", "f4", "f5"])
PE_PLAN = {1: "kv_tok", 2: "gcum", 3: "norm", 4: "gram", 6: "m0"}
PE_PLAN |= {7 + i: n for i, n in enumerate(PE_HEAD[5:-1])}


def counts(names):
    return {n: i + 1 for i, n in enumerate(names)}


_groups = [["k_tok"], ["v_tok"], ["norm"], [], ["gram"], ["gcum"], [], [], ["m0"], ["a1"], ["x1"], ["a2"], ["x2"]]
SAMP_PLAN = [[(n, None) for n in g] for g in _groups] + [[] for _ in range(13, 48)]
for _g in range(H // 2):
    for _at, _n in ((0, ("st", _g)), (2, ("tr", _g)), (3, ("u", _g)), (4, ("o", _g)), (5, ("ns", 2 * _g)),
                    (7, ("ns", 2 * _g + 1))):
        SAMP_PLAN[13 + 8 * _g + _at].append(_n)
SAMP_PLAN[46] = [("o_chan", None)]
ATT0 = 49
SATT0 = ATT0 + 3 * 16 - 1
SPE = counts([n if h is None else f"{n}{h}" for g in SAMP_PLAN for n, h in g])
SD = counts(["kg", "ssum", "vs", "dmask", "dmask2", "Mt", "Mtb", "attn", "X", "Xt", "X1", "Xt1", "Xt2"]
            + [f"{s}{h}" for g in range(H // 2) for s, h in (("r", g), ("vp", g), ("o", g), ("S", 2 * g), ("S", 2 * g + 1))]
            + ["on"])
SA = counts(["sq", "decay", "A1", "A2"] + [f"{s}{g}" for g in range(H // 2) for s in ("ks", "q")] + ["osq"])
SP_ = counts(["gB", "nrm", "rn", "bn", "bp", "L0", "L1", "L2"] + [f"vx{h}" for h in range(H)]
             + ["f1", "f2", "f3", "f4", "f5"])
SATT_PLAN = {1: "last_turn", 3: "last", 5: "scores", 11: "turn", 13: "turn_new", 16: "v_new0", 19: "weigh0", 22: "v_new1",
             25: "weigh1"}
SAP = counts(list(SATT_PLAN.values())[2:])
SATT_ACT = {2: ["last"], 3: ["last_out"], 8: ["exp"], 12: ["turned"], 17: ["v_new0"], 23: ["v_new1"]}
PE_AT = {n: i for i, n in PE_PLAN.items()}
ACT_PLAN = {1: ["sq"], 2: ["decay"]} | {PE_AT[f"a{i}"]: [f"A{i}"] for i in LV}
ACT_PLAN |= {PE_AT[f"s{c}"]: [f"q{c}"] for c in range(1, NC)} | {30: ["osq"]}
DVE_PLAN = {1: ["kg"], 2: ["dmask"], 3: ["ssum"], 4: ["vs", "Mt", "attn"], 6: ["X", "Xt"]}
DVE_PLAN |= {PE_AT[f"x{i}"]: [f"X{i}"] for i in LV} | {PE_AT["u0"]: ["vp0"], PE_AT["so0"]: ["S0", "o0"]}
for _c in range(1, NC):
    DVE_PLAN |= {PE_AT[f"s{_c}"]: [f"r{_c}"], PE_AT[f"u{_c}"]: [f"vp{_c}"], PE_AT[f"so{_c}"]: [f"S{_c}", f"o{_c}"]}
DVE_PLAN |= {31: ["on"]}
_at = {(n if h is None else f"{n}{h}"): i for i, g in enumerate(SAMP_PLAN) for n, h in g}
_after = {"kg": "k_tok", "ssum": "norm", "vs": "v_tok", "dmask": "gcum", "dmask2": "gcum", "Mt": "gcum",
          "Mtb": "gcum", "attn": "gcum", "X": "m0", "Xt": "m0", "X1": "x1", "Xt1": "x1", "Xt2": "x2",
          "on": f"ns{H - 1}"}
_after |= {f"{s}{g}": f"{q}{g}" for g in range(H // 2) for s, q in (("r", "tr"), ("vp", "u"), ("o", "o"))}
_after |= {f"S{h}": f"ns{h}" for h in range(H)}
_aact = {"sq": "k_tok", "decay": "gcum", "A1": "a1", "A2": "a2", "osq": f"o{H // 2 - 1}"}
_aact |= {f"{s}{g}": f"{q}{g}" for g in range(H // 2) for s, q in (("ks", "st"), ("q", "tr"))}


def by_slot(order, after):
    plan, last = {}, 0
    for n in order:
        last = max(last, _at[after[n]])
        plan.setdefault(last, []).append(n)
    return plan


SAMP_DVE, SAMP_ACT = by_slot(SD, _after), by_slot(SA, _aact)
LN_SQ = {3: range(0, 6), 4: range(6, 12), 5: range(12, 16)}
LN_Y = {7: (0, 1), 8: (2, 3), 9: (4, 5), 10: (6, 7), 11: (8, 9)} | {k + 2: (k,) for k in range(10, 13)}
LN_Y |= {15: (13, 14), 16: (15,)}
SAD = counts(["bias0", "bias1", "bias2", "max", "max2", "neg", "sub", "den", "inv", "prob", "turned_new",
              "out0", "out1"])
SAA = counts(["exp", "turned", "v_new0", "v_new1"])
SATT_DVE = {5: "bias", 10: "prob", 14: "turned_new", 20: "out0", 26: "out1"}
POOL_PLAN = {0: ["scalars", "gB"], 3: ["nrm", "rn", "bn", "bp"], 4: ["L0", "L1"], 7: ["L2"]}
POOL_PLAN |= {PE_AT[f"a{l - 2}"] + 1: [f"L{l}"] for l in range(3, LEVELS)} | {30: ["f1", "f2", "f3", "f4", "f5"]}
DVE_TAPS = 16
POOL_TAPS = CF - DVE_TAPS
POOL_SUMS = POOL_TAPS - 1
assert POOL_TAPS % 3 == 0
ZRING = 7


LOW_LAG = (2, 12, 2, 2)


def split_order(turn):
    return [(k + 8) % KT for k in range(KT)] if turn == 1 else list(range(KT))


def blk(c):
    return (c // 2) * HALF + (c % 2) * P


def hybrid_step(nc, x, wt, const, param, dn_prev, state_in, k_cache, v_cache, cf_prev,
                y, win_k, win_v, dn_out, dnc_out, cf_out, cfs_out, swk_out, swv_out, sdn_out):
    x1_dram = nc.dram_tensor("x1_scratch", (KT, P, TOK), F32, kind="Internal").ap()
    with ExitStack() as ctx:
        def sb(name, shape, dt=F32):
            return ctx.enter_context(nc.sbuf_tensor(name, shape, dt))

        def sem(name):
            return ctx.enter_context(nc.semaphore(name))

        act_hi = sb("act_hi", [P, KT, TOK], F32R)
        act_lo = sb("act_lo", [P, KT, TOK], F32R)
        full = sb("full", [P, KT, TOK])
        w_raw = sb("w_raw", [P, 2, 8 * P])
        w_hi = sb("w_hi", [P, 2, KT * P], F32R)
        w_lo = sb("w_lo", [P, 2, KT * P], F32R)
        cst = sb("cst", [P, N_CONST])
        par = sb("par", [P, N_PARAM])
        small = sb("small", [P, 464])
        arena = sb("arena", [P, 12076])
        acc = ctx.enter_context(nc.psum_tensor("acc", [P, 2, 2, 512], F32))
        gp = ctx.enter_context(nc.psum_tensor("gp", [P, 4, 512], F32))

        ident, tri, ones = cst[:, C_ID:C_ID + P], cst[:, C_TRI:C_TRI + P], cst[:, C_ONE:C_ONE + P]
        negm, caus = cst[:, C_NEG:C_NEG + P], cst[:, C_CAU:C_CAU + 2 * P]

        cfw = par[:, P_CFW:P_CFW + KT * CF].rearrange("p (j t) -> p j t", t=CF)
        cfb = par[:, P_CFB:P_CFB + KT].unsqueeze(2)

        def halves(ap):
            return ap.rearrange("p (a c) -> p a c", a=2)

        def half_blocks(ap, level, half):
            return ap.rearrange("p (n a b) -> p n a b", a=2, b=1 << level)[:, :, half, :]

        def bank4(lo, n=1):
            return gp[:, lo:lo + n, :].rearrange("p b (c t) -> p (b c) t", t=P)

        o = 0

        def cut(n, *dims):
            nonlocal o
            a = arena[:, o:o + n]
            o += n
            assert o <= 11500, o
            return a

        conv_in = cut(3 + SEQ + NB * (3 + NT) + 1)
        cin_p = conv_in[:, 0:3 + SEQ]
        cin_s = conv_in[:, 3 + SEQ:3 + SEQ + NB * (3 + NT)].rearrange("p (b t) -> p b t", b=NB)
        kqv0 = cut(3 * SEQ).rearrange("p (s t) -> p s t", s=3)
        conv_y = cut(SEQ + NS)
        conv_t = cut(SEQ + NS)
        kqv1 = cut(3 * SEQ).rearrange("p (s t) -> p s t", s=3)
        kqv = [kqv0, kqv1]
        kg = cut(SEQ).rearrange("p (c t) -> p c t", t=P)
        vs = cut(SEQ).rearrange("p (c t) -> p c t", t=P)
        attn = cut(SEQ).rearrange("p (c t) -> p c t", t=P)
        o_tok = cut(SEQ).rearrange("p (c t) -> p c t", t=P)
        a1 = cut(SEQ).rearrange("p (c t) -> p c t", t=P)
        st = cut(P)
        rr, vp, qs = cut(P), cut(P), cut(P)
        head_top = o
        dnc = cut(3 * H * 27).rearrange("p (n s t) -> p n s t", s=9, t=3)
        samp = cut(H * 3 * NS).rearrange("p (h s t) -> p h s t", h=H, s=3)
        gates = cut(H * 35).rearrange("p (h k c) -> p h k c", h=H, k=7)
        KG, KNG, KEG, KNEG, KEK, KEL, KBETA = range(7)
        fa = full[:, 0:8, :].rearrange("p k t -> p (k t)")
        dec = fa[:, 0:512].rearrange("p (c t) -> p c t", t=P)
        mt = fa[:, 512:1024].rearrange("p (c t) -> p c t", t=P)
        mtl = [fa[:, 1024 + 512 * i:1536 + 512 * i].rearrange("p (c t) -> p c t", t=P) for i in range(2)]
        gB = fa[:, 2048:2560].rearrange("p (c t) -> p c t", t=P)
        xx = fa[:, 2560:3584].rearrange("p (s c t) -> p s c t", s=2, t=P)
        sqkq = fa[:, 3584:4608].rearrange("p (s t) -> p s t", s=2)
        sqkq_c = fa[:, 3584:4608].rearrange("p (s c t) -> p (s c) t", s=2, t=P)
        on = fa[:, 3584:4096].rearrange("p (c t) -> p c t", t=P)
        hs = small[:, 0:35].rearrange("p (k c) -> p k c", k=7)
        cw = [small[:, 40:52], small[:, 52:64]]
        ssum, nrm, rn = small[:, 64:72], small[:, 72:80], small[:, 80:88]
        bp, bn = small[:, 88:92], small[:, 92:96]
        osum, f_a, f_b = small[:, 96:100], small[:, 100:104], small[:, 104:108]
        mhalf = small[:, 108:124]
        dng = small[:, 124:125]
        ea = small[:, 128:136]
        lg, lb = small[:, 136:152], small[:, 152:168]
        sm4 = small[:, 168:464]

        cb = 0

        def tiny(n):
            nonlocal cb
            cb += n
            assert cb <= 296
            return sm4[:, cb - n:cb]

        nmax, esum, esink, dsink = ([tiny(4), tiny(4)] for _ in range(4))
        amax, nmax_s, esum_s, amax_s, dsink_s = tiny(4), tiny(8), tiny(8), tiny(8), tiny(8)
        sos, ssum_s, nrm_s, rn_s = tiny(8), tiny(16)[0:NS], tiny(16)[0:NS], tiny(16)[0:NS]
        bn_s, bp_s, fa_s, fb_s = (tiny(8)[0:NS] for _ in range(4))
        egl_s = tiny(64).rearrange("p (h b) -> p h b", h=H)
        sos = sos[0:NS]
        eps_p2 = tiny(8)
        mh = mhalf

        x_in = [sem(f"x_in{i}") for i in range(8)]
        cst_in, par_in, prev_in = sem("cst_in"), sem("par_in"), sem("prev_in")
        raw_in = [sem("raw_in0"), sem("raw_in1")]
        whi_done, wlo_done = sem("whi_done"), sem("wlo_done")
        w_used = sem("w_used")
        acc_free = [sem("acc_free0"), sem("acc_free1")]
        ahi_done, alo_even, alo_odd = sem("ahi_done"), sem("alo_even"), sem("alo_odd")
        scaled, sq_used = sem("scaled"), sem("sq_used")
        sq_done, sq_summed = sem("sq_done"), sem("sq_summed")
        ones_set = sem("ones_set")
        norm_sum, var_ready, root = sem("norm_sum"), sem("var_ready"), sem("root")
        root_wide, root_out = sem("root_wide"), sem("root_out")
        dve_t, act_t, pool_t = Tally(sem("dve_order")), Tally(sem("act_order")), Tally(sem("pool_order"))
        pe_h, dve_h = Steps(sem("pe_head"), PE_HEAD), Steps(sem("dve_head"), DVE_HEAD)
        act_h, pool_h = Steps(sem("act_head"), ACT_HEAD), Steps(sem("pool_head"), POOL_HEAD)
        conv_tanh, conv_done = sem("conv_tanh"), sem("conv_done")
        conv_silu = sem("conv_silu")
        prev_put, last_taken = sem("prev_put"), sem("last_taken")
        z_tanh = sem("z_tanh")
        state_out = sem("state_out")
        out_small, vnew_stored, dnc_stored = sem("out_small"), sem("vnew_stored"), sem("dnc_stored")
        prep, prep_pe, prep_act = sem("prep"), sem("prep_pe"), sem("prep_act")
        s0_in = [sem(f"s0_in{i}") for i in range(4)]
        sdn_stored = [sem(f"sdn_stored{i}") for i in range(4)]
        ys_done = sem("ys_done")
        gated, halved = sem("gated"), sem("halved")
        samp_pe, samp_dve = sem("samp_pe"), sem("samp_dve")
        samp_act, samp_pool = sem("samp_act"), sem("samp_pool")
        kc_in, vc_in = sem("kc_in"), sem("vc_in")
        vtok_pe, vtok_done = sem("vtok_pe"), sem("vtok_done")
        scores, biased, exped, probs = sem("scores"), sem("biased"), sem("exped"), sem("probs")
        turned, turned_out, weighed, attn_out = sem("turned"), sem("turned_out"), sem("weighed"), sem("attn_out")
        q_samp_put = sem("q_samp_put")
        sa_pe, sa_dve, sa_act = sem("sa_pe"), sem("sa_dve"), sem("sa_act")
        res_in = [sem("res_in0"), sem("res_in1")]
        res_free, x1_stored = sem("res_free"), sem("x1_stored")
        u_free, uprev_in = [sem("u_free0"), sem("u_free1")], [sem("uprev_in0"), sem("uprev_in1")]
        cf_stored = sem("cf_stored")
        tap_prod, tap_sum, c_done, c_summed = sem("tap_prod"), sem("tap_sum"), sem("c_done"), sem("c_summed")
        zz_tanh = sem("zz_tanh")
        centred, ln_sq, ln_aff, ln_tanh, y_done = (sem("centred"), sem("ln_sq"), sem("ln_aff"), sem("ln_tanh"),
                                                   sem("y_done"))
        ln_scaled = sem("ln_scaled")
        fin_stored = sem("fin_stored")
        n_small = 10
        finals = [(x1_stored, 16 * KT), (state_out, 16 * H), (dnc_stored, 16), (out_small, 16 * n_small),
                  (vnew_stored, 32), (cf_stored, 32 * KT), (fin_stored, 16 * KT)] \
            + [(s, 16 * (H // 4)) for s in sdn_stored]
        block = ctx.enter_context(nc.Block())

        kv = arena[:, 0:4 * TOK].rearrange("p (s t) -> p s t", s=4)
        v_tok = arena[:, 2304:3328].rearrange("p (c r d) -> p c r d", c=NC, r=2)
        kc = arena[:, 3328:5376].rearrange("p (r b t) -> p r b t", r=2, b=NB)
        vc = arena[:, 5376:7424].rearrange("p (b d) -> p b d", b=NB)
        prob = [arena[:, 7424 + 1024 * i:8448 + 1024 * i].rearrange("p (g t) -> p g t", g=4)
                for i in range(2)]
        probT = arena[:, 9472:10496].rearrange("p (w g t) -> p w g t", w=2, g=4)
        zs_samp = arena[:, 10988:11500].rearrange("p (k a c) -> p k a c", k=8, a=2)
        prob_s = arena[:, 7424:8512].rearrange("p (b t) -> p b t", b=NB)
        probT_s = arena[:, 8512:9536].rearrange("p (b t) -> p b t", b=NB)
        q_samp = arena[:, 8512:9024].rearrange("p (r b q) -> p r b q", r=2, b=NB)
        probT_n = arena[:, 9536:10560].rearrange("p (b t) -> p b t", b=NB)
        v_new = arena[:, 2304:4352 - 1024].rearrange("p (b d) -> p b d", b=NB)
        s0 = [a.rearrange("p (b d) -> p b d", b=NB) for a in
              (fa[:, 2304:3328], arena[:, 7424:8448], arena[:, 2304:3328], arena[:, 3328:4352])]
        vpx = arena[0:NS, 4352:5376].rearrange("p (b d) -> p b d", b=NB)
        osq_s = arena[0:NS, 10364:11388].rearrange("p (h d) -> p h d", h=H)
        ksqs = arena[:, 11388:11644].rearrange("p (i s t) -> p i s t", i=2, s=2)
        rs_ = arena[0:NS, 11644:11900].rearrange("p (i d) -> p i d", i=2)
        vps = rs_
        kg_s = arena[0:NS, 5376:6400].rearrange("p (h d) -> p h d", h=H)
        o_s = arena[0:NS, 6400:7424].rearrange("p (h d) -> p h d", h=H)
        sq_s = arena[:, 2304:3328].rearrange("p (h t) -> p h t", h=H)
        a1_s = arena[0:NS, 6400:6912].rearrange("p (h t) -> p h t", h=H)
        dec_s, mt_s, gB_s, x_s = (arena[0:NS, 2304 + 512 * i:2816 + 512 * i].rearrange("p (h t) -> p h t", h=H)
                                  for i in range(4))
        mtl_s = [arena[0:NS, 4352 + 512 * i:4864 + 512 * i].rearrange("p (h t) -> p h t", h=H)
                 for i in range(2)]
        attn_s = arena[0:NS, 10364:10876].rearrange("p (h t) -> p h t", h=H)
        xt_s = arena[0:NS, 10876:11388].rearrange("p (h t) -> p h t", h=H)
        vs_s = fa[0:NS, 3328:4352].rearrange("p (h d) -> p h d", h=H)
        za_t = arena[:, 11500:11500 + TOK]
        sqb4 = [arena[:, i * TOK:(i + 1) * TOK] for i in range(4)]
        ab_t = arena[:, 7000:7000 + TOK]
        xm, sp_e, tb, xa = (arena[:, 7680 + 40 * i:7720 + 40 * i].rearrange("p (c k) -> p c k", k=8) for i in range(4))
        gmask = arena[0:NS, 6936:7000].rearrange("p (h b) -> p h b", h=H)
        ab_tok = arena[:, 7600:7680].rearrange("p (c k) -> p c k", k=16)
        sqb = [arena[:, 0:TOK], arena[:, TOK:2 * TOK]]
        res = [arena[:, 2 * TOK:3 * TOK], arena[:, 3 * TOK:4 * TOK]]
        ssq, rstd = arena[:, 4 * TOK:5 * TOK], arena[:, 5 * TOK:6 * TOK]
        rstd_ps = gp[:, 0:2, 0:HALF]
        LIN = CP + SEQ + NB * (CP + NT)
        u_in = [arena[:, 6 * TOK + LIN * i:6 * TOK + LIN * (i + 1)] for i in range(2)]
        o = 6 * TOK + 2 * LIN
        u_p = [u[:, 0:CP + SEQ] for u in u_in]
        u_s = [u[:, CP + SEQ:LIN].rearrange("p (b t) -> p b t", b=NB) for u in u_in]
        c_buf = arena[:, o:o + TOK]
        prod = [arena[:, o + 8 * TOK + i * SEQ:o + 8 * TOK + (i + 1) * SEQ] for i in range(3)]
        pacc = arena[:, o + 8 * TOK + 3 * SEQ:o + 8 * TOK + 4 * SEQ]
        c_odd = arena[:, o + 8 * TOK + 4 * SEQ:o + 8 * TOK + 4 * SEQ + NS]
        tg = [arena[:, 3 * TOK:4 * TOK], arena[:, o + TOK:o + 2 * TOK]]
        csum, mean = ssq, rstd
        ms6, r6, one_col = tiny(6), tiny(6), tiny(1)
        r6_wide = arena[:, 4 * TOK:4 * TOK + 6 * P].rearrange("p (c t) -> p c t", t=P)
        NORM_CHUNKS = [a * HALF + o_ for a in range(2) for o_ in (0, P, HALF - P)]
        zring = [arena[:, o + (2 + i) * TOK:o + (3 + i) * TOK] for i in range(ZRING)]
        assert ZRING * TOK <= 6 * TOK + 2 * SEQ

        def acc_of(s):
            return acc[:, s, :, 0:HALF]

        def per_row(ap, n):
            return ap.unsqueeze(2).to_broadcast([ap.shape[0], ap.shape[1], n])

        def per_group(ap, g):
            return ap.unsqueeze(1).to_broadcast([ap.shape[0], g, ap.shape[1]])

        @block.sync
        def _(sp):
            def weights(n, first=False):
                for half in range(2):
                    if not first:
                        sp.wait_ge(wlo_done, 2 * n + half - 1)
                    sp.dma_start(w_raw[:, half, :], wt[n, :, half * 1024:(half + 1) * 1024]) \
                        .then_inc(raw_in[half], 16)

            for i in range(8):
                if i == 1:
                    sp.dma_start(par[:], param).then_inc(par_in, 16)
                sp.dma_start(full[:, 2 * i:2 * i + 2, :], x[2 * i:2 * i + 2].rearrange("k p t -> p k t")) \
                    .then_inc(x_in[i], 16)
            sp.dma_start(cst[:], const).then_inc(cst_in, 16)
            weights(0, first=True)
            sp.dma_start(dnc[:, :, 1:9, :], dn_prev).then_inc(prev_in, 16)
            with sp.Fori(1, N_Q) as n:
                weights(n)

            def sampled_state(h):
                if h == 0:
                    sp.wait_ge(dve_h.sem, dve_h.at("y", H - 1))
                    sp.wait_ge(state_out, 16 * H)
                    sp.wait_ge(dnc_stored, 16)
                if h == 2:
                    sp.wait_ge(samp_dve, SD["Xt2"])
                if h >= 4:
                    sp.wait_ge(sdn_stored[h % 4], 16)
                sp.dma_start(s0[h % 4], state_in[h].rearrange("p (b d) -> p b d", b=NB)).then_inc(s0_in[h % 4], 16)

            for n, heads in ((0, ()), (1, (0, 1)), (2, (2, 3)), (3, ()), (4, (4, 5, 6, 7))):
                weights(N_Q + n)
                for h in heads:
                    sampled_state(h)
            for n in range(N_Q + 5, N_ZA + 1):
                weights(n)
            for s in sdn_stored:
                sp.wait_ge(s, 16 * (H // 4))
            sp.wait_ge(ys_done, 1)
            sp.dma_start(kc, k_cache.rearrange("r p b t -> p r b t")).then_inc(kc_in, 16)
            sp.dma_start(vc, v_cache.rearrange("p (b d) -> p b d", b=NB)).then_inc(vc_in, 16)
            for n in range(N_ZA + 1, N_OUT0):
                weights(n)

            def out_section(n0, source):
                weights(n0)
                weights(n0 + 1)
                if n0 == N_OUT0:
                    sp.wait_ge(res_free, 1)
                else:
                    sp.wait_ge(acc_free[0], N_VG // 2 + 1 + KT)
                    sp.wait_ge(x1_stored, 16 * KT)
                for j in range(2):
                    sp.dma_start(res[j], source[j]).then_inc(res_in[j], 16)
                with sp.Fori(0, KT // 2 - 1) as i:
                    for j in range(2):
                        weights(2 * i + (n0 + 2 + j))
                        sp.wait_ge(acc_free[1 - j], i + ((n0 + j) // 2 + 1))
                        sp.dma_start(res[j], source[2 * i + 2 + j]).then_inc(res_in[j], 16)

            out_section(N_OUT0, x)
            with sp.Fori(0, KT // 2) as i:
                for b in range(2):
                    weights(4 * i + (N_VG + 2 * b))
                    weights(4 * i + (N_VG + 2 * b + 1))
                    sp.wait_ge(u_free[b], i + 1)
                    sp.dma_start(u_s[b][:, :, 0:CP], cf_prev[2 * i + b]).then_inc(uprev_in[b], 16)
            with sp.Fori(N_Z1, N_OUT1) as n:
                weights(n)
            out_section(N_OUT1, x1_dram)
            for s, v in finals:
                sp.wait_ge(s, v)

        @block.tensor
        def _(pe):
            def proj(m, s, e):
                half = e // 4
                if e % 4 == 0:
                    pe.wait_ge(wlo_done, 4 * m + (2 * s + half + 1))
                if e == 0 and not (isinstance(m, int) and m == 0):
                    pe.wait_ge(acc_free[s], m)
                for k in (2 * e, 2 * e + 1):
                    wk = slice(k * P, (k + 1) * P)
                    for j, (w, a) in enumerate(((w_hi, act_hi), (w_hi, act_lo), (w_lo, act_hi))):
                        for i in range(2):
                            ins = pe.matmul(acc[:, s, i, 0:HALF], w[:, s, wk], a[:, k, i * HALF:(i + 1) * HALF],
                                            start=(k == 0 and j == 0), stop=(k == KT - 1 and j == 2))
                if e % 4 == 3:
                    ins.then_inc(w_used, 1)

            def tile_of(m, s):
                for e in range(8):
                    proj(m, s, e)

            def first_tile(n, turn):
                m, s = n // 2, n % 2
                pe.wait_ge(wlo_done, 4 * m + (2 * s + 2))
                if n:
                    pe.wait_ge(acc_free[s], m)
                order = split_order(turn)
                for step in range(KT + LOW_LAG[turn]):
                    for low, pos in ((False, step), (True, step - LOW_LAG[turn])):
                        if not 0 <= pos < KT:
                            continue
                        k = order[pos]
                        wk = slice(k * P, (k + 1) * P)
                        if low:
                            pe.wait_ge((alo_even, alo_odd)[k % 2], 8 * turn + pos // 2 + 1)
                        else:
                            pe.wait_ge(ahi_done, KT * turn + pos + 1)
                        for j, (w, a) in enumerate([(w_hi, act_lo)] if low else [(w_hi, act_hi), (w_lo, act_hi)]):
                            for i in range(2):
                                ins = pe.matmul(acc[:, s, i, 0:HALF], w[:, s, wk], a[:, k, i * HALF:(i + 1) * HALF],
                                                start=(not low and pos == 0 and j == 0), stop=(low and pos == KT - 1))
                ins.then_inc(w_used, 2)

            def sum_channels(source):
                for i in range(2):
                    ins = pe.matmul(gp[:, i, 0:HALF], ones, source[:, i * HALF:(i + 1) * HALF],
                                    start=True, stop=True)
                ins.then_inc(norm_sum, 1)

            def channel_sums(source, start, stop):
                for c, lo in enumerate(NORM_CHUNKS):
                    ins = pe.matmul(gp[:, 3, c:c + 1], source[:, lo:lo + P], one_col, start=(start and c == 0),
                                    stop=(stop and c == len(NORM_CHUNKS) - 1))
                return ins

            def token_norm(turn, last, count):
                channel_sums(ssq, True, False)
                pe.wait_ge(*count)
                channel_sums(last, False, True).then_inc(norm_sum, 1)
                if turn != 2:
                    spread_roots(turn)

            def spread_roots(turn):
                pe.wait_ge(root_wide, turn + 1)
                for c, lo in enumerate(NORM_CHUNKS):
                    ins = pe.matmul(gp[:, lo // HALF, lo % HALF:lo % HALF + P], r6_wide[:, c, :], ident,
                                    start=True, stop=True)
                ins.then_inc(root_out, 1)

            pe.wait_ge(ones_set, 1)
            pe.wait_ge(sq_used, KT)
            channel_sums(ssq, True, True).then_inc(norm_sum, 1)
            pe.wait_ge(cst_in, 16)
            spread_roots(0)
            first_tile(0, 0)

            def gates_by_token():
                pe.wait_ge(acc_free[0], 1)
                for c in range(NC):
                    pe.transpose(gp[:, 0, 16 * c:16 * c + 16], ab_t[0:16, c * P:(c + 1) * P], ident[0:16, 0:16])
                pe.transpose(gp[0:NS, 0, 64:80], ab_t[0:16, SEQ:SEQ + NS], ident[0:16, 0:16]).then_inc(prep_pe, 1)

            def gate_sums():
                pe.wait_ge(prep, 2)
                gk = gates[:, :, KG, 0:4]
                gks = gates[0:NS, :, KG, 4]
                pe.matmul(gp[:, 1, 80:144], ones[0:NS, :], gmask.rearrange("p h b -> p (h b)"), start=True, stop=True)
                pe.matmul(gp[:, 1, 0:32], tri, gk, start=True, stop=True)
                pe.matmul(gp[:, 1, 32:64], ones, gk, start=True, stop=True)
                pe.matmul(gp[0:NS, 1, 64:72], cst[0:NS, C_TRIS:C_TRIS + NS], gks, start=True, stop=True)
                pe.matmul(gp[0:NS, 1, 72:80], cst[0:NS, C_ONES:C_ONES + NS], gks, start=True,
                          stop=True).then_inc(prep_pe, 1)

            def head_step(it, kb, name):
                kt, qt, vt = kqv[kb][:, 0, :], kqv[kb][:, 1, :], kqv[kb][:, 2, :]
                ck = lambda c: slice(c * P, (c + 1) * P)
                if name == "kv_tok":
                    pe.wait_ge(conv_silu, 3 * it + 3)
                    if not (isinstance(it, int) and it == 0):
                        pe.wait_ge(dve_h.sem, dve_h.at("y", it - 1))
                    else:
                        pe.wait_ge(prep, 4)
                    for c in range(NC):
                        pe.transpose(gp[:, 0, ck(c)], kt[:, ck(c)], ident)
                    for c in range(NC):
                        ins = pe.transpose(gp[:, 1, ck(c)], vt[:, ck(c)], ident)
                elif name == "gcum":
                    pe.wait_ge(pool_h.sem, pool_h.at("gB", it))
                    for c in range(NC):
                        ins = pe.matmul(gp[:, 2, ck(c)], gB[:, c, :], tri, start=True, stop=True)
                elif name == "norm":
                    pe.wait_ge(act_h.sem, act_h.at("sq", it))
                    for c in range(8):
                        ins = pe.matmul(gp[:, 3, c:c + 1], sqkq_c[:, c, :], ones[:, 0:1], start=True, stop=True)
                elif name == "gram":
                    pe.wait_ge(dve_h.sem, dve_h.at("ssum", it))
                    for c in range(NC):
                        ins = pe.matmul(gp[:, 2 + c // 2, (c % 2) * 256:(c % 2) * 256 + 256], kt[:, ck(c)],
                                        kqv[kb][:, 0:2, ck(c)], start=True, stop=True)
                elif name == "m0":
                    pe.wait_ge(pool_h.sem, pool_h.at("L0", it))
                    pe.wait_ge(dve_h.sem, dve_h.at("vs", it))
                    for c in range(NC):
                        ins = pe.transpose(gp[:, 0, ck(c)], mtl[0][:, c, :], ident)
                elif name[0] == "a":
                    l = int(name[1])
                    pe.wait_ge(pool_h.sem, pool_h.at(f"L{l}", it))
                    pe.wait_ge(dve_h.sem, dve_h.at("Xt" if l == 1 else f"X{l - 1}", it))
                    for c in range(NC):
                        ins = pe.matmul(gp[:, 1, ck(c)], mtl[l % 2][:, c, :], xx[:, 0, c, :], start=True, stop=True)
                elif name[0] == "x":
                    l = int(name[1])
                    pe.wait_ge(act_h.sem, act_h.at(f"A{l}", it))
                    if l == 1:
                        pe.wait_ge(dve_h.sem, dve_h.at("attn", it))
                    if l < LEVELS - 1:
                        for c in range(NC):
                            pe.matmul(half_blocks(gp[:, 2, ck(c)], l, 0), xx[:, 1, c, :], half_blocks(a1[:, c, :], l, 0),
                                      start=True, stop=True)
                    for c in range(NC):
                        ins = pe.matmul(half_blocks(gp[:, 3, ck(c)], l, 1), a1[:, c, :],
                                        half_blocks(xx[:, 1, c, :], l, 1), start=True, stop=True)
                elif name == "o_chan":
                    pe.wait_ge(dve_h.sem, dve_h.at("on", it))
                    for c in range(NC):
                        ins = pe.transpose(gp[:, 0, ck(c)], on[:, c, :], ident)
                elif name[0:2] == "so":
                    c = int(name[2])
                    pe.wait_ge(dve_h.sem, dve_h.at(f"vp{c}", it))
                    pe.matmul(gp[:, 3, 0:P], kg[:, c, :], vp, start=True, stop=True)
                    ins = pe.matmul(gp[:, 0, 0:P], attn[:, c, :], vp, start=True, stop=True)
                elif name[0] == "s":
                    c = int(name[1])
                    pe.wait_ge(dve_h.sem, dve_h.at(f"o{c - 1}", it))
                    if c > 1:
                        pe.wait_ge(act_h.sem, act_h.at(f"q{c - 1}", it))
                    pe.matmul(gp[:, 0, 0:P], kt[:, ck(c)], st, start=True, stop=True)
                    ins = pe.matmul(gp[:, 1, 0:P], qt[:, ck(c)], st, start=True, stop=True)
                elif name[0] == "u":
                    c = int(name[1])
                    pe.wait_ge(dve_h.sem, dve_h.at(f"X{LEVELS - 1}" if c == 0 else f"r{c}", it))
                    ins = pe.matmul(gp[:, 2, 0:P], xx[:, 1, c, :], vs[:, 0, :] if c == 0 else rr,
                                    start=True, stop=True)
                ins.then_inc(pe_h.sem, 1)

            def head_unit(hp, it=None, kb=0):
                for ti in range(4):
                    for e in range(8):
                        proj(2 * hp + (1 + ti) // 2, (1 + ti) % 2, e)
                        if 8 * ti + e == 0 and not (isinstance(it, int) and it == 0):
                            head_step(it - 1, 1 - kb, "o_chan")
                        if 8 * ti + e in PE_PLAN:
                            head_step(it, kb, PE_PLAN[8 * ti + e])

            for ti in range(4):
                for e in range(8):
                    proj((1 + ti) // 2, (1 + ti) % 2, e)
                    if (ti, e) == (0, 2):
                        gates_by_token()
                    if (ti, e) == (0, 7):
                        gate_sums()
            head_unit(1, 0, 0)
            with pe.Fori(0, 3) as i:
                head_unit(2 * i + 2, 2 * i + 1, 1)
                head_unit(2 * i + 3, 2 * i + 2, 0)
            head_unit(8, 7, 1)

            def samp_step(name, h=None):
                col = lambda h: slice((h % 4) * P, (h % 4 + 1) * P)
                sc = lambda h: slice(h * NS, (h + 1) * NS)
                if name == "k_tok":
                    pe.wait_ge(dve_h.sem, dve_h.at("y", H - 1))
                    pe.wait_ge(conv_silu, 3 * H)
                    for h in range(H):
                        ins = pe.transpose(gp[0:NS, h // 4, col(h)], samp[:, h, 0, :], ident)
                elif name == "v_tok":
                    pe.wait_ge(samp_dve, SD["kg"])
                    for h in range(H):
                        ins = pe.transpose(gp[0:NS, 2 + h // 4, col(h)], samp[:, h, 2, :], ident)
                elif name == "norm":
                    pe.wait_ge(samp_act, SA["sq"])
                    for h in range(H):
                        for j in range(2):
                            ins = pe.matmul(gp[0:NS, 0, 2 * h + j:2 * h + j + 1], sq_s[:, h, j * NS:(j + 1) * NS],
                                            ones[:, 0:1], start=True, stop=True)
                elif name == "gram":
                    pe.wait_ge(samp_dve, SD["ssum"])
                    for h in range(H):
                        ins = pe.matmul(gp[0:NS, h // 4, col(h)], samp[:, h, 0, :], samp[:, h, 0:2, :],
                                        start=True, stop=True)
                elif name == "gcum":
                    pe.wait_ge(samp_dve, SD["vs"])
                    pe.wait_ge(samp_pool, SP_["gB"])
                    for h in range(H):
                        ins = pe.matmul(gp[0:NS, 2, sc(h)], gB_s[:, h, :], cst[0:NS, C_TRIS:C_TRIS + NS],
                                        start=True, stop=True)
                elif name == "m0":
                    pe.wait_ge(samp_pool, SP_["L0"])
                    for h in range(H):
                        ins = pe.transpose(gp[0:NS, 2, sc(h)], mtl_s[0][:, h, :], ident[0:NS, 0:NS])
                elif name in ("a1", "a2"):
                    l = int(name[1])
                    pe.wait_ge(samp_pool, SP_[f"L{l}"])
                    pe.wait_ge(samp_dve, SD["Xt"] if l == 1 else SD["Xt1"])
                    for h in range(H):
                        ins = pe.matmul(gp[0:NS, 3, sc(h)], mtl_s[l % 2][:, h, :], x_s[:, h, :], start=True, stop=True)
                elif name in ("x1", "x2"):
                    l = int(name[1])
                    pe.wait_ge(samp_act, SA[f"A{l}"])
                    if l == 1:
                        for h in range(H):
                            pe.matmul(gp[0:NS, 2, sc(h)], xt_s[:, h, :], a1_s[:, h, :], start=True, stop=True)
                    for h in range(H):
                        ins = pe.matmul(gp[0:NS, 0, sc(h)], a1_s[:, h, :], xt_s[:, h, :], start=True, stop=True)
                elif name == "st":
                    g = h
                    pe.wait_ge(samp_dve, SD["Xt2"] if g == 0 else SD[f"vp{g - 1}"])
                    for i in range(2):
                        h = 2 * g + i
                        pe.wait_ge(s0_in[h % 4], 16 * (h // 4 + 1))
                        dst = gp[:, 2, i * P:(i + 1) * P].rearrange("p (s t) -> p s t", s=2)
                        for b in range(NB):
                            ins = pe.matmul(dst[:, :, b * NT:(b + 1) * NT], s0[h % 4][:, b, :],
                                            samp[:, h, 0:2, b * NT:(b + 1) * NT], start=True, stop=True)
                elif name == "tr":
                    pe.wait_ge(samp_act, SA[f"ks{h}"])
                    if h:
                        pe.wait_ge(samp_dve, SD[f"S{2 * h - 1}"])
                    for s_, bank in ((0, 3), (1, 1)):
                        for i in range(2):
                            ins = pe.transpose(gp[0:NS, bank, i * P:(i + 1) * P], ksqs[:, i, s_, :], ident)
                elif name == "u":
                    pe.wait_ge(samp_dve, SD[f"r{h}"])
                    for i in range(2):
                        ins = pe.matmul(gp[0:NS, 2, i * P:(i + 1) * P], xt_s[:, 2 * h + i, :], rs_[:, i, :],
                                        start=True, stop=True)
                elif name == "o":
                    pe.wait_ge(samp_dve, SD[f"vp{h}"])
                    for i in range(2):
                        ins = pe.matmul(gp[0:NS, 3, i * P:(i + 1) * P], attn_s[:, 2 * h + i, :], vps[:, i, :],
                                        start=True, stop=True)
                elif name == "ns":
                    pe.wait_ge(samp_pool, SP_[f"vx{h}"])
                    pe.wait_ge(samp_act, SA[f"q{h // 2}"])
                    if h % 2:
                        pe.wait_ge(samp_dve, SD[f"S{h - 1}"])
                    for i in range(2):
                        ins = pe.matmul(gp[:, i, :], kg_s[:, h, :], vpx[:, 4 * i:4 * i + 4, :], start=True, stop=True)
                elif name == "o_chan":
                    pe.wait_ge(samp_dve, SD["on"])
                    for h in range(H):
                        ins = pe.transpose(gp[:, 2, sc(h)], o_s[:, h, :], ident[0:NS, 0:NS])
                ins.then_inc(samp_pe, 1)

            def values_by_token():
                pe.wait_ge(ys_done, 1)
                for r in range(2):
                    for c in range(NC):
                        ins = pe.transpose(gp[:, r, c * P:(c + 1) * P], kv[:, 2 * r + 1, blk(c):blk(c) + P], ident)
                ins.then_inc(vtok_pe, 1)

            def att_scores(u):
                r, c, jj = u // 8, (u // 2) % 4, u % 2
                n = N_Q + 4 * r + 3
                pe.wait_ge(acc_free[n % 2], n // 2 + 1)
                if u == 0:
                    pe.wait_ge(vtok_done, 1)
                else:
                    pe.wait_ge(biased, u)
                for q in range(2):
                    rows = slice(64 * q, 64 * q + 64)
                    for j in range(2):
                        lhs = full[rows, 4 * r + 2 * jj + j, blk(c):blk(c) + P]
                        for w in range(0 if c else 1, 2):
                            ins = pe.matmul(gp[:, q, j * 256 + w * P:j * 256 + (w + 1) * P], lhs,
                                            kv[rows, 2 * r, blk(c - 1 + w):blk(c - 1 + w) + P],
                                            start=True, stop=True)
                ins.then_inc(scores, 1)

            def att_turn(u):
                c = (u // 2) % 4
                pe.wait_ge(probs, u + 1)
                if u:
                    pe.wait_ge(attn_out, u)
                for w in range(0 if c else 1, 2):
                    for g in range(4):
                        ins = pe.transpose(gp[:, 2 + w, g * P:(g + 1) * P], prob[u % 2][:, g, w * P:(w + 1) * P], ident)
                ins.then_inc(turned, 1)

            def att_weigh(u):
                r, c = u // 8, (u // 2) % 4
                pe.wait_ge(turned_out, u + 1)
                for q in range(2):
                    for w in range(0 if c else 1, 2):
                        ins = pe.matmul(gp[64 * q:64 * q + 64, 2, 0:256], v_tok[:, c - 1 + w, r, 64 * q:64 * q + 64],
                                        probT[:, w, 2 * q:2 * q + 2, :], start=(w == (0 if c else 1)), stop=(w == 1))
                ins.then_inc(weighed, 1)

            def sampled_attention(name):
                if name == "scores":
                    pe.wait_ge(kc_in, 16)
                    pe.wait_ge(biased, 16)
                    pe.wait_ge(attn_out, 16)
                    pe.wait_ge(q_samp_put, 4)
                    for b in range(NB):
                        sc = (b // 4) * HALF + HP + (b % 4) * NT
                        for g in range(4):
                            rows = slice(64 * (g % 2), 64 * (g % 2) + 64)
                            lhs = q_samp[rows, g // 2, b, :]
                            o_ = gp[32 * g:32 * g + 32, b // 3, (b % 3) * 136:(b % 3) * 136 + 136]
                            pe.matmul(o_[:, 0:W], lhs, kc[rows, g // 2, b, :], start=True, stop=True)
                            ins = pe.matmul(o_[:, W:W + NT], lhs, kv[rows, 2 * (g // 2), sc:sc + NT],
                                            start=True, stop=True)
                elif name == "turn":
                    pe.wait_ge(sa_dve, SAD["prob"])
                    for b in range(NB):
                        ins = pe.transpose(gp[:, b // 4, (b % 4) * P:(b % 4 + 1) * P], prob_s[:, b, 0:W], ident)
                elif name == "turn_new":
                    for b in range(NB):
                        ins = pe.transpose(gp[0:NT, 2 + b // 4, (b % 4) * P:(b % 4 + 1) * P], prob_s[:, b, W:W + NT],
                                           ident)
                elif name[0:5] == "v_new":
                    r = int(name[5])
                    pe.wait_ge(sa_act if r == 0 else sa_dve, SAA["turned"] if r == 0 else SAD["out0"])
                    if r == 0:
                        pe.wait_ge(sa_dve, SAD["turned_new"])
                    for b in range(NB):
                        sc = (b // 4) * HALF + HP + (b % 4) * NT
                        ins = pe.transpose(gp[0:NT, b // 4, (b % 4) * P:(b % 4 + 1) * P],
                                           kv[:, 2 * r + 1, sc:sc + NT], ident)
                elif name[0:5] == "weigh":
                    r = int(name[5])
                    pe.wait_ge(sa_act, SAA[f"v_new{r}"])
                    pe.wait_ge(vc_in, 16)
                    for q in range(2):
                        g = 2 * r + q
                        for b in range(NB):
                            o_ = gp[64 * q:64 * q + 64, 2, 0:256].rearrange("p (j b t) -> p b j t", j=4, b=NB)[:, b]
                            pe.matmul(o_, vc[:, b, 64 * g:64 * g + 64], probT_s[:, b, 32 * g:32 * g + 32],
                                      start=True, stop=False)
                            ins = pe.matmul(o_, v_new[0:NT, b, 64 * q:64 * q + 64],
                                            probT_n[0:NT, b, 32 * g:32 * g + 32], start=False, stop=True)
                ins.then_inc(sa_pe, 1)

            def attention_unit(u, phase):
                if phase == 0:
                    att_scores(u)
                    if u:
                        att_turn(u - 1)
                if phase == 2 and u:
                    att_weigh(u - 1)

            for t in range(16):
                n = N_Q + t
                for e in range(8):
                    slot = 8 * t + e
                    proj(n // 2, n % 2, e)
                    if slot == 0:
                        head_step(H - 1, 1, "o_chan")
                    if slot < ATT0 - 1:
                        for name, h in SAMP_PLAN[slot]:
                            samp_step(name, h)
                    elif slot < ATT0:
                        values_by_token()
                    elif slot <= SATT0:
                        attention_unit((slot - ATT0) // 3, (slot - ATT0) % 3)
                    elif slot - SATT0 in SATT_PLAN:
                        name = SATT_PLAN[slot - SATT0]
                        if name == "last_turn":
                            att_turn(15)
                        elif name == "last":
                            att_weigh(15)
                        else:
                            sampled_attention(name)
            def out_section(n0, turn):
                first_tile(n0, turn)
                assert n0 % 2 == 1
                with pe.Fori(0, KT // 2 - 1) as i:
                    tile_of(i + (n0 + 1) // 2, 0)
                    tile_of(i + (n0 + 1) // 2, 1)
                tile_of((n0 + KT - 1) // 2, 0)
                pe.wait_ge(sq_summed, KT - 1 if turn == 1 else 2 * (KT - 1))
                token_norm(turn, sqb[1], (sq_done, 2 * KT if turn == 1 else 3 * KT))

            out_section(N_OUT0, 1)
            first_tile(N_VG, 2)
            tile_of((N_VG + 1) // 2, (N_VG + 1) % 2)
            with pe.Fori(0, KT - 1) as i:
                tile_of(i + (N_VG + 2) // 2, (N_VG + 2) % 2)
                tile_of(i + (N_VG + 3) // 2, (N_VG + 3) % 2)

            def z_tiles(first, last):
                for n in range(N_Z1 + first, N_Z1 + last):
                    tile_of(n // 2, n % 2)

            z_tiles(0, 3)
            pe.wait_ge(c_summed, KT)
            sum_channels(csum)
            z_tiles(3, 6)
            pe.wait_ge(c_summed, 2 * KT - 1)
            token_norm(2, sqb[1], (ln_sq, KT))
            tile_of((N_Z1 + 6) // 2, (N_Z1 + 6) % 2)
            spread_roots(2)
            with pe.Fori((N_Z1 + 7) // 2, N_OUT1 // 2) as i:
                tile_of(i, 0)
                tile_of(i, 1)
            tile_of(N_OUT1 // 2, 0)
            out_section(N_OUT1, 3)

        @block.scalar
        def _(act):
            def copy(out, in_, scale=1.0):
                return act.activation(out, in_, ACT.Copy, scale=scale)

            def split_hi(m, s, half):
                act.wait_ge(raw_in[half], 32 * m + (16 * s + 16))
                if not (isinstance(m, int) and m == 0):
                    act.wait_ge(w_used, 4 * m + (2 * s - 3 + half))
                hs_ = slice(half * 1024, (half + 1) * 1024)
                copy(w_hi[:, s, hs_], w_raw[:, half, :]).then_inc(whi_done, 1)

            def next_split(m, s, e):
                if e in (0, 4):
                    split_hi(m + s, 1 - s, e // 4)

            def tile_done(m, s):
                act.wait_ge(w_used, 4 * m + (2 * s + 2))

            def act_split(turn, first=0, last=KT):
                for k in split_order(turn)[first:last]:
                    if turn in (0, 2):
                        act.wait_ge(scaled, 8 * turn + k + 1)
                    if turn == 3:
                        act.wait_ge(y_done, k + 1)
                    copy(act_hi[:, k, :], full[:, k, :]).then_inc(ahi_done, 1)

            for k in range(KT):
                act.wait_ge(x_in[k // 2], 16)
                if k >= 4:
                    act.wait_ge(sq_used, k - 3)
                act.activation(sqb4[k % 4], full[:, k, :], ACT.Square).then_inc(sq_done, 1)
            split_hi(0, 0, 0)
            split_hi(0, 0, 1)
            split_hi(0, 1, 0)
            act_split(0)
            split_hi(0, 1, 1)

            def head_act(it, kb, name):
                if name == "sq":
                    act.wait_ge(conv_silu, 3 * it + 3)
                    if not (isinstance(it, int) and it == 0):
                        act.wait_ge(pe_h.sem, pe_h.at("o_chan", it - 1))
                    ins = act.activation(sqkq, kqv[kb][:, 0:2, :], ACT.Square)
                elif name == "decay":
                    act.wait_ge(dve_h.sem, dve_h.at("dmask", it))
                    for c in range(NC):
                        ins = act.activation(dec[:, c, :], dec[:, c, :], ACT.Exp, bias=hs[:, KNG, c:c + 1])
                elif name[0] == "A":
                    act.wait_ge(pe_h.sem, pe_h.at(f"a{name[1]}", it))
                    ins = copy(a1, bank4(1))
                elif name[0] == "q":
                    c = int(name[1])
                    act.wait_ge(pe_h.sem, pe_h.at(f"s{c}", it))
                    ins = copy(qs, gp[:, 1, 0:P], hs[:, KEG, c:c + 1])
                elif name == "osq":
                    act.wait_ge(dve_h.sem, dve_h.at("o3", it))
                    for c in range(NC):
                        ins = act.activation(a1[:, c, :], o_tok[:, c, :], ACT.Square, accum_out=osum[:, c:c + 1])
                ins.then_inc(act_h.sem, 1)

            def evacuate_qkv(hp, j):
                m, s = 2 * hp + (1 + j) // 2, (1 + j) % 2
                tile_done(m, s)
                if not (isinstance(hp, int) and hp == 0 and j == 0):
                    act.wait_ge(conv_done, 3 * hp + j)
                    act.wait_ge(last_taken, 3 * hp + j)
                copy(halves(cin_p[:, 3:3 + SEQ]), acc[:, s, :, 0:HP])
                copy(cin_s[:, :, 3:3 + NT].rearrange("p (a b) t -> p a b t", a=2),
                     acc[:, s, :, HP:HALF].rearrange("p a (b t) -> p a b t", t=NT)).then_inc(acc_free[s], 1)

            def conv_tanh_(hp, j):
                act.wait_ge(conv_done, 3 * hp + (j + 1))
                act.activation(conv_t, conv_y, ACT.Tanh).then_inc(conv_tanh, 1)

            def z_gate(hp):
                tile_done(2 * hp + 2, 0)
                act.wait_ge(conv_silu, 3 * hp + 3)
                act.activation(halves(conv_t), acc_of(0), ACT.Tanh, scale=0.5).then_inc(z_tanh, 1)

            def head_unit(hp, it=None, kb=0, convs=True):
                for ti in range(4):
                    for e in range(8):
                        next_split(2 * hp + (1 + ti) // 2, (1 + ti) % 2, e)
                        if it is not None:
                            for name in ACT_PLAN.get(8 * ti + e, ()):
                                head_act(it, kb, name)
                        if e == 1 and ti == 0 and it is not None:
                            z_gate(hp - 1)
                        if convs and ti and e == 1:
                            evacuate_qkv(hp, ti - 1)
                        if convs and ti and e == 6:
                            conv_tanh_(hp, ti - 1)
                        if not convs and ti and e == 1:
                            evacuate_kv(ti - 1)

            def evacuate_kv(j):
                tile_done((N_KV + j) // 2, (N_KV + j) % 2)
                if j == 0:
                    act.wait_ge(conv_silu, 3 * H)
                    act.wait_ge(acc_free[0], 2 * H + 1)
                    act.wait_ge(last_taken, 3 * H)
                    act.wait_ge(pe_h.sem, pe_h.at("o_chan", H - 2))
                copy(halves(kv[:, j, :]), acc_of((N_KV + j) % 2)).then_inc(acc_free[(N_KV + j) % 2], 1)

            for ti in range(4):
                for e in range(8):
                    next_split((1 + ti) // 2, (1 + ti) % 2, e)
                    if ti == 0 and e == 1:
                        tile_done(0, 0)
                        copy(halves(ab_t[0:16, 0:SEQ]), acc[0:16, 0, :, 0:HP])
                        copy(halves(ab_t[0:16, SEQ:TOK]), acc[0:16, 0, :, HP:HALF]).then_inc(acc_free[0], 1)
                    if ti == 0 and e == 4:
                        act.wait_ge(prep, 1)
                        act.activation(sp_e, xm, ACT.Exp).then_inc(act_t.sem, 1)
                        act.activation(tb, ab_tok[:, :, 8:16], ACT.Tanh, scale=0.5)
                        act.activation(ea, par[:, P_ALOG:P_ALOG + 8], ACT.Exp)
                        act.wait_ge(act_t.sem, 1)
                        act.activation(sp_e, sp_e, ACT.Ln, bias=1.0).then_inc(prep_act, 1)
                    if ti == 1 and e == 2:
                        act.wait_ge(prep, 3)
                        act.activation(egl_s, egl_s, ACT.Exp)
                        act.activation(gates[:, :, KEG, :], gates[:, :, KEG, :], ACT.Exp)
                        act.activation(gates[:, :, KEK:KEL + 1, :], gates[:, :, KEK:KEL + 1, :], ACT.Exp) \
                           .then_inc(prep_act, 1)
                    if ti and e == 1:
                        evacuate_qkv(0, ti - 1)
                    if ti and e == 6:
                        conv_tanh_(0, ti - 1)
            head_unit(1, 0, 0)
            with act.Fori(0, 3) as i:
                head_unit(2 * i + 2, 2 * i + 1, 1)
                head_unit(2 * i + 3, 2 * i + 2, 0)
            head_unit(8, 7, 1, convs=False)

            def query(j):
                tile_done((N_Q + j) // 2, (N_Q + j) % 2)
                if j == 4:
                    for h in (4, 5):
                        act.wait_ge(sdn_stored[h % 4], 32)
                if j == 0:
                    act.wait_ge(dve_h.sem, dve_h.at("y", H - 1))
                copy(full[:, j, :].rearrange("p (a c) -> p a c", a=2), acc_of((N_Q + j) % 2)) \
                    .then_inc(acc_free[(N_Q + j) % 2], 1)

            def samp_act_step(name):
                if name == "sq":
                    act.wait_ge(samp_dve, SD["kg"])
                    ins = act.activation(sq_s, samp[:, :, 0:2, :].rearrange("p h s t -> p h (s t)"), ACT.Square)
                elif name == "decay":
                    act.wait_ge(samp_dve, SD["dmask2"])
                    ins = act.activation(dec_s, dec_s, ACT.Exp)
                elif name in ("A1", "A2"):
                    act.wait_ge(samp_pe, SPE[f"a{name[1]}"])
                    act.wait_ge(state_out, 16 * H)
                    ins = copy(a1_s, gp[0:NS, 3, :].rearrange("p (h t) -> p h t", h=H))
                elif name[0:2] == "ks":
                    g = int(name[2:])
                    act.wait_ge(samp_pe, SPE[f"st{g}"])
                    ins = copy(ksqs, gp[:, 2, 0:2 * P].rearrange("p (i s t) -> p i s t", i=2, s=2))
                elif name[0] == "q":
                    g = int(name[1:])
                    act.wait_ge(samp_pe, SPE[f"tr{g}"])
                    for i in range(2):
                        ins = copy(o_s[:, 2 * g + i, :], gp[0:NS, 1, i * P:(i + 1) * P],
                                   gates[0:NS, 2 * g + i, KEG, 4:5])
                elif name == "osq":
                    act.wait_ge(samp_dve, SD[f"o{H // 2 - 1}"])
                    act.wait_ge(samp_pe, SPE[f"o{H // 2 - 1}"])
                    for h in range(H):
                        ins = act.activation(osq_s[:, h, :], o_s[:, h, :], ACT.Square,
                                             accum_out=sos[:, h:h + 1])
                ins.then_inc(samp_act, 1)

            def att_exp(u):
                c = (u // 2) % 4
                lo = 0 if c else P
                act.wait_ge(biased, u + 1)
                pr = prob[u % 2]
                for g in range(4):
                    act.activation(pr[:, g, lo:], pr[:, g, lo:], ACT.Exp, bias=nmax[u % 2][:, g:g + 1],
                                   accum_out=esum[u % 2][:, g:g + 1])
                act.activation(esink[u % 2], dsink[u % 2], ACT.Exp).then_inc(exped, 1)

            def att_out(u):
                r, c, jj = u // 8, (u // 2) % 4, u % 2
                act.wait_ge(weighed, u + 1)
                copy(full[:, 4 * r + 2 * jj:4 * r + 2 * jj + 2, blk(c):blk(c) + P],
                     gp[:, 2, 0:256].rearrange("p (j t) -> p j t", j=2)).then_inc(attn_out, 1)

            def att_turn_out(u):
                act.wait_ge(turned, u + 1)
                if u:
                    act.wait_ge(weighed, u)
                for w in range(0 if (u // 2) % 4 else 1, 2):
                    ins = copy(probT[:, w, :, :], bank4(2 + w))
                ins.then_inc(turned_out, 1)

            def copy_values():
                act.wait_ge(ys_done, 1)
                for s in sdn_stored:
                    act.wait_ge(s, 16 * (H // 4))
                act.wait_ge(vtok_pe, 1)
                copy(v_tok.rearrange("p c r d -> p r c d"), bank4(0, 2).rearrange("p (r c) d -> p r c d", r=2)) \
                    .then_inc(vtok_done, 1)

            for t in range(16):
                n = N_Q + t
                for e in range(8):
                    slot = 8 * t + e
                    next_split(n // 2, n % 2, e)
                    if slot == ATT0 - 1:
                        copy_values()
                    if slot == 1:
                        act.wait_ge(w_used, 2 * N_Q)
                        copy(halves(kv[:, 3, :]), acc_of(0)).then_inc(acc_free[0], 1)
                    elif e == 1 and t <= 8:
                        query(t - 1)
                    for name in SAMP_ACT.get(slot, ()):
                        samp_act_step(name)
                    if e == 4 and t > 8:
                        tile_done((n - 1) // 2, (n - 1) % 2)
                        if t > 9:
                            act.wait_ge(acc_free[n % 2], (n - 2) // 2 + 1)
                        act.activation(halves(za_t), acc_of((n - 1) % 2), ACT.Tanh, scale=0.5).then_inc(z_tanh, 1)
                    if ATT0 <= slot <= SATT0:
                        u = (slot - ATT0) // 3
                        if (slot - ATT0) % 3 == 1:
                            if u:
                                att_turn_out(u - 1)
                            att_exp(u)
                        if (slot - ATT0) % 3 == 2 and u:
                            att_out(u - 1)
                    else:
                        for name in SATT_ACT.get(slot - SATT0, ()):
                            if name == "last":
                                att_turn_out(15)
                            elif name == "last_out":
                                att_out(15)
                            elif name == "exp":
                                act.wait_ge(sa_dve, SAD["sub"])
                                for b in range(NB):
                                    act.activation(prob_s[:, b, :], prob_s[:, b, :], ACT.Exp,
                                                   bias=nmax_s[:, b:b + 1], accum_out=esum_s[:, b:b + 1])
                                act.activation(dsink_s, dsink_s, ACT.Exp).then_inc(sa_act, 1)
                            elif name == "turned":
                                act.wait_ge(sa_pe, SAP["turn"])
                                copy(probT_s, bank4(0, 2)).then_inc(sa_act, 1)
                            elif name[0:5] == "v_new":
                                act.wait_ge(sa_pe, SAP[name])
                                if name == "v_new0":
                                    act.wait_ge(out_small, 16 * n_small)
                                if name == "v_new1":
                                    act.wait_ge(sa_pe, SAP["weigh0"])
                                    act.wait_ge(vnew_stored, 16)
                                copy(v_new[0:NT], gp[0:NT, 0:2, :].rearrange("p k (b d) -> p (k b) d", d=P)) \
                                    .then_inc(sa_act, 1)

            n = N_OUT0 - 1
            tile_done(n // 2, n % 2)
            act.wait_ge(acc_free[1 - n % 2], (n - 1) // 2 + 1)
            act.activation(halves(za_t), acc_of(n % 2), ACT.Tanh, scale=0.5).then_inc(z_tanh, 1)

            def out_section(n0, turn):
                def post(j, jp, first=False):
                    if isinstance(j, int):
                        act.wait_ge(acc_free[(n0 + j) % 2], (n0 + j) // 2 + 1)
                    if not first:
                        act.wait_ge(sq_summed, (0 if turn == 1 else KT - 1) + j - 1)
                    act.activation(sqb[jp], full[:, j, :], ACT.Square).then_inc(sq_done, 1)
                    if turn == 1:
                        act.dma_start(x1_dram[j], full[:, j, :]).then_inc(x1_stored, 16)

                if turn == 1:
                    act.wait_ge(w_used, 2 * n0)
                    act_split(turn, 0, 8)
                    act.wait_ge(gated, 1)
                act_split(turn, 8)
                split_hi((n0 + 1) // 2, (n0 + 1) % 2, 0)
                split_hi((n0 + 1) // 2, (n0 + 1) % 2, 1)
                for j in (1, 2):
                    n = n0 + j
                    split_hi((n + 1) // 2, (n + 1) % 2, 0)
                    split_hi((n + 1) // 2, (n + 1) % 2, 1)
                    post(j - 1, (j - 1) % 2, first=True)
                with act.Fori(0, KT // 2 - 2) as i:
                    for b in range(2):
                        n = n0 + 3 + b
                        for half in range(2):
                            split_hi(i + (n + 1) // 2, (n + 1) % 2, half)
                        act.wait_ge(acc_free[1 - b], i + ((n0 + 2 + b) // 2 + 1))
                        post(2 * i + 2 + b, b)
                n = n0 + KT - 1
                if n + 1 < N_TILES:
                    split_hi((n + 1) // 2, (n + 1) % 2, 0)
                    split_hi((n + 1) // 2, (n + 1) % 2, 1)
                post(KT - 2, 0)
                post(KT - 1, 1)

            out_section(N_OUT0, 1)
            act_split(2)
            split_hi((N_VG + 1) // 2, (N_VG + 1) % 2, 0)
            split_hi((N_VG + 1) // 2, (N_VG + 1) % 2, 1)

            def gate(m, s, j, b, first=False):
                act.wait_ge(w_used, 4 * m + (2 * s + 2))
                if not first:
                    act.wait_ge(acc_free[0], j + N_VG // 2)
                act.activation(halves(tg[b]), acc_of(s), ACT.Sigmoid).then_inc(acc_free[1], 1)

            def taps(j, b, part):
                act.wait_ge(acc_free[0], j + (N_VG // 2 + 2))
                for i in (range(0, 8) if part == 0 else range(8, POOL_TAPS)):
                    tap = DVE_TAPS + i
                    act.wait_ge(tap_sum, j * POOL_SUMS + (i // 2 if i < 3 else 1 + max(i - 3, 1)))
                    copy(prod[i % 3], u_p[b][:, tap:tap + SEQ],
                         cfw[:, j, tap:tap + 1]).then_inc(tap_prod, 1)

            n = N_VG
            for half in range(2):
                split_hi((n + 2) // 2, 1, half)
            gate(n // 2, 1, 0, 0, first=True)
            with act.Fori(0, KT // 2 - 1) as i:
                for b in (1, 0):
                    m = 2 * i + (n + 2) // 2 + (1 - b)
                    j = 2 * i + (2 - b)
                    for half in range(2):
                        split_hi(m + 1, 0, half)
                    taps(j - 1, 1 - b, 0)
                    for half in range(2):
                        split_hi(m + 1, 1, half)
                    gate(m, 1, j, b)
                    taps(j - 1, 1 - b, 1)
            m = (n + 2 * (KT - 1)) // 2
            for half in range(2):
                split_hi(m + 1, 0, half)
            taps(KT - 2, 0, 0)
            for half in range(2):
                split_hi(m + 1, 1, half)
            gate(m, 1, KT - 1, 1)
            taps(KT - 2, 0, 1)

            def z_tanh_(j):
                act.wait_ge(w_used, 2 * (N_Z1 + j + 1))
                if j >= ZRING:
                    act.wait_ge(y_done, j - ZRING + 1)
                act.activation(halves(zring[j % ZRING]), acc_of((N_Z1 + j) % 2), ACT.Tanh, scale=0.5) \
                    .then_inc(zz_tanh, 1)

            def affine(k):
                act.wait_ge(ln_scaled, k + 1)
                act.activation(full[:, k, :], full[:, k, :], ACT.Identity, scale=lg[:, k:k + 1],
                               bias=lb[:, k:k + 1]).then_inc(ln_aff, 1)
                act.wait_ge(ln_aff, k + 1)
                if k >= 2:
                    act.wait_ge(y_done, k - 1)
                act.activation(sqb[k % 2], full[:, k, :], ACT.Tanh).then_inc(ln_tanh, 1)

            for t in range(KT + 1):
                n = N_Z1 + t
                if t < KT:
                    split_hi((n + 1) // 2, (n + 1) % 2, 0)
                    split_hi((n + 1) // 2, (n + 1) % 2, 1)
                if t == 0:
                    taps(KT - 1, 1, 0)
                    taps(KT - 1, 1, 1)
                if 0 < t < KT:
                    z_tanh_(t - 1)
                for k in LN_SQ.get(t, ()):
                    act.wait_ge(centred, k + 1)
                    if k >= 2:
                        act.wait_ge(c_summed, KT + k - 1)
                    act.activation(sqb[k % 2], full[:, k, :], ACT.Square).then_inc(ln_sq, 1)
                if t == KT:
                    act.wait_ge(w_used, 2 * N_OUT1)
                    act_split(3, 0, 6)
                    z_tanh_(t - 1)
                    act_split(3, 6, 8)
                for k in LN_Y.get(t, ()):
                    affine(k)
            out_section(N_OUT1, 3)
            for k in range(KT):
                act.wait_ge(scaled, 2 * KT + k + 1)
                act.dma_start(y[k], full[:, k, :]).then_inc(fin_stored, 16)
            act.wait_ge(fin_stored, 16 * KT)

        @block.vector
        def _(dve):
            def order(ins):
                dve_t.inc(ins)

            def fence():
                dve.wait_ge(dve_t.sem, dve_t.now())

            def tt(out, a, b, op):
                return dve.tensor_tensor(out, a, b, op)

            def stt(out, a, scalar, b, op0, op1):
                return dve.scalar_tensor_tensor(out=out, in0=a, scalar=scalar, in1=b, op0=op0, op1=op1)

            def ts(out, a, s0_, s1_=None, op0=ALU.mult, op1=None):
                if s1_ is None:
                    return dve.tensor_scalar(out, a, s0_, None, op0)
                return dve.tensor_scalar(out, a, s0_, s1_, op0, op1)

            ADD, SUB, MUL = ALU.add, ALU.subtract, ALU.mult

            def split_lo(m, s, half):
                dve.wait_ge(whi_done, 4 * m + (2 * s + half + 1))
                hs_ = slice(half * 1024, (half + 1) * 1024)
                tt(w_lo[:, s, hs_], w_raw[:, half, :], w_hi[:, s, hs_].bitcast(F32), SUB).then_inc(wlo_done, 1)

            def next_split(m, s, e):
                if e in (0, 4):
                    split_lo(m + s, 1 - s, e // 4)

            def act_lo_even(turn, k):
                dve.wait_ge(ahi_done, KT * turn + split_order(turn).index(k) + 1)
                tt(act_lo[:, k, :], full[:, k, :], act_hi[:, k, :].bitcast(F32), SUB).then_inc(alo_even, 1)

            def token_norm(turn, sums):
                dve.wait_ge(norm_sum, sums)
                ts(ms6, gp[:, 3, 0:6], 1.0 / D, EPS, MUL, ADD).then_inc(var_ready, 1)
                if turn == 0:
                    split_lo(0, 0, 0)
                dve.wait_ge(root, turn + 1)
                dve.tensor_copy(r6_wide, per_row(r6, P)).then_inc(root_wide, 1)
                if turn == 0:
                    split_lo(0, 0, 1)
                if turn != 2:
                    dve.wait_ge(root_out, turn + 1)

            def scale_and_split(turn, gain, sems_before=()):
                for s_, v_ in sems_before:
                    dve.wait_ge(s_, v_)
                for k in range(KT):
                    stt(halves(full[:, k, :]), halves(full[:, k, :]), par[:, gain + k:gain + k + 1], rstd_ps, MUL, MUL) \
                        .then_inc(scaled, 1)
                    if k >= 2 and k % 2 == 0:
                        act_lo_even(turn, k - 2)
                act_lo_even(turn, KT - 2)

            dve.wait_ge(par_in, 16)
            ts(par[:, P_DNW:P_DNW + 96], par[:, P_DNW:P_DNW + 96], 0.5)
            ts(dng, par[:, P_DNG:P_DNG + 1], 0.5 * P ** 0.5)
            ts(lg, par[:, P_LNG:P_LNG + KT], 0.5)
            ts(lb, par[:, P_LNB:P_LNB + KT], 0.5).then_inc(halved, 1)
            for k in range(KT):
                dve.wait_ge(sq_done, k + 1)
                if k == 0:
                    dve.tensor_copy(ssq, sqb4[0]).then_inc(sq_used, 1)
                else:
                    dve.wait_ge(sq_used, k)
                    tt(ssq, ssq, sqb4[k % 4], ADD).then_inc(sq_used, 1)
            token_norm(0, 1)
            scale_and_split(0, P_G0)
            split_lo(0, 1, 0)
            split_lo(0, 1, 1)

            chan = lambda k: gates[:, :, k, :].rearrange("p h c -> p c h")

            def gate_inputs():
                order(dve.memset(gates, 0.0))
                order(dve.memset(ab_tok, 0.0))
                fence()
                dve.wait_ge(prep_pe, 1)
                dve.tensor_copy(ab_tok[:, 0:4, :], gp[:, 0, 0:64].rearrange("p (c k) -> p c k", k=16))
                order(dve.tensor_copy(ab_tok[0:NS, 4, :], gp[0:NS, 0, 64:80]))
                fence()
                order(tt(xa, ab_tok[:, :, 0:8], per_group(par[:, P_DTB:P_DTB + 8], 5), ADD))
                fence()
                stt(xm, xa, -1.0, xa, MUL, ALU.min).then_inc(prep, 1)

            def gate_scalars():
                dve.wait_ge(prep_act, 1)
                order(stt(xa, xa, 0.0, sp_e, ALU.max, ADD))
                fence()
                stt(chan(KG), xa, -1.0, per_group(ea, 5), MUL, MUL)
                order(ts(chan(KBETA), tb, 0.5, 0.5, MUL, ADD))
                fence()
                tt(gmask, gates[0:NS, :, KG, 4].unsqueeze(2).to_broadcast([NS, H, NB]),
                   per_group(cst[0:NS, C_SEQ:C_SEQ + NB], H), MUL).then_inc(prep, 1)

            def gate_factors():
                dve.wait_ge(prep_pe, 2)
                gch = lambda lo: gp[:, 1, lo:lo + 32].rearrange("p (h c) -> p h c", h=H)
                for rows, c, gc, tot in ((slice(0, P), slice(0, 4), gch(0), gch(32)),
                                         (slice(0, NS), slice(4, 5), gp[0:NS, 1, 64:72].unsqueeze(2),
                                          gp[0:NS, 1, 72:80].unsqueeze(2))):
                    ts(gates[rows, :, KNG, c], gc, -1.0)
                    dve.tensor_copy(gates[rows, :, KEG, c], gc)
                    order(dve.tensor_copy(gates[rows, :, KEL, c], tot))
                    fence()
                    order(tt(gates[rows, :, KEK, c], tot, gates[rows, :, KNG, c], ADD))
                dve.tensor_copy(egl_s, gp[:, 1, 80:144].rearrange("p (h b) -> p h b", h=H)).then_inc(prep, 1)

            def gate_minus():
                dve.wait_ge(prep_act, 2)
                ts(gates[:, :, KNEG, :], gates[:, :, KEG, :], -1.0).then_inc(prep, 1)

            def conv_tap(hp, kb, j, tap):
                if tap == 0:
                    m, s = 2 * hp + (1 + j) // 2, (1 + j) % 2
                    dve.wait_ge(acc_free[s], m + 1)
                    dve.wait_ge(prev_put, 3 * hp + (j + 1))
                    if not (isinstance(hp, int) and hp == 0 and j == 0):
                        dve.wait_ge(conv_silu, 3 * hp + j)
                dst_s = conv_y[:, SEQ:SEQ + NS].rearrange("p (b t) -> p b t", b=NB)
                w = cw[kb][:, 4 * j + tap:4 * j + tap + 1]
                a_, b_ = cin_p[:, tap:tap + SEQ], cin_s[:, :, tap:tap + NT]
                if tap == 0:
                    order(ts(conv_y[:, 0:SEQ], a_, w))
                    order(ts(dst_s, b_, w))
                else:
                    dve.wait_ge(dve_t.sem, dve_t.now() - 1)
                    order(stt(conv_y[:, 0:SEQ], a_, w, conv_y[:, 0:SEQ], MUL, ADD))
                    dve.wait_ge(dve_t.sem, dve_t.now() - 1)
                    ins = stt(dst_s, b_, w, dst_s, MUL, ADD)
                    if tap == 3:
                        ins.then_inc(conv_done, 1)
                    else:
                        order(ins)

            def silu(hp, kb, j):
                dve.wait_ge(conv_tanh, 3 * hp + (j + 1))
                stt(kqv[kb][:, j, :], conv_t[:, 0:SEQ], 1.0, conv_y[:, 0:SEQ], ADD, MUL)
                stt(samp[:, hp, j, :], conv_t[:, SEQ:SEQ + NS], 1.0, conv_y[:, SEQ:SEQ + NS], ADD, MUL) \
                    .then_inc(conv_silu, 1)

            def z_product(hp):
                dve.wait_ge(z_tanh, hp + 1)
                stt(halves(full[:, 8 + hp, :]), halves(conv_t), 1.0, acc_of(0), ADD, MUL).then_inc(acc_free[0], 1)

            def head_dve(it, kb, name):
                pe_at = lambda n: dve.wait_ge(pe_h.sem, pe_h.at(n, it))
                col = lambda row, c: hs[:, row, c:c + 1]
                if name == "kg":
                    pe_at("kv_tok")
                    dve.wait_ge(pool_h.sem, pool_h.at("scalars", it))
                    ins = tt(kg, bank4(0), per_row(hs[:, KEK, 0:4], P), MUL)
                elif name == "dmask":
                    pe_at("gcum")
                    ins = tt(dec, bank4(2), per_group(negm, 4), ADD)
                elif name == "ssum":
                    pe_at("norm")
                    ins = ts(ssum, gp[:, 3, 0:8], EPS, None, ADD)
                elif name == "vs":
                    dve.wait_ge(pool_h.sem, pool_h.at("rn", it))
                    ins = tt(vs, bank4(1), per_row(rn[:, 0:4], P), MUL)
                elif name == "Mt":
                    pe_at("gram")
                    dve.wait_ge(act_h.sem, act_h.at("decay", it))
                    dve.wait_ge(pool_h.sem, pool_h.at("bp", it))
                    for c in range(NC):
                        ins = stt(mt[:, c, :], gp[:, 2 + c // 2, (c % 2) * 256:(c % 2) * 256 + P], bp[:, c:c + 1],
                                  dec[:, c, :], MUL, MUL)
                elif name == "attn":
                    qk = gp[:, 2:4, :].rearrange("p b (c s t) -> p (b c) s t", s=2, t=P)[:, :, 1, :]
                    ins = tt(attn, qk, dec, MUL)
                elif name == "X":
                    pe_at("m0")
                    ins = tt(xx[:, 0], per_group(ident, 4), bank4(0), SUB)
                elif name == "Xt":
                    ins = tt(xx[:, 1], per_group(ident, 4), mtl[0], SUB)
                elif name[0] == "X":
                    l = int(name[1])
                    pe_at(f"x{l}")
                    for s_ in range(0 if l < LEVELS - 1 else 1, 2):
                        part = half_blocks(xx[:, s_].rearrange("p c t -> p (c t)"), l, s_)
                        ins = tt(part, part, half_blocks(gp[:, 2 + s_, :], l, s_), SUB)
                elif name[0:2] == "vp":
                    c = int(name[2])
                    pe_at(f"u{c}")
                    ins = ts(vp, gp[:, 2, 0:P], bp[:, c:c + 1])
                elif name[0] == "S":
                    c = int(name[1])
                    pe_at(f"so{c}")
                    if c == 0:
                        if not (isinstance(it, int) and it == 0):
                            dve.wait_ge(state_out, 16 * it)
                        ins = dve.tensor_copy(st, gp[:, 3, 0:P])
                    else:
                        ins = stt(st, st, col(KEL, c), gp[:, 3, 0:P], MUL, ADD)
                elif name[0] == "o" and name != "on":
                    c = int(name[1])
                    if c == 0:
                        ins = dve.tensor_copy(o_tok[:, 0, :], gp[:, 0, 0:P])
                    else:
                        dve.wait_ge(act_h.sem, act_h.at(f"q{c}", it))
                        ins = tt(o_tok[:, c, :], gp[:, 0, 0:P], qs, ADD)
                elif name[0] == "r":
                    c = int(name[1])
                    pe_at(f"s{c}")
                    ins = stt(rr, gp[:, 0, 0:P], col(KNEG, c), vs[:, c, :], MUL, ADD)
                elif name == "on":
                    dve.wait_ge(pool_h.sem, pool_h.at("f5", it))
                    ins = tt(on, o_tok, per_row(f_a, P), MUL)
                else:
                    pe_at("o_chan")
                    dve.wait_ge(acc_free[0], 2 * it + 3)
                    dst = halves(full[:, 8 + it, :])[:, :, 0:HP]
                    ins = stt(dst, gp[:, 0, :].rearrange("p (a t) -> p a t", a=2), dng, dst, MUL, MUL)
                ins.then_inc(dve_h.sem, 1)

            def head_unit(hp, it=None, kb=0, convs=True):
                for ti in range(4):
                    for e in range(8):
                        if it is not None:
                            if 8 * ti + e == 0 and not (isinstance(it, int) and it == 0):
                                head_dve(it - 1, 1 - kb, "y")
                            for name in DVE_PLAN.get(8 * ti + e, ()):
                                head_dve(it, kb, name)
                            if ti == 0 and e == 2:
                                z_product(it)
                        elif (ti, e) in GATE_STEPS:
                            GATE_STEPS[ti, e]()
                        if convs and ti and 2 <= e <= 5:
                            conv_tap(hp, 1 - kb, ti - 1, e - 2)
                        if convs and ti and e == 7:
                            silu(hp, 1 - kb, ti - 1)
                        next_split(2 * hp + (1 + ti) // 2, (1 + ti) % 2, e)

            GATE_STEPS = {(0, 3): gate_inputs, (0, 6): gate_scalars, (1, 0): gate_factors, (1, 3): gate_minus}
            head_unit(0, kb=1)
            head_unit(1, 0, 0)
            with dve.Fori(0, 3) as i:
                dve_t.enter(i, 2 * 3 * 7)
                head_unit(2 * i + 2, 2 * i + 1, 1)
                head_unit(2 * i + 3, 2 * i + 2, 0)
                dve_t.leave(3)
            head_unit(8, 7, 1, convs=False)
            head_dve(H - 1, 1, "y")

            def samp_dve_step(name):
                pe_at = lambda n: dve.wait_ge(samp_pe, SPE[n])
                own = lambda n: dve.wait_ge(samp_dve, SD[n])
                gcol = lambda row, h: gates[0:NS, h, row, 4:5]
                b64 = lambda ap: ap.rearrange("p (h t) -> p h t", t=NS)
                ids = per_group(ident[0:NS, 0:NS], H)
                wide = lambda s_: gp[0:NS, 0:2, :].rearrange("p b (h s t) -> p (b h) s t", s=2, t=NS)[:, :, s_, :]
                if name == "kg":
                    pe_at("k_tok")
                    ins = tt(kg_s, gp[0:NS, 0:2, :].rearrange("p b (h d) -> p (b h) d", d=P),
                             per_row(gates[0:NS, :, KEK, 4], P), MUL)
                elif name == "ssum":
                    pe_at("norm")
                    ins = ts(ssum_s, gp[0:NS, 0, 0:16], EPS, None, ADD)
                elif name == "vs":
                    pe_at("v_tok")
                    dve.wait_ge(samp_pool, SP_["rn"])
                    ins = tt(vs_s, gp[0:NS, 2:4, :].rearrange("p b (h d) -> p (b h) d", d=P),
                             per_row(rn_s.rearrange("p (h s) -> p h s", s=2)[:, :, 0], P), MUL)
                elif name == "dmask":
                    pe_at("gcum")
                    ins = tt(dec_s, b64(gp[0:NS, 2, :]), per_group(cst[0:NS, C_NEGS:C_NEGS + NS], H), ADD)
                elif name == "dmask2":
                    own("dmask")
                    ins = tt(dec_s, dec_s, per_row(gates[0:NS, :, KNG, 4], NS), ADD)
                elif name == "Mt":
                    pe_at("gram")
                    dve.wait_ge(samp_act, SA["decay"])
                    ins = tt(mt_s, wide(0), dec_s, MUL)
                elif name == "Mtb":
                    own("Mt")
                    dve.wait_ge(samp_pool, SP_["bp"])
                    ins = tt(mt_s, mt_s, per_row(bp_s, NS), MUL)
                elif name == "attn":
                    ins = tt(attn_s, wide(1), dec_s, MUL)
                elif name == "X":
                    pe_at("m0")
                    ins = tt(x_s, ids, b64(gp[0:NS, 2, :]), SUB)
                elif name == "Xt":
                    ins = tt(xt_s, ids, mtl_s[0], SUB)
                elif name == "X1":
                    pe_at("x1")
                    ins = tt(x_s, x_s, b64(gp[0:NS, 2, :]), SUB)
                elif name in ("Xt1", "Xt2"):
                    pe_at(f"x{name[2]}")
                    ins = tt(xt_s, xt_s, b64(gp[0:NS, 0, :]), SUB)
                elif name == "on":
                    own(f"o{H // 2 - 1}")
                    dve.wait_ge(samp_pool, SP_["f5"])
                    ins = tt(o_s, o_s, per_row(fa_s, P), MUL)
                elif name[0] == "r":
                    g = int(name[1:])
                    pe_at(f"tr{g}")
                    if g:
                        dve.wait_ge(samp_pool, SP_[f"vx{2 * g - 1}"])
                    for i in range(2):
                        ins = stt(rs_[:, i, :], gp[0:NS, 3, i * P:(i + 1) * P], gcol(KNEG, 2 * g + i),
                                  vs_s[:, 2 * g + i, :], MUL, ADD)
                elif name[0:2] == "vp":
                    g = int(name[2:])
                    pe_at(f"u{g}")
                    ins = tt(vps, gp[0:NS, 2, 0:2 * P].rearrange("p (i d) -> p i d", i=2),
                             per_row(bp_s[:, 2 * g:2 * g + 2], P), MUL)
                elif name[0] == "o":
                    g = int(name[1:])
                    pe_at(f"o{g}")
                    dve.wait_ge(samp_act, SA[f"q{g}"])
                    ins = tt(o_s[:, 2 * g:2 * g + 2, :], gp[0:NS, 3, 0:2 * P].rearrange("p (i d) -> p i d", i=2),
                             o_s[:, 2 * g:2 * g + 2, :], ADD)
                else:
                    h = int(name[1:])
                    pe_at(f"ns{h}")
                    for b in range(NB):
                        ins = stt(s0[h % 4][:, b, :], s0[h % 4][:, b, :], egl_s[:, h, b:b + 1],
                                  gp[:, b // 4, (b % 4) * P:(b % 4 + 1) * P], MUL, ADD)
                ins.then_inc(samp_dve, 1)

            def samp_out():
                dve.wait_ge(samp_pe, SPE["o_chan"])
                for a_ in range(2):
                    dst = full[:, 8:16, a_ * HALF + HP:(a_ + 1) * HALF]
                    ins = stt(dst, gp[:, 2, :].rearrange("p (h a c) -> p h a c", h=H, a=2)[:, :, a_, :], dng, dst,
                              MUL, MUL)
                ins.then_inc(ys_done, 1)

            def att_bias(u):
                r, c, jj = u // 8, (u // 2) % 4, u % 2
                lo = 0 if c else P
                pr, sink = prob[u % 2][:, :, lo:], par[:, P_SINK + 8 * r + 4 * jj:P_SINK + 8 * r + 4 * jj + 4]
                dve.wait_ge(scores, u + 1)
                if u >= 2:
                    dve.wait_ge(turned, u - 1)
                if u == 1:
                    dve.wait_ge(dnc_stored, 16)
                s_ = gp[:, 0:2, :].rearrange("p q (j w) -> p (q j) w", j=2)[:, :, lo:]
                order(stt(pr, s_, 0.125, per_group(caus[:, lo:], 4), MUL, ADD))
                fence()
                order(dve.tensor_reduce(amax, pr, AX_X, ALU.max))
                fence()
                order(tt(amax, amax, sink, ALU.max))
                fence()
                ts(nmax[u % 2], amax, -1.0)
                tt(dsink[u % 2], sink, amax, SUB).then_inc(biased, 1)

            def att_probs(u):
                lo = 0 if (u // 2) % 4 else P
                pr = prob[u % 2][:, :, lo:]
                dve.wait_ge(exped, u + 1)
                order(tt(esum[u % 2], esum[u % 2], esink[u % 2], ADD))
                fence()
                order(dve.reciprocal(esum[u % 2], esum[u % 2]))
                fence()
                tt(pr, pr, per_row(esum[u % 2], 2 * P - lo), MUL).then_inc(probs, 1)

            def za_product(i):
                n = N_ZA + i
                dve.wait_ge(z_tanh, H + i + 1)
                order(stt(halves(za_t), halves(za_t), 1.0, acc_of(n % 2), ADD, MUL))
                dve.wait_ge(attn_out, 8 * (i // 4 + 1))
                fence()
                dst = halves(full[:, i, :])[:, :, 0:HP]
                stt(dst, halves(za_t)[:, :, 0:HP], 0.5, dst, MUL, MUL)
                dve.tensor_copy(zs_samp[:, i], halves(za_t)[:, :, HP:HALF]).then_inc(acc_free[n % 2], 1)

            def samp_att(name):
                if name == "bias":
                    dve.wait_ge(sa_pe, SAP["scores"])
                    for i_, nb in enumerate((3, 3, 2)):
                        stt(prob_s[:, 3 * i_:3 * i_ + nb, :],
                            gp[:, i_, 0:136 * nb].rearrange("p (b t) -> p b t", b=nb), 0.125,
                            per_group(cst[:, C_WIN:C_WIN + W + NT], nb), MUL, ADD).then_inc(sa_dve, 1)
                    own("bias2")
                    dve.tensor_reduce(amax_s, prob_s, AX_X, ALU.max).then_inc(sa_dve, 1)
                    own("max")
                    sink = par[:, P_SINKS:P_SINKS + 1]
                    ts(amax_s, amax_s, sink, None, ALU.max).then_inc(sa_dve, 1)
                    own("max2")
                    ts(nmax_s, amax_s, -1.0).then_inc(sa_dve, 1)
                    own("neg")
                    ts(dsink_s, nmax_s, sink, None, ADD).then_inc(sa_dve, 1)
                elif name == "prob":
                    dve.wait_ge(sa_act, SAA["exp"])
                    tt(esum_s, esum_s, dsink_s, ADD).then_inc(sa_dve, 1)
                    own("den")
                    dve.reciprocal(esum_s, esum_s).then_inc(sa_dve, 1)
                    own("inv")
                    tt(prob_s, prob_s, per_row(esum_s, W + NT), MUL).then_inc(sa_dve, 1)
                elif name == "turned_new":
                    dve.wait_ge(sa_pe, SAP["turn_new"])
                    dve.tensor_copy(probT_n[0:NT], bank4(2, 2)[0:NT]).then_inc(sa_dve, 1)
                else:
                    r = int(name[3])
                    dve.wait_ge(sa_pe, SAP[f"weigh{r}"])
                    for a_ in range(2):
                        ins = dve.tensor_copy(full[:, 4 * r:4 * r + 4, a_ * HALF + HP:(a_ + 1) * HALF],
                                              gp[:, 2, 0:256].rearrange("p (j a c) -> p j a c", j=4, a=2)[:, :, a_, :])
                    ins.then_inc(sa_dve, 1)

            own = lambda n_: dve.wait_ge(sa_dve, SAD[n_])
            for t in range(16):
                n = N_Q + t
                for e in range(8):
                    slot = 8 * t + e
                    for name in SAMP_DVE.get(slot, ()):
                        samp_dve_step(name)
                    if slot == ATT0 - 3:
                        samp_out()
                    if ATT0 <= slot <= SATT0:
                        u, phase = (slot - ATT0) // 3, (slot - ATT0) % 3
                        if phase == 0:
                            att_bias(u)
                        if phase == 2:
                            att_probs(u)
                    elif slot - SATT0 in SATT_DVE:
                        samp_att(SATT_DVE[slot - SATT0])
                    if e == 4 and t > 8:
                        za_product(t - 9)
                    next_split(n // 2, n % 2, e)
            act_lo_even(1, 8)
            za_product(7)
            own("out1")
            for n in (N_OUT0 - 2, N_OUT0 - 1):
                dve.wait_ge(acc_free[n % 2], n // 2 + 1)
            dve.wait_ge(out_small, 16 * n_small)
            dve.wait_ge(vnew_stored, 32)
            for a_ in range(2):
                dst = full[:, 0:8, a_ * HALF + HP:(a_ + 1) * HALF]
                stt(dst, zs_samp[:, :, a_, :], 0.5, dst, MUL, MUL).then_inc((res_free, gated)[a_], 1)

            def out_section(n0, turn):
                def add_residual(m, s, j, jp, rnd):
                    dve.wait_ge(w_used, 4 * m + (2 * s + 2))
                    dve.wait_ge(res_in[jp], 16 * rnd + (16 if turn == 1 else 16 + 8 * KT))
                    tt(halves(full[:, j, :]), acc_of(s), halves(res[jp]), ADD).then_inc(acc_free[s], 1)

                for k in split_order(turn)[2 if turn == 1 else 8::2]:
                    act_lo_even(turn, k)
                for half in range(2):
                    split_lo((n0 + 1) // 2, (n0 + 1) % 2, half)
                dve.wait_ge(ahi_done, KT * (turn + 1))
                dve.wait_ge(alo_odd, 8 * (turn + 1))
                for j in (1, 2):
                    n = n0 + j
                    add_residual((n - 1) // 2, (n - 1) % 2, j - 1, (j - 1) % 2, (j - 1) // 2)
                    for half in range(2):
                        split_lo((n + 1) // 2, (n + 1) % 2, half)
                with dve.Fori(0, KT // 2 - 2) as i:
                    for b in range(2):
                        n = n0 + 3 + b
                        add_residual(i + (n - 1) // 2, (n - 1) % 2, 2 * i + 2 + b, b, i + 1)
                        for half in range(2):
                            split_lo(i + (n + 1) // 2, (n + 1) % 2, half)
                n = n0 + KT - 1
                add_residual((n - 1) // 2, (n - 1) % 2, KT - 2, 0, KT // 2 - 1)
                if n + 1 < N_TILES:
                    split_lo((n + 1) // 2, (n + 1) % 2, 0)
                    split_lo((n + 1) // 2, (n + 1) % 2, 1)
                add_residual(n // 2, n % 2, KT - 1, 1, KT // 2 - 1)

            out_section(N_OUT0, 1)
            token_norm(1, 2)
            scale_and_split(2, P_G1, [(x1_stored, 16 * KT)])
            split_lo((N_VG + 1) // 2, (N_VG + 1) % 2, 0)
            split_lo((N_VG + 1) // 2, (N_VG + 1) % 2, 1)

            c_s = c_buf[:, SEQ:SEQ + NS].rearrange("p (b t) -> p b t", b=NB)
            c_o = c_odd.rearrange("p (b t) -> p b t", b=NB)

            def glu(j, b, rnd):
                dve.wait_ge(w_used, 4 * j + (4 * (N_VG // 2 + 1) + 2))
                dve.wait_ge(acc_free[1], j + (N_VG // 2 + 1))
                dve.wait_ge(u_free[b], rnd + 1)
                tt(halves(u_p[b][:, CP:CP + SEQ]), acc[:, 0, :, 0:HP], halves(tg[b])[:, :, 0:HP], MUL)
                tt(u_s[b][:, :, CP:CP + NT].rearrange("p (a b) t -> p a b t", a=2),
                   acc[:, 0, :, HP:HALF].rearrange("p a (b t) -> p a b t", t=NT),
                   halves(tg[b])[:, :, HP:HALF].rearrange("p a (b t) -> p a b t", t=NT), MUL).then_inc(acc_free[0], 1)

            def conv_taps(j, b, rnd, taps):
                for k in taps:
                    wk = cfw[:, j, k:k + 1]
                    c_ = (c_s, c_o)[k % 2]
                    if k == 0:
                        dve.wait_ge(acc_free[0], j + (N_VG // 2 + 2))
                        dve.wait_ge(uprev_in[b], 16 * rnd + 16)
                    if k < 2:
                        order(ts(c_, u_s[b][:, :, k:k + NT], wk))
                    else:
                        dve.wait_ge(dve_t.sem, dve_t.now() - 2)
                        order(stt(c_, u_s[b][:, :, k:k + NT], wk, c_, MUL, ADD))
                    if k % 2 == 1 or k == CF - 1:
                        q = k // 2
                        wq = cfw[:, j, q:q + 1]
                        if q == 0:
                            order(ts(c_buf[:, 0:SEQ], u_p[b][:, q:q + SEQ], wq))
                        else:
                            dve.wait_ge(dve_t.sem, dve_t.now() - 1 - k % 2)
                            order(stt(c_buf[:, 0:SEQ], u_p[b][:, q:q + SEQ], wq, c_buf[:, 0:SEQ], MUL, ADD))

            def combine(j, b):
                dve.wait_ge(tap_sum, POOL_SUMS * j + (1 + POOL_SUMS))
                dve.wait_ge(cf_stored, 32 * j + 32)
                fence()
                stt(halves(full[:, j, :])[:, :, 0:HP], halves(c_buf[:, 0:SEQ]), cfb[:, j, :], halves(pacc), ADD, ADD) \
                    .then_inc(u_free[b], 1)
                stt(halves(full[:, j, :])[:, :, HP:HALF], halves(c_buf[:, SEQ:SEQ + NS]), cfb[:, j, :], halves(c_odd),
                    ADD, ADD) \
                    .then_inc(c_done, 1)

            n = N_VG
            for half in range(2):
                split_lo((n + 2) // 2, 1, half)

            def conformer_pair(j, b, rnd):
                m = j + N_VG // 2
                glu(j - 1, 1 - b, rnd)
                for half in range(2):
                    split_lo(m + 1, 0, half)
                conv_taps(j - 1, 1 - b, rnd, range(0, 14))
                for half in range(2):
                    split_lo(m + 1, 1, half)
                conv_taps(j - 1, 1 - b, rnd, range(14, CF))
                if isinstance(j, int):
                    dve.wait_ge(ahi_done, 3 * KT)
                    dve.wait_ge(alo_odd, 24)
                combine(j - 1, 1 - b)

            conformer_pair(1, 1, 0)
            with dve.Fori(0, KT // 2 - 1) as i:
                dve_t.enter(i, 2 * (DVE_TAPS + CF))
                conformer_pair(2 * i + 2, 0, i)
                conformer_pair(2 * i + 3, 1, i + 1)
                dve_t.leave(KT // 2 - 1)
            glu(KT - 1, 1, KT // 2 - 1)
            for half in range(2):
                split_lo((N_Z1 + 1) // 2, (N_Z1 + 1) % 2, half)
            conv_taps(KT - 1, 1, KT // 2 - 1, range(CF))
            combine(KT - 1, 1)

            for t in range(1, KT + 1):
                n = N_Z1 + t
                if t == KT:
                    for k in (0, 2, 4):
                        act_lo_even(3, k)
                dve.wait_ge(zz_tanh, t)
                zr = zring[(t - 1) % ZRING]
                stt(halves(zr), halves(zr), 1.0, acc_of((n - 1) % 2), ADD, MUL).then_inc(acc_free[(n - 1) % 2], 1)
                if t < KT:
                    split_lo((n + 1) // 2, (n + 1) % 2, 0)
                    split_lo((n + 1) // 2, (n + 1) % 2, 1)
                if t == 3:
                    dve.wait_ge(norm_sum, 3)
                    order(ts(halves(mean), gp[:, 0:2, 0:HALF], 1.0 / D))
                    fence()
                    dve.wait_ge(c_done, KT)
                    for k in range(KT):
                        tt(full[:, k, :], full[:, k, :], mean, SUB).then_inc(centred, 1)
                if t == 6:
                    token_norm(2, 4)
                if t == 7:
                    dve.wait_ge(root_out, 3)
                for k in LN_Y.get(t, ()):
                    tt(halves(full[:, k, :]), halves(full[:, k, :]), rstd_ps, MUL).then_inc(ln_scaled, 1)
                if t == KT:
                    act_lo_even(3, 6)
                for k in LN_Y.get(t, ()):
                    dve.wait_ge(ln_tanh, k + 1)
                    order(stt(full[:, k, :], sqb[k % 2], 1.0, full[:, k, :], ADD, MUL))
                    fence()
                    dve.wait_ge(acc_free[(N_Z1 + k) % 2], (N_Z1 + k) // 2 + 1)
                    stt(full[:, k, :], full[:, k, :], 0.5, zring[k % ZRING], MUL, MUL).then_inc(y_done, 1)
            out_section(N_OUT1, 3)
            token_norm(3, 5)
            for k in range(KT):
                stt(halves(full[:, k, :]), halves(full[:, k, :]), par[:, P_GF + k:P_GF + k + 1], rstd_ps, MUL, MUL) \
                    .then_inc(scaled, 1)

        @block.gpsimd
        def _(pool):
            def order(ins):
                pool_t.inc(ins)

            def fence():
                pool.wait_ge(pool_t.sem, pool_t.now())

            def tt(out, a, b, op=ALU.mult):
                return pool.tensor_tensor(out, a, b, op)

            def copy(out, a):
                one = ones[0:a.shape[0], 0:1]
                return tt(out, a, (one if len(a.shape) == 2 else one.unsqueeze(2)).to_broadcast(list(a.shape)))

            def act_lo_odd(turn):
                for pos, k in list(enumerate(split_order(turn)))[1::2]:
                    pool.wait_ge(ahi_done, KT * turn + pos + 1)
                    tt(act_lo[:, k, :], full[:, k, :], act_hi[:, k, :].bitcast(F32), ALU.subtract) \
                        .then_inc(alo_odd, 1)

            pool.memset(one_col, 1.0).then_inc(ones_set, 1)
            pool.memset(mhalf, -0.5)
            order(pool.memset(eps_p2, EPS * P * P))

            def inverse_root(turn):
                pool.wait_ge(var_ready, turn + 1)
                tt(r6, ms6, mh[:, 0:6], ALU.pow).then_inc(root, 1)

            fence()
            inverse_root(0)
            act_lo_odd(0)
            order(pool.memset(cin_p[:, 0:3], 0.0))
            pool.wait_ge(halved, 1)
            pool.wait_ge(prev_in, 16)

            dnw = par[:, P_DNW:P_DNW + 12 * H].rearrange("p (h t) -> p h t", h=H)

            def put_prev(hp, kb, j):
                if not (isinstance(hp, int) and hp == 0 and j == 0):
                    pool.wait_ge(conv_done, 3 * hp + j)
                if j == 0:
                    copy(cw[kb], dnw[:, hp, :])
                copy(cin_s[:, :, 0:3], dnc[:, 3 * hp + j, 1:9, :]).then_inc(prev_put, 1)

            def take_last(hp, j):
                m, s = 2 * hp + (1 + j) // 2, (1 + j) % 2
                pool.wait_ge(acc_free[s], m + 1)
                pool.wait_ge(prev_put, 3 * hp + (j + 1))
                copy(dnc[:, 3 * hp + j, 0, :], cin_p[:, SEQ:SEQ + 3])
                copy(dnc[:, 3 * hp + j, 1:9, :], cin_s[:, :, NT:NT + 3]).then_inc(last_taken, 1)

            def head_pool(it, name):
                own = lambda n: pool.wait_ge(pool_h.sem, pool_h.at(n, it))
                dv = lambda n: pool.wait_ge(dve_h.sem, dve_h.at(n, it))
                if name == "scalars":
                    if isinstance(it, int) and it == 0:
                        pool.wait_ge(prep, 4)
                    else:
                        pool.wait_ge(dve_h.sem, dve_h.at(f"o{NC - 1}", it - 1))
                    ins = copy(hs, gates[:, it])
                elif name == "gB":
                    own("scalars")
                    ins = copy(gB, per_row(hs[:, KG, 0:4], P))
                elif name == "nrm":
                    dv("ssum")
                    ins = tt(nrm, ssum, mh[:, 0:8], ALU.pow)
                elif name == "rn":
                    own("nrm")
                    ins = tt(rn, ssum, nrm)
                elif name == "bn":
                    ins = tt(bn, hs[:, KBETA, 0:4], nrm[:, 0:4])
                elif name == "bp":
                    own("bn")
                    ins = tt(bp, bn, nrm[:, 0:4])
                elif name[0] == "L":
                    l = int(name[1])
                    dv("Mt")
                    if l == 2:
                        dv("Xt")
                    if l >= 2:
                        pool.wait_ge(pe_h.sem, pe_h.at("m0" if l == 2 else f"a{l - 2}", it))
                    lo = C_LVL + l * P
                    ins = tt(mtl[l % 2], mt, per_group(cst[:, lo:lo + P], 4))
                elif name == "f1":
                    pool.wait_ge(act_h.sem, act_h.at("osq", it))
                    ins = tt(f_a, osum, nrm[:, 4:8])
                elif name == "f2":
                    own("f1")
                    ins = tt(f_b, f_a, nrm[:, 4:8])
                elif name == "f3":
                    own("f2")
                    ins = tt(f_a, f_b, eps_p2[:, 0:4], ALU.add)
                elif name == "f4":
                    own("f3")
                    ins = tt(f_b, f_a, mh[:, 0:4], ALU.pow)
                else:
                    own("f4")
                    ins = tt(f_a, f_b, nrm[:, 4:8])
                ins.then_inc(pool_h.sem, 1)

            def head_unit(hp, it=None, kb=0, convs=True):
                for ti in range(4):
                    for e in range(8):
                        if it is not None:
                            for name in POOL_PLAN.get(8 * ti + e, ()):
                                head_pool(it, name)
                            if 8 * ti + e == 29:
                                pool.wait_ge(dve_h.sem, dve_h.at(f"S{NC - 1}", it))
                                pool.dma_start(dn_out[it], st).then_inc(state_out, 16)
                        if convs and ti and e == 1:
                            take_last(hp, ti - 1)
                        if convs and (ti == 0 or e == 5) and 8 * ti + e in (0, 13, 21):
                            put_prev(hp, 1 - kb, ti)

            head_unit(0, kb=1)
            head_unit(1, 0, 0)
            with pool.Fori(0, 3) as i:
                head_unit(2 * i + 2, 2 * i + 1, 1)
                head_unit(2 * i + 3, 2 * i + 2, 0)
            pool.wait_ge(last_taken, 3 * H)
            pool.dma_start(dnc_out, dnc.rearrange("p n s t -> p (n s t)")).then_inc(dnc_stored, 16)
            head_unit(8, 7, 1, convs=False)

            def samp_pool_step(name):
                own = lambda n: pool.wait_ge(samp_pool, SP_[n])
                kq = lambda ap, j: ap.rearrange("p (h s) -> p h s", s=2)[:, :, j]
                if name == "gB":
                    pool.wait_ge(dve_h.sem, dve_h.at("y", H - 1))
                    ins = copy(gB_s, per_row(gates[0:NS, :, KG, 4], NS))
                elif name == "nrm":
                    pool.wait_ge(samp_dve, SD["ssum"])
                    ins = tt(nrm_s, ssum_s, mh[0:NS, 0:16], ALU.pow)
                elif name == "rn":
                    own("nrm")
                    ins = tt(rn_s, ssum_s, nrm_s)
                elif name == "bn":
                    ins = tt(bn_s, gates[0:NS, :, KBETA, 4], kq(nrm_s, 0))
                elif name == "bp":
                    own("bn")
                    ins = tt(bp_s, bn_s, kq(nrm_s, 0))
                elif name[0] == "L":
                    l = int(name[1])
                    pool.wait_ge(samp_dve, SD["Mtb"])
                    if l == 2:
                        pool.wait_ge(samp_dve, SD["Xt"])
                    lo = C_LVL + l * P
                    ins = tt(mtl_s[l % 2], mt_s, per_group(cst[0:NS, lo:lo + NS], H))
                elif name[0:2] == "vx":
                    h = int(name[2:])
                    pool.wait_ge(samp_dve, SD[f"vp{h // 2}"])
                    if h:
                        pool.wait_ge(samp_pe, SPE[f"ns{h - 1}"])
                    ins = tt(vpx, vps[:, h % 2, :].unsqueeze(1).to_broadcast([NS, NB, P]), per_row(cst[0:NS, C_SEQ:C_SEQ + NB], P))
                elif name == "f1":
                    pool.wait_ge(samp_act, SA["osq"])
                    ins = tt(fa_s, sos, kq(nrm_s, 1))
                elif name == "f2":
                    own("f1")
                    ins = tt(fb_s, fa_s, kq(nrm_s, 1))
                elif name == "f3":
                    own("f2")
                    ins = tt(fa_s, fb_s, eps_p2[0:NS], ALU.add)
                elif name == "f4":
                    own("f3")
                    ins = tt(fb_s, fa_s, mh[0:NS, 0:8], ALU.pow)
                else:
                    own("f4")
                    ins = tt(fa_s, fb_s, kq(nrm_s, 1))
                ins.then_inc(samp_pool, 1)

            def store_state(h):
                pool.wait_ge(samp_dve, SD[f"S{h}"])
                pool.dma_start(sdn_out[h], s0[h % 4].rearrange("p b d -> p (b d)")).then_inc(sdn_stored[h % 4], 16)

            for name in SP_:
                samp_pool_step(name)
                if name in ("vx1", "vx3", "vx5", "f5"):
                    h = H - 1 if name == "f5" else int(name[2])
                    store_state(h - 1)
                    store_state(h)

            pool.wait_ge(vtok_done, 1)
            pool.dma_start(win_v, v_tok[:, NC - 1].rearrange("p r d -> p (r d)")).then_inc(out_small, 16)
            pool.wait_ge(kc_in, 16)
            for r in range(2):
                pool.dma_start(win_k[r], kv[:, 2 * r, blk(NC - 1):blk(NC - 1) + P]).then_inc(out_small, 16)
                pool.dma_start(swk_out[r, :, :, 0:W - NT], kc[:, r, :, NT:W]).then_inc(out_small, 16)
                for a_ in range(2):
                    pool.dma_start(swk_out[r, :, 4 * a_:4 * a_ + 4, W - NT:W],
                                   kv[:, 2 * r, a_ * HALF + HP:(a_ + 1) * HALF].rearrange("p (b t) -> p b t", t=NT)) \
                        .then_inc(out_small, 16)
            pool.wait_ge(vc_in, 16)
            pool.dma_start(swv_out[0:W - NT], vc[NT:W].rearrange("p b d -> p (b d)")).then_inc(out_small, 16)
            pool.wait_ge(turned, 16)
            pool.wait_ge(acc_free[(N_Q + 7) % 2], (N_Q + 7) // 2 + 1)
            for r in range(2):
                for a_ in range(2):
                    copy(q_samp[:, r, 4 * a_:4 * a_ + 4, :].rearrange("p b (g t) -> p g b t", g=4),
                                     full[:, 4 * r:4 * r + 4, a_ * HALF + HP:(a_ + 1) * HALF]
                                     .rearrange("p g (b t) -> p g b t", t=NT)).then_inc(q_samp_put, 1)
            for r in range(2):
                pool.wait_ge(sa_act, SAA[f"v_new{r}"])
                pool.dma_start(swv_out[W - NT:W].rearrange("p (b r d) -> p r b d", b=NB, r=2)[:, r], v_new[0:NT]) \
                    .then_inc(vnew_stored, 16)

            def out_section(turn):
                act_lo_odd(turn)
                base = KT if turn == 1 else 2 * KT
                summed = 0 if turn == 1 else KT - 1
                for j in range(2):
                    pool.wait_ge(sq_done, base + j + 1)
                    if j == 0:
                        pool.tensor_copy(ssq, sqb[0]).then_inc(sq_summed, 1)
                    else:
                        pool.wait_ge(sq_summed, summed + 1)
                        tt(ssq, ssq, sqb[1], ALU.add).then_inc(sq_summed, 1)
                with pool.Fori(0, KT // 2 - 2) as i:
                    for b in range(2):
                        pool.wait_ge(sq_done, 2 * i + (base + 3 + b))
                        pool.wait_ge(sq_summed, 2 * i + (summed + 2 + b))
                        tt(ssq, ssq, sqb[b], ALU.add).then_inc(sq_summed, 1)
                pool.wait_ge(sq_done, base + KT - 1)
                pool.wait_ge(sq_summed, summed + KT - 2)
                tt(ssq, ssq, sqb[0], ALU.add).then_inc(sq_summed, 1)
                inverse_root(turn)

            out_section(1)
            act_lo_odd(2)
            for b in range(2):
                pool.memset(u_p[b][:, 0:CP], 0.0).then_inc(u_free[b], 1)
            pool.memset(pacc, 0.0).then_inc(tap_sum, 1)

            def conv_tile(j, b, rnd):
                pool.wait_ge(acc_free[0], j + (N_VG // 2 + 2))
                pool.wait_ge(uprev_in[b], 16 * rnd + 16)
                pool.dma_start(cf_out[j], u_p[b][:, SEQ:SEQ + CP]).then_inc(cf_stored, 16)
                pool.dma_start(cfs_out[j].rearrange("p (b t) -> p b t", b=NB), u_s[b][:, :, NT:NT + CP]).then_inc(cf_stored, 16)
                for i_ in range(1, POOL_TAPS):
                    src = prod[i_ % 3]
                    pool.wait_ge(tap_prod, POOL_TAPS * j + (i_ + 1))
                    if i_ == 1:
                        if not (isinstance(j, int) and j == 0):
                            pool.wait_ge(c_done, j)
                        pool.wait_ge(tap_sum, POOL_SUMS * j + 1)
                        tt(pacc, prod[0], src, ALU.add).then_inc(tap_sum, 1)
                    else:
                        pool.wait_ge(tap_sum, POOL_SUMS * j + i_)
                        tt(pacc, pacc, src, ALU.add).then_inc(tap_sum, 1)

            def sum_tile(j, source, ready):
                pool.wait_ge(ready, j + 1)
                if isinstance(j, int) and j == 0:
                    return pool.tensor_copy(csum, source).then_inc(c_summed, 1)
                pool.wait_ge(c_summed, j)
                tt(csum, csum, source, ALU.add).then_inc(c_summed, 1)

            conv_tile(0, 0, 0)
            conv_tile(1, 1, 0)
            pool.wait_ge(scaled, 2 * KT)
            sum_tile(0, full[:, 0, :], c_done)
            with pool.Fori(0, KT // 2 - 1) as i:
                for b in range(2):
                    conv_tile(2 * i + 2 + b, b, i + 1)
                    sum_tile(2 * i + 1 + b, full[:, 2 * i + 1 + b, :], c_done)
            sum_tile(KT - 1, full[:, KT - 1, :], c_done)
            pool.wait_ge(norm_sum, 3)
            for k in range(KT - 1):
                pool.wait_ge(ln_sq, k + 1)
                if k == 0:
                    pool.tensor_copy(csum, sqb[0]).then_inc(c_summed, 1)
                else:
                    pool.wait_ge(c_summed, KT + k)
                    tt(csum, csum, sqb[k % 2], ALU.add).then_inc(c_summed, 1)
            inverse_root(2)
            out_section(3)


_OUT = [("y", (KT, P, TOK)), ("win_k", (2, P, P)), ("win_v", (P, 2 * P)), ("dn", (H, P, P)), ("dnc", (P, 3 * H * 27)),
        ("cf", (KT, P, CP)), ("cfs", (KT, P, NB * CP)), ("swk", (2, P, NB, W)), ("swv", (W, NB * 2 * P)),
        ("sdn", (H, P, NB * P))]


def _constants():
    i, j = np.arange(P)[None, :], np.arange(P)[:, None]
    c = np.zeros((P, N_CONST), np.float32)
    c[:, C_ID:C_ID + P] = i == j
    c[:, C_TRI:C_TRI + P] = j <= i
    c[:, C_ONE:C_ONE + P] = 1
    c[:, C_NEG:C_NEG + P] = np.where(j <= i, 0, NEG)
    c[:, C_CAU:C_CAU + P] = np.where(i >= j, 0, NEG)
    c[:, C_CAU + P:C_CAU + 2 * P] = np.where(i <= j, 0, NEG)
    for l in range(LEVELS):
        b = 1 << l
        c[:, C_LVL + l * P:C_LVL + (l + 1) * P] = (i // (2 * b) == j // (2 * b)) & (j // b % 2 == 0) & (i // b % 2 == 1)
    i, j = i[:, :NS], j[:NS]
    same = i // NT == j // NT
    c[:NS, C_TRIS:C_TRIS + NS] = same & (j <= i)
    c[:NS, C_ONES:C_ONES + NS] = same
    c[:NS, C_NEGS:C_NEGS + NS] = np.where(same & (j <= i), 0, NEG)
    c[:NS, C_SEQ:C_SEQ + NB] = j // NT == np.arange(NB)[None, :]
    t = np.arange(P)[:, None] % NT
    c[:, C_WIN:C_WIN + W] = np.where(np.arange(W)[None, :] >= t, 0, NEG)
    c[:, C_WIN + W:] = np.where(np.arange(NT)[None, :] <= t, 0, NEG)
    return c


def kernel(x_prompt, x_sample, cache_win_k, cache_win_v, state_dn, state_dn_conv, state_cf_conv, norm_gain,
           w_in_even, w_out_even, attn_sinks, dn_conv_w, dn_a_log, dn_dt_bias, dn_norm_gain, w_in_odd, w_out_odd,
           cf_conv_w, cf_conv_b, cf_ln_gain, cf_ln_bias, final_norm_gain):
    import concourse.bacc as bacc
    from concourse.bass_utils import run_bass_kernel_spmd

    f32 = np.float32
    x_prompt, x_sample, cache_win_k, cache_win_v, state_dn, state_dn_conv, state_cf_conv = (
        np.asarray(a) for a in (x_prompt, x_sample, cache_win_k, cache_win_v, state_dn, state_dn_conv, state_cf_conv))
    w0, wo0, w1, wo1 = (np.asarray(a)[0] for a in (w_in_even, w_out_even, w_in_odd, w_out_odd))

    def channel_major(prompt, sample):
        x = np.empty((2, HALF, D), f32)
        x[:, :HP] = prompt.reshape(2, HP, D)
        x[:, HP:] = sample.reshape(2, HS, D)
        return np.ascontiguousarray(x.reshape(TOK, KT, P).transpose(1, 2, 0))

    QA, KA, VA, ZA, QKV = 0, 1024, 1280, 1536, 2560
    AB, ZB = QKV + 3 * D // 2, QKV + 3 * D // 2 + 16

    def tiles(w, first=0):
        return w.reshape(KT, P, -1, P).transpose(2, 1, 0, 3).reshape(-1, P, KT * P)

    heads = [[(2 * r) * 4 + g, (2 * r + 1) * 4 + g] for r in range(2) for g in range(4)]
    perm = np.concatenate([np.arange(64 * h, 64 * h + 64) for pair in heads for h in pair])
    wt = np.zeros((N_TILES, P, D), f32)
    ab = np.zeros((D, P), f32)
    ab[:, 0:16] = w0[:, AB:AB + 16]
    wt[N_AB:N_AB + 1] = tiles(ab)
    for h in range(H):
        c = QKV + h * P
        cols = [w0[:, c + D // 2:c + D // 2 + P], w0[:, c:c + P], w0[:, c + D:c + D + P], w0[:, ZB + h * P:ZB + (h + 1) * P]]
        wt[N_HEAD + 4 * h:N_HEAD + 4 * h + 4] = tiles(np.concatenate(cols, 1))
    for r in range(2):
        wt[N_KV + 2 * r:N_KV + 2 * r + 2] = tiles(np.concatenate(
            [w0[:, KA + r * P:KA + (r + 1) * P], w0[:, VA + r * P:VA + (r + 1) * P]], 1))
    wt[N_Q:N_Q + 8] = tiles(w0[:, QA:QA + 1024][:, perm])
    wt[N_ZA:N_ZA + 8] = tiles(w0[:, ZA:ZA + 1024][:, perm])
    wt[N_OUT0:N_OUT0 + KT] = tiles(np.concatenate([wo0[:1024][perm], wo0[1024:]], 0))
    wt[N_VG:N_VG + 2 * KT:2] = tiles(w1[:, D:2 * D])
    wt[N_VG + 1:N_VG + 2 * KT:2] = tiles(w1[:, :D])
    wt[N_Z1:N_Z1 + KT] = tiles(w1[:, 2 * D:])
    wt[N_OUT1:] = tiles(wo1)

    param = np.zeros((P, N_PARAM), f32)
    per_channel = lambda v: np.asarray(v).reshape(-1, P).T
    for c, v in ((P_G0, norm_gain[0]), (P_G1, norm_gain[1]), (P_GF, final_norm_gain), (P_CFB, cf_conv_b[0]),
                 (P_LNG, cf_ln_gain[0]), (P_LNB, cf_ln_bias[0])):
        param[:, c:c + KT] = per_channel(v)
    dnw = np.asarray(dn_conv_w)[0].reshape(4, 3, H, P)[:, [1, 0, 2]]
    param[:, P_DNW:P_DNW + 12 * H] = dnw.transpose(3, 2, 1, 0).reshape(P, -1)
    param[:, P_CFW:P_CFW + KT * CF] = np.asarray(cf_conv_w)[0].reshape(CF, KT, P).transpose(2, 1, 0).reshape(P, -1)
    param[:, P_DNG] = np.asarray(dn_norm_gain)[0]
    param[:, P_ALOG:P_ALOG + H] = np.asarray(dn_a_log)[0]
    param[:, P_DTB:P_DTB + H] = np.asarray(dn_dt_bias)[0]
    sinks = np.asarray(attn_sinks)[0]
    order = [(2 * r + q) * 4 + 2 * jj + j for r in range(2) for jj in range(2) for q in range(2) for j in range(2)]
    param[:, P_SINK:P_SINK + 16] = sinks[order]
    param[:, P_SINKS] = np.repeat(sinks, NT)

    prev = state_dn_conv[0].reshape(NB, 3, 3, H, P)[:, :, [1, 0, 2]].transpose(4, 3, 2, 0, 1).reshape(P, 3 * H, NB, 3)
    arrays = dict(
        x=channel_major(x_prompt[0], x_sample), wt=wt, const=_constants(), param=param,
        dn_prev=prev,
        state_in=state_dn[0].transpose(1, 2, 0, 3).reshape(H, P, NB * P),
        k_cache=cache_win_k[0].reshape(NB, W, 2, P).transpose(2, 3, 0, 1),
        v_cache=cache_win_v[0].reshape(NB, W, 2 * P).transpose(1, 0, 2).reshape(W, -1),
        cf_prev=state_cf_conv[0].reshape(NB, CP, KT, P).transpose(2, 3, 0, 1))
    arrays = {k: np.ascontiguousarray(v) for k, v in arrays.items()}

    nc = bacc.Bacc("TRN2", target_bir_lowering=False, num_devices=1)
    args = [nc.dram_tensor(k, v.shape, F32, kind="ExternalInput").ap() for k, v in arrays.items()]
    args += [nc.dram_tensor("out_" + k, shape, F32, kind="ExternalOutput").ap() for k, shape in _OUT]
    hybrid_step(nc, *args)
    got = run_bass_kernel_spmd(nc, [arrays], core_ids=[0]).results[0]
    o = {k: got["out_" + k] for k, _ in _OUT}

    y = o["y"].transpose(2, 0, 1).reshape(2, HALF, D)
    dnc = o["dnc"].reshape(P, H, 3, 9, 3)[:, :, [1, 0, 2]].transpose(3, 4, 2, 1, 0).reshape(9, 3, 3 * H * P)
    return (y[:, :HP].reshape(1, SEQ, D), y[:, HP:].reshape(NB, NT, D),
            o["win_k"].transpose(2, 0, 1).reshape(1, 1, W, 4, 64), o["win_v"].reshape(1, 1, W, 4, 64),
            o["dn"].reshape(1, 1, H, P, P), dnc[0].reshape(1, 1, 3, -1),
            o["cf"].transpose(2, 0, 1).reshape(1, 1, CP, D),
            o["swk"].transpose(2, 3, 0, 1).reshape(1, NB, W, 4, 64),
            o["swv"].reshape(W, NB, 4, 64).transpose(1, 0, 2, 3)[None],
            o["sdn"].reshape(H, P, NB, P).transpose(2, 0, 1, 3)[None], dnc[1:][None],
            o["cfs"].reshape(KT, P, NB, CP).transpose(2, 3, 0, 1).reshape(1, NB, CP, D))
```
